# Optimizing a Trainium2 kernel written in Bass

```python
import math
import jax, jax.numpy as jnp
from jax import lax
import numpy as np

D_MODEL = 2048
BATCH = 1
SEQ = 512
DEPTH = 1

HEAD_DIM = 128
HEADS_PER_GROUP = 4
ATTN_GROUPS = ((128, 1), (512, 4), (2048, 16))
N_ATTN_HEADS = HEADS_PER_GROUP * len(ATTN_GROUPS)
ATTN_OUT_WIDTH = HEADS_PER_GROUP * HEAD_DIM
HQ = N_ATTN_HEADS * HEAD_DIM
SSM_WIDTH = D_MODEL // 2
SSM_GROUP = 16
SSM_GROUPS = SSM_WIDTH // SSM_GROUP
SSM_STATE = 64
D_FF = -(-8 * D_MODEL // (3 * 256)) * 256
IN_SIZES = (HQ, HQ, HQ, SSM_WIDTH, D_MODEL, D_MODEL)
IN_WIDTH = sum(IN_SIZES)
IN_SPLITS = tuple(int(i) for i in np.cumsum(IN_SIZES)[:-1])
EPS = 1e-6
DT_MIN = 1e-3
DT_MAX = 1e-1

kernel_name = 'hybrid_dilated_attn_s5_gated'

def rms_norm(x, gain):
    xf = x.astype(jnp.float32)
    y = xf * lax.rsqrt(jnp.mean(xf * xf, axis=-1, keepdims=True) + EPS)
    return (y * gain.astype(jnp.float32)).astype(x.dtype)

def alibi_slopes(n):
    return jnp.exp2(-8.0 * jnp.arange(1, n + 1, dtype=jnp.float32) / n)

def dilated_window_attention(q, k, v, slopes, window, dilation):
    b, s, h, e = q.shape
    blk = window // dilation
    sub_len = -(-s // dilation)
    n_blk = -(-sub_len // blk)
    s_pad = n_blk * blk * dilation

    def to_blocks(t):
        t = jnp.pad(t, ((0, 0), (0, s_pad - s), (0, 0), (0, 0)))
        t = t.reshape(b, n_blk * blk, dilation, h, e).transpose(0, 2, 1, 3, 4)
        return t.reshape(b, dilation, n_blk, blk, h, e)

    def with_prev(t):
        prev = jnp.pad(t, ((0, 0), (0, 0), (1, 0), (0, 0), (0, 0), (0, 0)))[:, :, :-1]
        return jnp.concatenate([prev, t], axis=3)

    def from_blocks(t):
        f = t.shape[-1]
        t = t.reshape(b, dilation, n_blk * blk, h, f).transpose(0, 2, 1, 3, 4)
        return t.reshape(b, s_pad, h, f)[:, :s]

    qb = to_blocks(q)
    kw = with_prev(to_blocks(k))
    vw = with_prev(to_blocks(v))
    scores = jnp.einsum('brnqhe,brnkhe->brnhqk', qb, kw).astype(jnp.float32) * (e ** -0.5)
    qi = jnp.arange(blk)[:, None]
    ki = jnp.arange(2 * blk)[None, :]
    dist = blk + qi - ki
    blk_idx = jnp.arange(n_blk)[:, None, None]
    valid = ((dist >= 0) & (dist <= blk))[None] & (blk_idx * blk - blk + ki[None] >= 0)
    bias = -slopes[:, None, None] * (dist * dilation).astype(jnp.float32)[None]
    scores = scores + bias[None, None, None]
    scores = jnp.where(valid[None, None, :, None], scores, -jnp.inf)
    lse = jax.nn.logsumexp(scores, axis=-1)
    probs = jnp.exp(scores - lse[..., None])
    out = jnp.einsum('brnhqk,brnkhe->brnqhe', probs.astype(v.dtype), vw)
    lse = from_blocks(lse.transpose(0, 1, 2, 4, 3)[..., None])[..., 0]
    return from_blocks(out), lse

def s5_ssm(u, a_re, a_im, log_dt, b_re, b_im, c_re, c_im, d_skip):
    bsz, s, _ = u.shape
    uf = u.astype(jnp.float32)
    ug = uf.reshape(bsz, s, SSM_GROUPS, SSM_GROUP)
    lam = lax.complex(a_re.astype(jnp.float32), a_im.astype(jnp.float32))
    dt = jnp.exp(log_dt.astype(jnp.float32))[:, None]
    lam_bar = jnp.exp(lam * dt)
    b_cplx = lax.complex(b_re.astype(jnp.float32), b_im.astype(jnp.float32))
    b_bar = ((lam_bar - 1.0) / lam)[..., None] * b_cplx
    bu = lax.complex(jnp.einsum('bsgc,gpc->sbgp', ug, jnp.real(b_bar)),
                     jnp.einsum('bsgc,gpc->sbgp', ug, jnp.imag(b_bar)))
    a_seq = jnp.broadcast_to(lam_bar[None, None], (s, 1) + lam_bar.shape)

    def combine(left, right):
        a_l, b_l = left
        a_r, b_r = right
        return a_r * a_l, a_r * b_l + b_r

    _, states = lax.associative_scan(combine, (a_seq, bu), axis=0)
    y = (jnp.einsum('sbgp,gcp->bsgc', jnp.real(states), c_re.astype(jnp.float32))
         - jnp.einsum('sbgp,gcp->bsgc', jnp.imag(states), c_im.astype(jnp.float32)))
    y = y.reshape(bsz, s, SSM_WIDTH) + d_skip.astype(jnp.float32) * uf
    return y.astype(u.dtype)

def hybrid_layer(x, norm_mix_pre, w_in, w_attn_up, ssm_a_re, ssm_a_im, ssm_log_dt, ssm_b_re, ssm_b_im,
                 ssm_c_re, ssm_c_im, ssm_d, w_glu_v, w_glu_g, w_out, norm_mix_post, norm_ffn_pre,
                 w_ffn_gate, w_ffn_up, w_ffn_down, norm_ffn_post):
    bsz, s, _ = x.shape
    h = rms_norm(x, norm_mix_pre)
    q, k, v, u, gate_a, gate_s = jnp.split(h @ w_in, IN_SPLITS, axis=-1)
    q = q.reshape(bsz, s, N_ATTN_HEADS, HEAD_DIM)
    k = k.reshape(bsz, s, N_ATTN_HEADS, HEAD_DIM)
    v = v.reshape(bsz, s, N_ATTN_HEADS, HEAD_DIM)
    slopes = alibi_slopes(N_ATTN_HEADS)
    outs, lses = [], []
    for g, (window, dilation) in enumerate(ATTN_GROUPS):
        hs = slice(g * HEADS_PER_GROUP, (g + 1) * HEADS_PER_GROUP)
        o, l = dilated_window_attention(q[:, :, hs], k[:, :, hs], v[:, :, hs], slopes[hs], window, dilation)
        outs.append(o)
        lses.append(l)
    mix_w = jax.nn.softmax(jnp.stack(lses), axis=0)
    attn = jnp.sum(mix_w[..., None] * jnp.stack(outs).astype(jnp.float32), axis=0)
    attn_branch = attn.reshape(bsz, s, ATTN_OUT_WIDTH).astype(x.dtype) @ w_attn_up
    y = jax.nn.gelu(s5_ssm(u, ssm_a_re, ssm_a_im, ssm_log_dt, ssm_b_re, ssm_b_im, ssm_c_re, ssm_c_im, ssm_d))
    ssm_branch = (y @ w_glu_v) * jax.nn.sigmoid(y @ w_glu_g)
    merged = jax.nn.sigmoid(gate_a) * attn_branch + jax.nn.sigmoid(gate_s) * ssm_branch
    x = x + rms_norm(merged @ w_out, norm_mix_post)
    h = rms_norm(x, norm_ffn_pre)
    f = (jax.nn.silu(h @ w_ffn_gate) * (h @ w_ffn_up)) @ w_ffn_down
    return x + rms_norm(f, norm_ffn_post)

def setup_inputs(seed: int = 0) -> dict:
    key = jax.random.key(seed)
    ks = jax.random.split(key, 24)

    def nrm(k, shape, scale):
        return jax.random.normal(k, shape, jnp.float32) * scale

    def gain(k, n):
        return 1.0 + 0.02 * jax.random.normal(k, (DEPTH, n), jnp.float32)

    g, p, c = SSM_GROUPS, SSM_STATE, SSM_GROUP
    return {
        'x': nrm(ks[0], (BATCH, SEQ, D_MODEL), 1.0),
        'norm_mix_pre': gain(ks[1], D_MODEL),
        'w_in': nrm(ks[2], (DEPTH, D_MODEL, IN_WIDTH), D_MODEL ** -0.5),
        'w_attn_up': nrm(ks[3], (DEPTH, ATTN_OUT_WIDTH, D_MODEL), ATTN_OUT_WIDTH ** -0.5),
        'ssm_a_re': -0.5 + 0.01 * jax.random.normal(ks[4], (DEPTH, g, p), jnp.float32),
        'ssm_a_im': jnp.pi * jnp.arange(p, dtype=jnp.float32)[None, None, :] + 0.01 * jax.random.normal(ks[5], (DEPTH, g, p), jnp.float32),
        'ssm_log_dt': jax.random.uniform(ks[6], (DEPTH, g), jnp.float32, math.log(DT_MIN), math.log(DT_MAX)),
        'ssm_b_re': nrm(ks[7], (DEPTH, g, p, c), (2 * c) ** -0.5),
        'ssm_b_im': nrm(ks[8], (DEPTH, g, p, c), (2 * c) ** -0.5),
        'ssm_c_re': nrm(ks[9], (DEPTH, g, c, p), (2 * p) ** -0.5 * 4.0),
        'ssm_c_im': nrm(ks[10], (DEPTH, g, c, p), (2 * p) ** -0.5 * 4.0),
        'ssm_d': nrm(ks[11], (DEPTH, SSM_WIDTH), 1.0),
        'w_glu_v': nrm(ks[12], (DEPTH, SSM_WIDTH, D_MODEL), SSM_WIDTH ** -0.5),
        'w_glu_g': nrm(ks[13], (DEPTH, SSM_WIDTH, D_MODEL), SSM_WIDTH ** -0.5),
        'w_out': nrm(ks[14], (DEPTH, D_MODEL, D_MODEL), D_MODEL ** -0.5),
        'norm_mix_post': gain(ks[15], D_MODEL),
        'norm_ffn_pre': gain(ks[16], D_MODEL),
        'w_ffn_gate': nrm(ks[17], (DEPTH, D_MODEL, D_FF), D_MODEL ** -0.5),
        'w_ffn_up': nrm(ks[18], (DEPTH, D_MODEL, D_FF), D_MODEL ** -0.5),
        'w_ffn_down': nrm(ks[19], (DEPTH, D_FF, D_MODEL), D_FF ** -0.5),
        'norm_ffn_post': gain(ks[20], D_MODEL),
    }

def reference(x, norm_mix_pre, w_in, w_attn_up, ssm_a_re, ssm_a_im, ssm_log_dt, ssm_b_re, ssm_b_im,
              ssm_c_re, ssm_c_im, ssm_d, w_glu_v, w_glu_g, w_out, norm_mix_post, norm_ffn_pre,
              w_ffn_gate, w_ffn_up, w_ffn_down, norm_ffn_post):
    for i in range(DEPTH):
        x = hybrid_layer(x, norm_mix_pre[i], w_in[i], w_attn_up[i], ssm_a_re[i], ssm_a_im[i], ssm_log_dt[i],
                         ssm_b_re[i], ssm_b_im[i], ssm_c_re[i], ssm_c_im[i], ssm_d[i], w_glu_v[i], w_glu_g[i],
                         w_out[i], norm_mix_post[i], norm_ffn_pre[i], w_ffn_gate[i], w_ffn_up[i],
                         w_ffn_down[i], norm_ffn_post[i])
    return x


_drawn_inputs = setup_inputs


def setup_inputs(seed=0):
    import zlib

    import numpy as np

    out = dict(_drawn_inputs(seed))
    spreads = {}
    factors = {'ssm_a_re': 8.0, 'norm_mix_post': 3.352, 'norm_ffn_pre': 3.499, 'norm_ffn_post': 4.975}
    for name, (base, spread) in spreads.items():
        noise = np.random.default_rng([zlib.crc32(name.encode()), seed]).standard_normal(out[name].shape)
        drawn = base * np.exp(spread * noise) if base else spread * noise
        out[name] = __import__('jax').numpy.asarray(drawn.astype(out[name].dtype))
    for name, factor in factors.items():
        out[name] = (out[name] * factor).astype(out[name].dtype)
    return out
```

```python
from contextlib import ExitStack
import math

import concourse.bass as bass
from concourse import mybir

F32 = mybir.dt.float32
F32R = mybir.dt.float32r
ALU = mybir.AluOpType
ACT = mybir.ActivationFunctionType
AX = mybir.AxisListType.X

P = 128
SEQ = 512
D = 2048
CLS = SEQ // P
KT = D // P
EPS = 1e-6
HEADS = 4
GROUPS = 3
HQ = HEADS * GROUPS * P
SCALE = float(P) ** -0.5
WINDOW0 = 128
BIG = 1e30
SSM = 1024
CH = 16
HG = SSM // CH // 2
NST = 64
L = 8
NCH = SEQ // L
OCT = 8
OG = HG // OCT
KPAD = (2 * L - 1) * CH
FF = 5632
FFG = FF // SEQ
U_COL = 3 * HQ
GA_COL = U_COL + SSM
GS_COL = GA_COL + D
TWO_PI = 2 * math.pi
PI_A = 6.28125
PI_B = 0.0019340515136718750
PI_C = TWO_PI - PI_A - PI_B
ROUND = 12582912.0

N_QKV = GROUPS * 12
B_U = 0
B_QKV = (16, 16 + N_QKV)
B_AU = B_QKV[1] + N_QKV
B_MRG = B_AU + 8
B_WO = B_MRG + 8 * 12
B_FF = B_WO + 32


def group(b, gh, e):
    return 16 * (b // 2) + 8 * gh + OG * (b % 2) + e


def slope(head):
    return 2.0 ** (-8.0 * (head + 1) / (HEADS * GROUPS))


def build(nc, A, out):
    ctx = ExitStack()
    with ctx:
        def sem(name):
            return ctx.enter_context(nc.semaphore(name))

        base = 16512

        def at_kb(name, kb, shape, dt=F32):
            return nc.alloc_sbuf_tensor_at(name, shape, dt, offset=base + int(kb * 1024))

        a_hi = at_kb("a_hi", 0, [P, KT, SEQ], F32R)
        a_lo = at_kb("a_lo", 32, [P, KT, SEQ], F32R)
        raw = at_kb("raw", 64, [P, 4, 1024])
        w_hi = at_kb("w_hi", 80, [P, 2, 1024], F32R)
        w_lo = at_kb("w_lo", 88, [P, 2, 1024], F32R)
        ident = at_kb("ident", 96, [P, P])
        pen = at_kb("pen", 96.5, [P, P])
        scan_a = at_kb("scan_a", 97, [P, 2, HG, 2])
        scan_t = at_kb("scan_t", 97.5, [P, 2, HG, 2])
        hot = at_kb("hot", 98, [4, P])
        gain_t = at_kb("gain_t", 98.5, [P, 2, KT])
        stat = at_kb("stat", 98.75, [P, 3, CLS])
        smx = at_kb("smx", 98.875, [P, 2, 5])
        x_tok = at_kb("x_tok", 100, [P, CLS, D])
        x_sq = at_kb("x_sq", 132, [P, D])
        u_st = at_kb("u_st", 100, [P, 2, 2, SEQ])
        q_t = at_kb("q_t", 100, [P, GROUPS, 2, SEQ])
        k_t = at_kb("k_t", 112, [P, GROUPS, 2, SEQ])
        v_t = at_kb("v_t", 124, [P, GROUPS, CLS, 2 * P])
        bias = at_kb("bias", 136, [P, 2, 9, P])
        at_hi = at_kb("at_hi", 145, [P, HEADS, SEQ], F32R)
        at_lo = at_kb("at_lo", 153, [P, HEADS, SEQ], F32R)
        s_t = at_kb("s_t", 161, [P, HG, 2, NCH])
        sc = at_kb("sc", 177, [P, 2, 768])
        p_t = at_kb("p_t", 183, [P, 2, 768])
        a_raw = at_kb("a_raw", 140, [HG, 2, 2 * NST])
        b_raw = at_kb("b_raw", 141, [P, 2, HG, CH])
        bl = at_kb("bl", 145, [P, 4, OG, 2, L, CH])
        hc = at_kb("hc", 161, [P, 4, OG, 2, L + 1, CH])
        g_st = at_kb("g_st", 179, [P, OG, 2, P])
        c_raw = at_kb("c_raw", 179, [P, 2, 4, 2, NST])
        b_bar = at_kb("b_bar", 183, [P, 2, HG, CH])
        c_t = at_kb("c_t", 187, [P, 2, HG, CH])
        lam = at_kb("lam", 191, [P, L + 1, 2, HG])
        lam_r = at_kb("lam_r", 193.25, [P, L, 2, HG])
        k_st = at_kb("k_st", 195.5, [P, 2, 2, 2, P])
        prm = at_kb("prm", 195.5, [P, 24, HG])
        ptmp = at_kb("ptmp", 199.5, [P, 2, OG * (L + 1) * CH])
        d_blk = at_kb("d_blk", 204, [P, 2 * OCT, CH])
        e16 = at_kb("e16", 205, [P, CH])
        d_pad = at_kb("d_pad", 205.125, [P, 2 * OCT])
        zero = at_kb("zero", 205.25, [P, 4 * (L - 1) * CH])
        g_r = at_kb("g_r", 177, [P, 2, OG, 2, P])
        u_all = at_kb("u_all", 191.75, [P, 2 * HG, NCH])
        t_q = [at_kb(f"t_q{q}", kb, [P, 16, P]) for q, kb in enumerate((177, 132, 145, 153))]
        h_r = [at_kb(f"h_r{s}", kb, [P, OG, 2, P]) for s, kb in enumerate((185, 140))]
        mrg = at_kb("mrg", 100, [P, KT, SEQ])
        sig_a = at_kb("sig_a", 132, [P, 1024])
        sig_s = at_kb("sig_s", 136, [P, 1024])
        sig_g = at_kb("sig_g", 140, [P, 1024])
        y_hi = at_kb("y_hi", 161, [P, SSM // P, SEQ], F32R)
        y_lo = at_kb("y_lo", 145, [P, SSM // P, SEQ], F32R)
        y_in = at_kb("y_in", 177, [P, 2, SEQ])
        y_act = at_kb("y_act", 181, [P, 2, SEQ])
        o_t = at_kb("o_t", 132, [P, CLS, D])
        x2 = at_kb("x2", 164, [P, CLS, D])
        gain_b = at_kb("gain_b", 196, [P, D])
        f_hi = at_kb("f_hi", 100, [P, 4, SEQ], F32R)
        f_lo = at_kb("f_lo", 108, [P, 4, SEQ], F32R)
        f_sg = at_kb("f_sg", 116, [P, 1024])
        f_t = at_kb("f_t", 120, [P, 1024])
        sq_t = at_kb("sq_t", 124, [P, D])

        ps = ctx.enter_context(nc.psum_tensor("ps", [P, 8, 512], F32))

        def pair(p):
            return ps[:, 2 * p:2 * p + 2, :].rearrange("p b n -> p (b n)")

        u_d = nc.dram_tensor("u_d", [L, SSM, NCH], F32, kind="Internal").ap()
        y_d = nc.dram_tensor("y_d", [L, SSM, NCH], F32, kind="Internal").ap()
        g_d = nc.dram_tensor("g_d", [OCT, P, OG * 2 * P], F32, kind="Internal").ap()
        h_d = nc.dram_tensor("h_d", [OCT, P, OG * 2, (L + 1) * CH], F32, kind="Internal").ap()
        k_d = nc.dram_tensor("k_d", [SSM, KPAD], F32, kind="Internal").ap()

        landed = [sem(f"landed{s}") for s in range(4)]
        hi_ready = sem("hi_ready")
        lo_ready = sem("lo_ready")
        piece_done = sem("piece_done")
        x_in = [sem(f"x_in{c}") for c in range(CLS)]
        par_in = sem("par_in")
        c_in = sem("c_in")
        gain_in = sem("gain_in")
        b_in = sem("b_in")
        dp_in = sem("dp_in")
        const = sem("const")
        pool_step = sem("pool_step")
        dve_step = sem("dve_step")
        act_step = sem("act_step")
        par_tr = sem("par_tr")
        par_act = sem("par_act")
        par_dve = sem("par_dve")
        sq_done = sem("sq_done")
        rstd_in = sem("rstd_in")
        rstd_sqrt = sem("rstd_sqrt")
        scaled = sem("scaled")
        turned = sem("turned")
        turned_hi = sem("turned_hi")
        turned_lo = sem("turned_lo")
        u_copied = sem("u_copied")
        u_stored = [sem(f"u_stored{s}") for s in range(2)]
        tab_ready = sem("tab_ready")
        h_stored = sem("h_stored")
        zero_stored = sem("zero_stored")
        k_bank = sem("k_bank")
        k_made = sem("k_made")
        k_copied = sem("k_copied")
        k_stored = sem("k_stored")
        g_made = sem("g_made")
        g_copied = sem("g_copied")
        g_stored = sem("g_stored")
        q_copied = sem("q_copied")
        k_act = sem("k_act")
        v_copied = sem("v_copied")
        bias_ready = sem("bias_ready")
        scores = sem("scores")
        biased = sem("biased")
        negmax = sem("negmax")
        exped = sem("exped")
        normed = sem("normed")
        probs_t = sem("probs_t")
        probs_copied = sem("probs_copied")
        heads = sem("heads")
        heads_hi = sem("heads_hi")
        heads_lo = sem("heads_lo")
        g_in = [sem(f"g_in{s}") for s in range(2)]
        u_in = sem("u_in")
        s_made = sem("s_made")
        s_copied = sem("s_copied")
        scan_step = sem("scan_step")
        h_in = [sem(f"h_in{s}") for s in range(2)]
        t_in = [sem(f"t_in{q}") for q in range(4)]
        y_made = sem("y_made")
        y_copied = sem("y_copied")
        y_stored = sem("y_stored")
        y_back = [sem(f"y_back{s}") for s in range(2)]
        gelu = sem("gelu")
        gelu_hi = sem("gelu_hi")
        gelu_lo = sem("gelu_lo")
        au_copied = sem("au_copied")
        gated = sem("gated")
        merge_step = sem("merge_step")
        mrg_hi = sem("mrg_hi")
        mrg_lo = sem("mrg_lo")
        o_copied = sem("o_copied")
        x_again = sem("x_again")
        gb_in = [sem(f"gb_in{s}") for s in range(2)]
        x2_ready = sem("x2_ready")
        acc_zero = sem("acc_zero")
        silu = sem("silu")
        f_made = sem("f_made")
        f_hi_ready = sem("f_hi_ready")
        f_lo_ready = sem("f_lo_ready")
        down = sem("down")
        down_added = sem("down_added")
        out_ready = sem("out_ready")
        stored = sem("stored")

        def load(sp, m, quads, w, row_tiles, rows0, cols0, n):
            if not isinstance(rows0, int):
                rows0 = sp.snap(rows0)
            if not isinstance(cols0, int):
                cols0 = sp.snap(cols0)
            src = w_tiles(w, row_tiles, rows0, cols0, n)
            if m >= 4:
                sp.wait_ge(lo_ready, m - 3 + 4 * quads)
            sp.dma_start(raw[:, m % 4, :].rearrange("p (k n) -> p k n", n=src.shape[-1]), src
                         ).then_inc(landed[m % 4], 16)

        def split_hi(act, m, quads):
            act.wait_ge(landed[m % 4], 16 * (m // 4 + 1) + 16 * quads)
            if m >= 2:
                act.wait_ge(piece_done, m - 1 + 4 * quads)
            nc.scalar.activation(w_hi[:, m % 2, :], raw[:, m % 4, :], ACT.Copy).then_inc(hi_ready, 1)

        def split_lo(dve, m, quads):
            dve.wait_ge(hi_ready, m + 1 + 4 * quads)
            nc.vector.tensor_tensor(w_lo[:, m % 2, :], raw[:, m % 4, :], w_hi[:, m % 2, :].bitcast(F32),
                                    ALU.subtract).then_inc(lo_ready, 1)

        def piece_f(pe, m, quads, banks, x_hi, x_lo, kt0, first, last):
            pe.wait_ge(lo_ready, m + 1 + 4 * quads)
            wh = w_hi[:, m % 2, :].rearrange("p (k n) -> p k n", n=256)
            wl = w_lo[:, m % 2, :].rearrange("p (k n) -> p k n", n=256)
            for k in range(4):
                for f in range(2):
                    cols = slice(f * P, f * P + P)
                    o = ps[:, 2 * banks + f, :]
                    nc.tensor.matmul(o, wh[:, k, cols], x_hi[:, kt0 + k, :], start=first and k == 0, stop=False)
                    nc.tensor.matmul(o, wh[:, k, cols], x_lo[:, kt0 + k, :], start=False, stop=False)
                    mm = nc.tensor.matmul(o, wl[:, k, cols], x_hi[:, kt0 + k, :], start=False,
                                          stop=last and k == 3)
            mm.then_inc(piece_done, 1)

        def piece_v(pe, m, quads, banks, kt0, first, last):
            pe.wait_ge(lo_ready, m + 1 + 4 * quads)
            wh = w_hi[:, m % 2, :].rearrange("p (k n) -> p k n", n=256)
            wl = w_lo[:, m % 2, :].rearrange("p (k n) -> p k n", n=256)
            for k in range(4):
                for c in range(CLS):
                    o = ps[:, 2 * banks + c // 2, 256 * (c % 2):256 * (c % 2) + 256]
                    toks = slice(c * P, c * P + P)
                    nc.tensor.matmul(o, a_hi[:, kt0 + k, toks], wh[:, k, :], start=first and k == 0 and c % 2 == 0,
                                     stop=False, skip_group_check=True)
                    nc.tensor.matmul(o, a_hi[:, kt0 + k, toks], wl[:, k, :], start=False, stop=False,
                                     skip_group_check=True)
                    mm = nc.tensor.matmul(o, a_lo[:, kt0 + k, toks], wh[:, k, :], start=False,
                                          stop=last and k == 3, skip_group_check=True)
            mm.then_inc(piece_done, 1)

        def piece_t(pe, m, quads, bank0, x_hi, x_lo, kt0, first, last, before=None, done=None):
            pe.wait_ge(lo_ready, m + 1 + 4 * quads)
            wh = w_hi[:, m % 2, :].rearrange("p (k n) -> p k n", n=512)
            wl = w_lo[:, m % 2, :].rearrange("p (k n) -> p k n", n=512)
            for c in range(CLS):
                if before:
                    before(c)
                toks = slice(c * P, c * P + P)
                o = ps[:, bank0 + c, :]
                for k in range(2):
                    nc.tensor.matmul(o, x_hi[:, kt0 + k, toks], wh[:, k, :], start=first and k == 0, stop=False)
                    nc.tensor.matmul(o, x_hi[:, kt0 + k, toks], wl[:, k, :], start=False, stop=False)
                    mm = nc.tensor.matmul(o, x_lo[:, kt0 + k, toks], wh[:, k, :], start=False,
                                          stop=last and k == 1)
                if done is not None and c < CLS - 1:
                    mm.then_inc(done, 1)
            mm.then_inc(piece_done, 1)

        def w_tiles(w, row_tiles, rows0, cols0, n):
            return w[bass.ds(rows0, row_tiles * P), bass.ds(cols0, n)].rearrange("(k p) n -> p k n", p=P)

        w_in, w_up = A["w_in"][0], A["w_attn_up"][0]
        w_gv, w_gg, w_out = A["w_glu_v"][0], A["w_glu_g"][0], A["w_out"][0]
        w_fg, w_fu, w_fd = A["w_ffn_gate"][0], A["w_ffn_up"][0], A["w_ffn_down"][0]
        x_cls = A["x"][0].rearrange("(j c) d -> c j d", c=CLS)
        out_cls = out[0].rearrange("(j c) d -> c j d", c=CLS)

        block = ctx.enter_context(nc.Block())

        @block.sync
        def _(sp):
            for c in range(CLS):
                sp.dma_start(x_tok[:, c, :], x_cls[c]).then_inc(x_in[c], 16)
            for k in range(16):
                load(sp, B_U + k, 0, w_in, 4, 4 * P * (k % 4), U_COL + 256 * (k // 4), 256)
            for pr in range(2):
                with sp.Fori(0, GROUPS) as g:
                    for k in range(12):
                        col = HQ * (k // 4) + 256 * pr
                        load(sp, B_QKV[pr] + k, 3 * g, w_in, 4, 4 * P * (k % 4), 512 * g + col, 256)
            with sp.Fori(0, 2) as it:
                for k in range(4):
                    load(sp, B_AU + k, it, w_up, 4, 0, 1024 * it + 256 * k, 256)
            with sp.Fori(1, 9) as it:
                for k in range(12):
                    if k < 8:
                        src = (w_in, 4, 4 * P * (k % 4), 256 * it + (GA_COL, GS_COL)[k // 4] - 256, 256)
                    else:
                        src = ((w_gv, w_gg)[k // 2 - 4], 4, 4 * P * (k % 2), 256 * it - 256, 256)
                    load(sp, B_MRG + k - 12, 3 * it, *src)
            with sp.Fori(0, 2) as it:
                for k in range(16):
                    load(sp, B_WO + k, 4 * it, w_out, 2, 2 * P * (k % 8), 1024 * it + 512 * (k // 8), 512)
            sp.wait_ge(mrg_lo, 4)
            sp.dma_start(x2[:, :, :], A["x"][0].rearrange("(j c) d -> j c d", c=CLS)).then_inc(x_again, 16)
            sp.dma_start(gain_b[:, :], A["norm_mix_post"][0:1, :].partition_broadcast(P)).then_inc(gb_in[0], 16)
            with sp.Fori(0, FFG) as g:
                for k in range(24):
                    if k < 16:
                        src = ((w_fg, w_fu)[k // 4 % 2], 4, 4 * P * (k % 4), 512 * g + 256 * (k // 8), 256)
                    else:
                        src = (w_fd, 2, 512 * g + 2 * P * (k % 2), 512 * ((k - 16) // 2), 512)
                    load(sp, B_FF + k, 6 * g, *src)
            sp.wait_ge(x2_ready, CLS)
            sp.dma_start(gain_b[:, :], A["norm_ffn_post"][0:1, :].partition_broadcast(P)).then_inc(gb_in[1], 16)
            for c in range(CLS):
                sp.wait_ge(out_ready, c + 1)
                sp.dma_start(out_cls[c], x2[:, c, :]).then_inc(stored, 16)
            sp.wait_ge(stored, 16 * CLS)

        k_banks = (4, 0)

        def pe_turn(pe, src, first):
            for kt in range(KT):
                n = KT * first + kt
                if kt >= 8:
                    pe.wait_ge(turned_lo, n - 7)
                for c in range(CLS):
                    if kt == 0:
                        pe.wait_ge(scaled, CLS * first + c + 1)
                    mm = nc.tensor.transpose(ps[:, kt % 8, c * P:c * P + P], src[:, c, kt * P:kt * P + P], ident[:, :])
                mm.then_inc(turned, 1)

        def pe_tables(pe, half):
            for q in range(4):
                b = 4 * half + q
                pe.wait_ge(tab_ready, b + 1)
                if b == 0:
                    pe.wait_ge(k_bank, 1)
                if b == 1:
                    pe.wait_ge(u_copied, 3)
                if b == 5:
                    pe.wait_ge(q_copied, 3)
                if b >= 2:
                    pe.wait_ge(k_copied, b - 1)
                for gh in range(2):
                    ph = slice(NST * gh, NST * gh + NST)
                    for e in range(OG):
                        for ri in range(2):
                            mm = nc.tensor.matmul(
                                ps[32 * e:32 * e + CH, k_banks[b % 2] + gh, 0:P],
                                b_bar[ph, ri, OG * b + e, :],
                                hc[ph, q, e, ri, 0:L, :].rearrange("p k o -> p (k o)"),
                                start=ri == 0, stop=ri == 1)
                mm.then_inc(k_made, 1)
                if b >= 1:
                    pe.wait_ge(g_copied, b)
                for e in range(OG):
                    for ri in range(2):
                        mm = nc.tensor.transpose(
                            pair(3)[:, (2 * e + ri) * P:(2 * e + ri) * P + P],
                            bl[:, q, e, ri, :, :].rearrange("p s i -> p (s i)"), ident[:, :])
                mm.then_inc(g_made, 1)

        def pe_qkv(pe, pr):
            with pe.Fori(0, GROUPS) as g:
                for k in range(12):
                    m, quads, kt0, first, last = B_QKV[pr] + k, 3 * g, 4 * (k % 4), k % 4 == 0, k % 4 == 3
                    if k == 0:
                        pe.wait_ge(q_copied, 3 * pr + g)
                    if k == 4:
                        pe.wait_ge(k_act, 3 * pr + g)
                    if k == 8:
                        pe.wait_ge(v_copied, 3 * pr + g)
                    if k < 8:
                        piece_f(pe, m, quads, k // 4, a_hi, a_lo, kt0, first, last)
                    else:
                        piece_v(pe, m, quads, 2, kt0, first, last)

        def pe_attention(pe, pr):
            n0 = 8 * pr
            pe.wait_ge(q_copied, 3 * pr + 3)
            pe.wait_ge(k_act, 3 * pr + 3)
            pe.wait_ge(v_copied, 3 * pr + 3)
            for t in range(8 + 2):
                if t < 8:
                    h, c, n = t // CLS, t % CLS, n0 + t
                    if n >= 2:
                        pe.wait_ge(biased, n - 1)
                    qs = slice(c * P, c * P + P)
                    s2 = pair(t % 2)
                    nc.tensor.matmul(s2[:, 0:512], q_t[:, 0, h, qs], k_t[:, 0, h, :], start=True, stop=True)
                    nc.tensor.matmul(s2[:, 512:640], q_t[:, 1, h, qs], k_t[:, 1, h, qs], start=True, stop=True)
                    nc.tensor.matmul(s2[:, 640:768], q_t[:, 2, h, qs], k_t[:, 2, h, qs], start=True,
                                     stop=True).then_inc(scores, 1)
                if 1 <= t < 9:
                    n = n0 + t - 1
                    pe.wait_ge(normed, n + 1)
                    if n >= 1:
                        pe.wait_ge(probs_copied, n)
                    for k in range(6):
                        mm = nc.tensor.transpose(pair(2)[:, k * P:k * P + P], sc[:, (t - 1) % 2, k * P:k * P + P],
                                                 ident[:, :])
                    mm.then_inc(probs_t, 1)
                if t >= 2:
                    h, c, n = (t - 2) // CLS, (t - 2) % CLS, n0 + t - 2
                    pe.wait_ge(probs_copied, n + 1)
                    if n >= 2:
                        pe.wait_ge(heads_lo, n - 1)
                    es = slice(h * P, h * P + P)
                    for k in range(6):
                        v = v_t[:, 0, k, es] if k < CLS else v_t[:, k - 3, c, es]
                        mm = nc.tensor.matmul(ps[:, 6 + t % 2, 0:P], v, p_t[:, t % 2, k * P:k * P + P],
                                              start=k == 0, stop=k == 5)
                    mm.then_inc(heads, 1)

        def pe_chunk_inputs(pe):
            for b in range(OCT):
                pe.wait_ge(g_in[b % 2], 16 * (b // 2 + 1))
                if b == 0:
                    pe.wait_ge(u_in, 16 * L)
                if b >= 2:
                    pe.wait_ge(s_copied, b - 1)
                for gh in range(2):
                    for e in range(OG):
                        for ri in range(2):
                            col = (2 * e + ri) * NCH
                            mm = nc.tensor.matmul(
                                ps[NST * gh:NST * gh + NST, b % 2, col:col + NCH],
                                g_r[:, b % 2, e, ri, NST * gh:NST * gh + NST], u_all[:, group(b, gh, e), :],
                                start=True, stop=True)
                mm.then_inc(s_made, 1)

        def pe_outputs(pe):
            pe.wait_ge(scan_step, 3 * (NCH - 1))
            for b in range(OCT):
                s = b % 2
                pe.wait_ge(h_in[s], 16 * (b // 2 + 1))
                pe.wait_ge(t_in[b // 2], 16 * L)
                if b >= 2:
                    pe.wait_ge(y_copied, b - 1)
                for gh in range(2):
                    ph = slice(NST * gh, NST * gh + NST)
                    for e in range(OG):
                        col, bank = e * NCH, 2 * s + gh
                        g = group(b, gh, e)
                        nc.tensor.matmul(ps[:, bank, col:col + NCH], t_q[b // 2][:, g % 16, :], u_all[:, g, :],
                                         start=True, stop=True)
                        for ri in range(2):
                            mm = nc.tensor.matmul(ps[:, bank, col + 1:col + NCH], h_r[s][ph, e, ri, :],
                                                  s_t[ph, OG * b + e, ri, 0:NCH - 1], start=False, stop=True,
                                                  skip_group_check=True)
                mm.then_inc(y_made, 1)

        @block.tensor
        def _(pe):
            pe.wait_ge(const, 1)
            pe.wait_ge(par_in, 64)
            for ri in range(2):
                nc.tensor.transpose(ps[:, 0, ri * HG:ri * HG + HG], a_raw[:, ri, :], ident[0:HG, 0:HG])
            pe.wait_ge(c_in, 32)
            for ri in range(2):
                for k in range(4):
                    mm = nc.tensor.transpose(ps[:, 1 + ri, k * P:k * P + P],
                                             c_raw[:, ri, k, :, :].rearrange("p a b -> p (a b)"), ident[:, :])
            mm = nc.tensor.matmul(ps[:, 3, 0:P], hot[:, :], hot[:, :], start=True, stop=True)
            mm.then_inc(par_tr, 1)
            pe.wait_ge(par_dve, 1)
            pe_turn(pe, x_tok, 0)
            pe.wait_ge(turned_lo, KT)
            with pe.Fori(0, 2) as it:
                for k in range(8):
                    if k % 4 == 0:
                        pe.wait_ge(u_copied, 2 * it + k // 4)
                    piece_f(pe, B_U + k, 2 * it, k // 4, a_hi, a_lo, 4 * (k % 4), k % 4 == 0, k % 4 == 3)
            pe_tables(pe, 0)
            pe.wait_ge(u_copied, 4)
            pe.wait_ge(k_copied, 4)
            pe_qkv(pe, 0)
            pe.wait_ge(v_copied, 3)
            pe_tables(pe, 1)
            pe.wait_ge(q_copied, 3)
            pe.wait_ge(k_copied, 8)
            pe.wait_ge(g_copied, 8)
            pe_attention(pe, 0)
            pe_chunk_inputs(pe)
            pe.wait_ge(s_copied, OCT)
            pe_qkv(pe, 1)
            pe_attention(pe, 1)
            pe.wait_ge(heads_lo, 16)
            with pe.Fori(0, 2) as it:
                for k in range(4):
                    pe.wait_ge(au_copied, 4 * it + k)
                    piece_f(pe, B_AU + k, it, k, at_hi, at_lo, 0, True, True)
            pe.wait_ge(au_copied, 8)
            pe_outputs(pe)
            pe.wait_ge(y_copied, OCT)
            with pe.Fori(0, 8) as it:
                for k in range(12):
                    if k < 8:
                        if k % 4 == 0:
                            pe.wait_ge(gated, 3 * it if k == 0 else 3 * it)
                        piece_f(pe, B_MRG + k, 3 * it, k // 4, a_hi, a_lo, 4 * (k % 4), k % 4 == 0, k % 4 == 3)
                    else:
                        if k == 8:
                            pe.wait_ge(gelu_lo, SSM // P)
                        if k % 2 == 0:
                            pe.wait_ge(merge_step, 4 * it)
                        piece_f(pe, B_MRG + k, 3 * it, k // 2 - 2, y_hi, y_lo, 4 * (k % 2), k % 2 == 0, k % 2 == 1)
            pe.wait_ge(merge_step, 32)
            with pe.Fori(0, 2) as it:
                for k in range(16):
                    if k % 2 == 0 and k < 8:
                        pe.wait_ge(mrg_lo, k // 2 + 1)
                    if k % 8 == 0:
                        pe.wait_ge(o_copied, 2 * it + k // 8)
                    piece_t(pe, B_WO + k, 4 * it, 4 * (k // 8), a_hi, a_lo, 2 * (k % 8), k % 8 == 0, k % 8 == 7)
            pe.wait_ge(o_copied, 4)
            pe_turn(pe, o_t, 1)
            pe.wait_ge(turned_lo, 2 * KT)
            with pe.Fori(0, FFG) as g:
                for k in range(24):
                    m = B_FF + k
                    if k < 16:
                        if k % 8 == 0:
                            pe.wait_ge(silu, 2 * g + k // 8)
                        if k % 8 == 4:
                            pe.wait_ge(f_made, 2 * g + k // 8)
                        piece_f(pe, m, 6 * g, k // 4 % 2, a_hi, a_lo, 4 * (k % 4), k % 4 == 0, k % 4 == 3)
                    else:
                        d = (k - 16) // 2
                        if k < 18:
                            pe.wait_ge(f_lo_ready, 2 * g + k - 15)

                        def bank_free(c, d=d, k=k, g=g):
                            if k % 2 == 0:
                                if d == 0:
                                    if c == 0:
                                        pe.wait_ge(down_added, 16 * g)
                                else:
                                    pe.wait_ge(down_added, 16 * g + 4 * d + c - 3)

                        piece_t(pe, m, 6 * g, 4, f_hi, f_lo, 2 * (k % 2), k % 2 == 0, k % 2 == 1,
                                before=bank_free, done=down if k % 2 else None)

        def act_turn(act, first):
            for kt in range(KT):
                act.wait_ge(turned, KT * first + kt + 1)
                nc.scalar.activation(a_hi[:, kt, :], ps[:, kt % 8, :], ACT.Copy,
                                     scale=gain_t[:, first, kt:kt + 1]).then_inc(turned_hi, 1)

        def act_stats(act, src, scratch, waits, n0):
            for c in range(CLS):
                waits(c)
                if c:
                    act.wait_ge(sq_done, CLS * n0 + c)
                nc.scalar.activation(scratch[:, :], src[:, c, :], ACT.Square,
                                     accum_out=stat[:, 0, c:c + 1]).then_inc(sq_done, 1)
            act.wait_ge(rstd_in, n0 + 1)
            nc.scalar.activation(stat[:, 1, :], stat[:, 1, :], ACT.Sqrt).then_inc(rstd_sqrt, 1)

        def act_tables(act, half):
            for q in range(4):
                b = 4 * half + q
                act.wait_ge(g_made, b + 1)
                if b >= 1:
                    act.wait_ge(g_stored, 16 * b)
                nc.scalar.activation(g_st[:, :, :, :].rearrange("p a b n -> p (a b n)"), pair(3),
                                     ACT.Copy).then_inc(g_copied, 1)
                act.wait_ge(g_copied, b + 1)
                act.dma_start(g_d[b], g_st[:, :, :, :].rearrange("p a b n -> p (a b n)")).then_inc(g_stored, 16)
            act.wait_ge(k_copied, 4 * half + 4)
            for e in range(OG):
                dst = bass.AP(tensor=k_d.tensor, offset=(group(4 * half, 0, e) * CH) * KPAD + (L - 1) * CH,
                              ap=[[KPAD, CH], [OG * CH * KPAD, 8], [1, P]])
                act.dma_start(dst, k_st[32 * e:32 * e + CH, :, :, :, :].rearrange("p q a b n -> p (q a b) n")
                              ).then_inc(k_stored, 16)

        def act_qkv(act, pr):
            with act.Fori(0, GROUPS) as g:
                for k in range(1, 13):
                    split_hi(act, B_QKV[pr] + k, 3 * g)
                    if k == 5:
                        nc.scalar.activation(q_t[:, bass.ds(g, 1), :, :].rearrange("p g h n -> p (g h n)"), pair(0),
                                             ACT.Copy).then_inc(q_copied, 1)
                act.wait_ge(piece_done, B_QKV[pr] + 12 + 12 * g)
                nc.scalar.activation(v_t[:, bass.ds(g, 1), :, :].rearrange("p g c n -> p (g c n)"), pair(2),
                                     ACT.Copy).then_inc(v_copied, 1)

        def act_attention(act, pr):
            n0 = 8 * pr
            for t in range(8 + 3):
                if t < 8:
                    n = n0 + t
                    act.wait_ge(negmax, n + 1)
                    nc.scalar.activation(sc[:, t % 2, :], sc[:, t % 2, :], ACT.Exp, bias=smx[:, t % 2, 2:3],
                                         scale=SCALE, accum_out=smx[:, t % 2, 3:4]).then_inc(exped, 1)
                if 1 <= t < 9:
                    n = n0 + t - 1
                    act.wait_ge(probs_t, n + 1)
                    if n >= 2:
                        act.wait_ge(heads, n - 1)
                    nc.scalar.activation(p_t[:, (t - 1) % 2, :], pair(2)[:, 0:768], ACT.Copy
                                         ).then_inc(probs_copied, 1)
                if t >= 3:
                    h, c, n = (t - 3) // CLS, (t - 3) % CLS, n0 + t - 3
                    act.wait_ge(heads, n + 1)
                    nc.scalar.activation(at_hi[:, 2 * pr + h, c * P:c * P + P], ps[:, 6 + (t - 3) % 2, 0:P], ACT.Copy
                                         ).then_inc(heads_hi, 1)

        @block.scalar
        def _(act):
            for ri, name in enumerate(("ssm_a_re", "ssm_a_im")):
                for gh in range(2):
                    act.dma_start(a_raw[:, ri, NST * gh:NST * gh + NST],
                                  A[name][0].rearrange("(q a e) p -> a q e p", q=4, a=2)[gh]).then_inc(par_in, 16)
            for gh in range(2):
                act.dma_start(prm[NST * gh:NST * gh + NST, 0, :].rearrange("p (q e) -> p q e", q=4),
                              bass.AP(tensor=A["ssm_log_dt"].tensor, offset=8 * gh, ap=[[0, NST], [16, 4], [1, 8]])
                              ).then_inc(dp_in, 16)
            for ri, name in enumerate(("ssm_c_re", "ssm_c_im")):
                act.dma_start(c_raw[:, ri, :, :, :].rearrange("p k a n -> p (k a) n"),
                              A[name][0].rearrange("(k e) c p -> (e c) k p", e=8)).then_inc(c_in, 16)
            for ri, name in enumerate(("ssm_b_re", "ssm_b_im")):
                for gh in range(2):
                    for q in range(4):
                        act.dma_start(b_raw[NST * gh:NST * gh + NST, ri, 8 * q:8 * q + 8, :],
                                      A[name][0, 16 * q + 8 * gh:16 * q + 8 * gh + 8].rearrange("g p c -> p g c")
                                      ).then_inc(b_in, 16)
            for i, name in enumerate(("norm_mix_pre", "norm_ffn_pre")):
                act.dma_start(gain_t[:, i, :], A[name][0].rearrange("(k p) -> p k", p=P),
                              allow_slow_non_contiguous=True).then_inc(gain_in, 16)
            act.wait_ge(const, 1)
            d_src = A["ssm_d"][0].rearrange("(m e i) -> e i m", m=2 * OCT, e=OG)
            for e in range(OG):
                act.dma_start(d_pad[32 * e:32 * e + CH, :], d_src[e],
                              allow_slow_non_contiguous=True).then_inc(gain_in, 16)

            act.wait_ge(dp_in, 32)
            nc.scalar.activation(prm[:, 1, :], prm[:, 0, :], ACT.Exp).then_inc(par_act, 1)
            act.wait_ge(par_dve, 1)
            nc.scalar.activation(prm[:, 6, :], prm[:, 4, :], ACT.Exp).then_inc(par_act, 1)
            act.wait_ge(par_dve, 2)
            nc.scalar.activation(prm[:, 9, :], prm[:, 7, :], ACT.Sin).then_inc(par_act, 1)
            nc.scalar.activation(prm[:, 10, :], prm[:, 8, :], ACT.Sin).then_inc(par_act, 1)

            act_stats(act, x_tok, x_sq, lambda c: act.wait_ge(x_in[c], 16), 0)
            split_hi(act, 0, 0)
            act.wait_ge(gain_in, 16 * (2 + OG))
            act_turn(act, 0)

            with act.Fori(0, 2) as it:
                for k in range(1, 9):
                    split_hi(act, B_U + k, 2 * it)
                    if k % 4 == 0:
                        s = k // 4 - 1
                        act.wait_ge(piece_done, k + 8 * it)
                        act.wait_ge(u_stored[s], 32 * it)
                        for f in range(2):
                            mm = nc.scalar.activation(
                                u_st[:, s, f, :].rearrange("p (b c n) -> p b c n", b=2, c=CLS),
                                ps[:, 2 * s + f, :].rearrange("p (c n b) -> p b c n", b=2, c=CLS), ACT.Copy)
                        mm.then_inc(u_copied, 1)
                        act.wait_ge(u_copied, 2 * it + s + 1)
                        for f in range(2):
                            act.dma_start(u_d[:, bass.ds(512 * it + 256 * s + P * f, P), :].rearrange("s p n -> p s n"),
                                          u_st[:, s, f, :].rearrange("p (s n) -> p s n", s=L)
                                          ).then_inc(u_stored[s], 16)
            act_tables(act, 0)
            act.wait_ge(u_stored[0], 64)
            act.wait_ge(u_stored[1], 64)
            act_qkv(act, 0)
            act_tables(act, 1)
            act_attention(act, 0)
            act_qkv(act, 1)
            act_attention(act, 1)
            with act.Fori(0, 2) as it:
                for k in range(1, 5):
                    split_hi(act, B_AU + k, it)
                    if k % 2 == 1:
                        act.wait_ge(piece_done, B_AU + k + 4 * it)
                        nc.scalar.activation(mrg[:, bass.ds(8 * it + 2 * (k - 1), 2), :].rearrange("p a n -> p (a n)"),
                                             pair(k - 1), ACT.Copy).then_inc(au_copied, 1)
            for t in range(SSM // P):
                act.wait_ge(y_back[t % 2], 16 * (t // 2 + 1))
                if t >= 2:
                    act.wait_ge(gelu_lo, t - 1)
                nc.scalar.activation(y_act[:, t % 2, :].rearrange("p (c n b) -> p b c n", b=2, c=CLS),
                                     y_in[:, t % 2, :].rearrange("p (b c n) -> p b c n", b=2, c=CLS),
                                     ACT.Gelu_apprx_tanh).then_inc(gelu, 1)
                act.wait_ge(gelu, t + 1)
                nc.scalar.activation(y_hi[:, t, :], y_act[:, t % 2, :], ACT.Copy).then_inc(gelu_hi, 1)
            with act.Fori(0, 8) as it:
                for k in range(1, 13):
                    split_hi(act, B_MRG + k, 3 * it)
                    if k % 4 == 0:
                        j = k // 4 - 1
                        if j == 0:
                            act.wait_ge(merge_step, 4 * it)
                        act.wait_ge(piece_done, B_MRG + k + 12 * it)
                        nc.scalar.activation((sig_a, sig_s, sig_g)[j][:, :], pair((0, 1, 3)[j]), ACT.Sigmoid
                                             ).then_inc(gated, 1)
            act.wait_ge(merge_step, 32)
            for q in range(4):
                nc.scalar.activation(a_hi[:, 4 * q:4 * q + 4, :], mrg[:, 4 * q:4 * q + 4, :], ACT.Copy
                                     ).then_inc(mrg_hi, 1)
            with act.Fori(0, 2) as it:
                for k in range(1, 17):
                    split_hi(act, B_WO + k, 4 * it)
            act_stats(act, o_t, sq_t, lambda c: act.wait_ge(o_copied, 4) if c == 0 else None, 1)
            act_stats(act, x2, sq_t, lambda c: act.wait_ge(x2_ready, c + 1), 2)
            act_turn(act, 1)

            def ffn(g, last):
                for k in range(1, 25):
                    if not (last and k == 24):
                        split_hi(act, B_FF + k, 6 * g)
                    if k in (4, 12):
                        act.wait_ge(piece_done, B_FF + k + 24 * g)
                        act.wait_ge(f_made, 2 * g + k // 8)
                        nc.scalar.activation(f_sg[:, :], pair(0), ACT.Silu).then_inc(silu, 1)
                    if k in (8, 16):
                        a = k // 8 - 1
                        act.wait_ge(f_made, 2 * g + a + 1)
                        nc.scalar.activation(f_hi[:, 2 * a:2 * a + 2, :].rearrange("p a n -> p (a n)"), f_t[:, :],
                                             ACT.Copy).then_inc(f_hi_ready, 1)

            with act.Fori(0, FFG - 1) as g:
                ffn(g, False)
            ffn(FFG - 1, True)
            act_stats(act, o_t, sq_t, lambda c: act.wait_ge(down_added, 16 * FFG) if c == 0 else None, 3)

        chain = [0]

        @block.vector
        def _(dve):
            def link(ins):
                chain[0] += 1
                ins.then_inc(dve_step, 1)
                dve.wait_ge(dve_step, chain[0])

            tt, ts, stt = nc.vector.tensor_tensor, nc.vector.tensor_scalar, nc.vector.scalar_tensor_tensor

            def dve_turn(first):
                for kt in range(KT):
                    dve.wait_ge(turned_hi, KT * first + kt + 1)
                    stt(a_lo[:, kt, :], ps[:, kt % 8, :], gain_t[:, first, kt:kt + 1], a_hi[:, kt, :].bitcast(F32),
                        ALU.mult, ALU.subtract).then_inc(turned_lo, 1)

            def dve_rstd(n0):
                dve.wait_ge(sq_done, CLS * (n0 + 1))
                ts(stat[:, 1, :], stat[:, 0, :], 1.0 / D, EPS, ALU.mult, ALU.add).then_inc(rstd_in, 1)
                dve.wait_ge(rstd_sqrt, n0 + 1)
                link(nc.vector.reciprocal(stat[:, 2, :], stat[:, 1, :]))

            def dve_tables(half):
                for q in range(4):
                    b = 4 * half + q
                    dve.wait_ge(k_made, b + 1)
                    if b == 4:
                        dve.wait_ge(k_stored, 16 * OG)
                    st = k_st[:, q // 2, :, q % 2, :]
                    link(nc.vector.tensor_copy(st, ps[:, k_banks[b % 2]:k_banks[b % 2] + 2, 0:P]))
                    i = 4 * (b // 2) + b % 2
                    tt(st[:, :, 0:CH], st[:, :, 0:CH], d_blk[:, i:i + 3:2, :], ALU.add).then_inc(k_copied, 1)

            def dve_qkv(pr):
                with dve.Fori(0, GROUPS) as g:
                    for k in range(1, 13):
                        split_lo(dve, B_QKV[pr] + k, 3 * g)
                        if k == 9:
                            nc.vector.tensor_copy(k_t[:, bass.ds(g, 1), :, :].rearrange("p g h n -> p (g h n)"),
                                                  pair(1)).then_inc(k_act, 1)

            def dve_attention(pr):
                n0 = 8 * pr
                for t in range(8 + 4):
                    if t < 8:
                        h, c, n = t // CLS, t % CLS, n0 + t
                        s = t % 2
                        dve.wait_ge(scores, n + 1)
                        if t % CLS == 0:
                            dve.wait_ge(bias_ready, 2 * pr + h + 1)
                        if n >= 2:
                            dve.wait_ge(probs_t, n - 1)
                        link(nc.vector.tensor_tensor_reduce(
                            out=sc[:, s, 0:512], in0=pair(s)[:, 0:512],
                            in1=bias[:, h, 3 - c:7 - c, :].rearrange("p a b -> p (a b)"), scale=1.0, scalar=-3e38,
                            op0=ALU.add, op1=ALU.max, accum_out=smx[:, s, 0:1]))
                        nc.vector.tensor_tensor_reduce(
                            out=sc[:, s, 512:768], in0=pair(s)[:, 512:768],
                            in1=bias[:, h, 7:9, :].rearrange("p a b -> p (a b)"), scale=1.0, scalar=smx[:, s, 0:1],
                            op0=ALU.add, op1=ALU.max, accum_out=smx[:, s, 1:2]).then_inc(biased, 1)
                        dve.wait_ge(biased, n + 1)
                        ts(smx[:, s, 2:3], smx[:, s, 1:2], -SCALE, None, ALU.mult).then_inc(negmax, 1)
                    if 1 <= t < 9:
                        n, s = n0 + t - 1, (t - 1) % 2
                        dve.wait_ge(exped, n + 1)
                        link(nc.vector.reciprocal(smx[:, s, 4:5], smx[:, s, 3:4]))
                        ts(sc[:, s, :], sc[:, s, :], smx[:, s, 4:5], None, ALU.mult).then_inc(normed, 1)
                    if t >= 4:
                        h, c, n = (t - 4) // CLS, (t - 4) % CLS, n0 + t - 4
                        dve.wait_ge(heads_hi, n + 1)
                        qs = slice(c * P, c * P + P)
                        tt(at_lo[:, 2 * pr + h, qs], ps[:, 6 + t % 2, 0:P], at_hi[:, 2 * pr + h, qs].bitcast(F32),
                           ALU.subtract).then_inc(heads_lo, 1)

            DT, ARE, AIM, RE, TH, ER, ANG, CANG, SIN, COS, T0, T1, T2, T3, QR, QI = (
                1, 2, 3, 4, 5, 6, 7, 8, 9, 10, 11, 12, 13, 14, 15, 16)

            def r(i):
                return prm[:, i, :]

            nc.vector.memset(ps[:, 4:6, 0:256], 0.0).then_inc(k_bank, 1)
            dve.wait_ge(par_tr, 1)
            dve.wait_ge(par_act, 1)
            nc.vector.tensor_copy(prm[:, ARE:AIM + 1, :], ps[:, 0, 0:2 * HG].rearrange("p (a g) -> p a g", a=2))
            nc.vector.tensor_copy(c_t[:, 0, :, :].rearrange("p g c -> p (g c)"), ps[:, 1, :])
            ts(c_t[:, 1, :, :].rearrange("p g c -> p (g c)"), ps[:, 2, :], -1.0, None, ALU.mult)
            link(ts(pen[:, :], ps[:, 3, 0:P], -BIG, BIG, ALU.mult, ALU.add))
            tt(r(RE), r(ARE), r(DT), ALU.mult).then_inc(par_dve, 1)
            link(tt(r(TH), r(AIM), r(DT), ALU.mult))
            link(ts(r(T0), r(TH), 1.0 / TWO_PI, ROUND, ALU.mult, ALU.add))
            link(ts(r(T1), r(T0), ROUND, None, ALU.subtract))
            link(stt(r(T2), r(T1), -PI_A, r(TH), ALU.mult, ALU.add))
            link(stt(r(T3), r(T1), -PI_B, r(T2), ALU.mult, ALU.add))
            link(stt(r(T2), r(T1), -PI_C, r(T3), ALU.mult, ALU.add))
            link(ts(r(ANG), r(T2), 3.1415925, -3.1415925, ALU.min, ALU.max))
            link(ts(r(T3), r(ANG), -1.0, None, ALU.mult))
            link(tt(r(T3), r(T3), r(ANG), ALU.max))
            ts(r(CANG), r(T3), -1.0, math.pi / 2, ALU.mult, ALU.add).then_inc(par_dve, 1)
            link(tt(r(T0), r(ARE), r(ARE), ALU.mult))
            link(tt(r(T1), r(AIM), r(AIM), ALU.mult))
            link(tt(r(T0), r(T0), r(T1), ALU.add))
            link(nc.vector.reciprocal(r(T1), r(T0)))
            dve.wait_ge(par_act, 4)
            link(nc.vector.memset(lam[:, 0, 0, :], 1.0))
            link(nc.vector.memset(lam[:, 0, 1, :], 0.0))
            link(tt(lam[:, 1, 0, :], r(ER), r(COS), ALU.mult))
            link(tt(lam[:, 1, 1, :], r(ER), r(SIN), ALU.mult))
            link(ts(r(T0), lam[:, 1, 0, :], -1.0, None, ALU.add))
            link(tt(r(T2), r(T0), r(ARE), ALU.mult))
            link(tt(r(T3), lam[:, 1, 1, :], r(AIM), ALU.mult))
            link(tt(r(T2), r(T2), r(T3), ALU.add))
            link(tt(r(QR), r(T2), r(T1), ALU.mult))
            link(tt(r(T2), lam[:, 1, 1, :], r(ARE), ALU.mult))
            link(tt(r(T3), r(T0), r(AIM), ALU.mult))
            link(tt(r(T2), r(T2), r(T3), ALU.subtract))
            tt(r(QI), r(T2), r(T1), ALU.mult).then_inc(par_dve, 1)
            dve.wait_ge(const, 1)
            dve.wait_ge(gain_in, 16 * (2 + OG))
            link(nc.vector.tensor_reduce(e16[:, :], ident[:, :].rearrange("p (j o) -> p o j", j=4)[:, 0:CH, :],
                                         AX, ALU.add))
            tt(d_blk[:, :, :],
               e16[:, :].unsqueeze(1).broadcast_to([P, 2 * OCT, CH]),
               d_pad[:, :].unsqueeze(2).broadcast_to([P, 2 * OCT, CH]), ALU.mult)

            dve_rstd(0)
            for c in range(CLS):
                ts(x_tok[:, c, :], x_tok[:, c, :], stat[:, 2, c:c + 1], None, ALU.mult).then_inc(scaled, 1)
            split_lo(dve, 0, 0)
            dve_turn(0)
            with dve.Fori(0, 2) as it:
                for k in range(1, 9):
                    split_lo(dve, B_U + k, 2 * it)
            dve_tables(0)
            dve_qkv(0)
            dve_tables(1)
            dve.wait_ge(h_stored, 16 * OCT)
            dve.wait_ge(g_stored, 16 * OCT)
            dve_attention(0)
            for b in range(OCT):
                dve.wait_ge(s_made, b + 1)
                nc.vector.tensor_copy(s_t[:, OG * b:OG * b + OG, :, :].rearrange("p e r n -> p (e r n)"),
                                      ps[:, b % 2, :]).then_inc(s_copied, 1)
            dve_qkv(1)
            dve_attention(1)
            with dve.Fori(0, 2) as it:
                for k in range(1, 5):
                    split_lo(dve, B_AU + k, it)
                    if k % 2 == 0:
                        dve.wait_ge(piece_done, B_AU + k + 4 * it)
                        dve.wait_ge(au_copied, k - 1 + 4 * it)
                        nc.vector.tensor_copy(mrg[:, bass.ds(8 * it + 2 * (k - 1), 2), :].rearrange("p a n -> p (a n)"),
                                              pair(k - 1)).then_inc(au_copied, 1)
            for b in range(OCT):
                dve.wait_ge(y_made, b + 1)
                for gh in range(2):
                    g = group(b, gh, 0)
                    ins = nc.vector.tensor_copy(u_all[:, g:g + OG, :].rearrange("p e n -> p (e n)"),
                                                ps[:, 2 * (b % 2) + gh, 0:OG * NCH])
                ins.then_inc(y_copied, 1)
            for t in range(SSM // P):
                dve.wait_ge(gelu_hi, t + 1)
                tt(y_lo[:, t, :], y_act[:, t % 2, :], y_hi[:, t, :].bitcast(F32), ALU.subtract).then_inc(gelu_lo, 1)
            with dve.Fori(0, 8) as it:
                for k in range(1, 13):
                    split_lo(dve, B_MRG + k, 3 * it)
                    m2 = mrg[:, bass.ds(2 * it, 2), :].rearrange("p a n -> p (a n)")
                    if k == 8:
                        dve.wait_ge(gated, 3 * it + 2)
                        tt(m2, m2, sig_a[:, :], ALU.mult).then_inc(merge_step, 1)
                dve.wait_ge(gated, 3 * it + 3)
                tt(sig_g[:, :], pair(2), sig_g[:, :], ALU.mult).then_inc(merge_step, 1)
                dve.wait_ge(merge_step, 4 * it + 2)
                tt(sig_g[:, :], sig_g[:, :], sig_s[:, :], ALU.mult).then_inc(merge_step, 1)
                dve.wait_ge(merge_step, 4 * it + 3)
                tt(m2, m2, sig_g[:, :], ALU.add).then_inc(merge_step, 1)
            for q in range(4):
                dve.wait_ge(mrg_hi, q + 1)
                tt(a_lo[:, 4 * q:4 * q + 4, :], mrg[:, 4 * q:4 * q + 4, :], a_hi[:, 4 * q:4 * q + 4, :].bitcast(F32),
                   ALU.subtract).then_inc(mrg_lo, 1)
            with dve.Fori(0, 2) as it:
                for k in range(1, 17):
                    split_lo(dve, B_WO + k, 4 * it)
                    if k % 8 == 0:
                        dve.wait_ge(piece_done, B_WO + k + 16 * it)
                        nc.vector.tensor_copy(o_t[:, :, bass.ds(1024 * it + 512 * (k // 8 - 1), 512)],
                                              ps[:, 4 * (k // 8 - 1):4 * (k // 8), :]).then_inc(o_copied, 1)
            dve_rstd(1)
            dve.wait_ge(x_again, 16)
            dve.wait_ge(gb_in[0], 16)
            for c in range(CLS):
                link(stt(o_t[:, c, :], o_t[:, c, :], stat[:, 2, c:c + 1], gain_b[:, :], ALU.mult, ALU.mult))
                tt(x2[:, c, :], x2[:, c, :], o_t[:, c, :], ALU.add).then_inc(x2_ready, 1)
            dve_rstd(2)
            dve.wait_ge(x2_ready, CLS)
            for c in range(CLS):
                ts(o_t[:, c, :], x2[:, c, :], stat[:, 2, c:c + 1], None, ALU.mult).then_inc(scaled, 1)
            dve_turn(1)

            def ffn(g, last):
                for k in range(1, 25):
                    if not (last and k == 24):
                        split_lo(dve, B_FF + k, 6 * g)
                    if k in (8, 16):
                        a = k // 8 - 1
                        dve.wait_ge(piece_done, B_FF + k + 24 * g)
                        dve.wait_ge(silu, 2 * g + a + 1)
                        tt(f_t[:, :], pair(1), f_sg[:, :], ALU.mult).then_inc(f_made, 1)
                        dve.wait_ge(f_hi_ready, 2 * g + a + 1)
                        tt(f_lo[:, 2 * a:2 * a + 2, :].rearrange("p a n -> p (a n)"), f_t[:, :],
                           f_hi[:, 2 * a:2 * a + 2, :].rearrange("p a n -> p (a n)").bitcast(F32), ALU.subtract
                           ).then_inc(f_lo_ready, 1)
                    if k >= 18 and k % 2 == 0:
                        d = (k - 18) // 2
                        if d == 0:
                            dve.wait_ge(acc_zero, 1)
                        for c in range(CLS):
                            if c < CLS - 1:
                                dve.wait_ge(down, 12 * g + 3 * d + c + 1)
                            else:
                                dve.wait_ge(piece_done, B_FF + k + 24 * g)
                            o = o_t[:, c, 512 * d:512 * d + 512]
                            tt(o, o, ps[:, 4 + c, :], ALU.add).then_inc(down_added, 1)

            with dve.Fori(0, FFG - 1) as g:
                ffn(g, False)
            ffn(FFG - 1, True)
            dve_rstd(3)
            dve.wait_ge(gb_in[1], 16)
            for c in range(CLS):
                link(stt(o_t[:, c, :], o_t[:, c, :], stat[:, 2, c:c + 1], gain_b[:, :], ALU.mult, ALU.mult))
                tt(x2[:, c, :], x2[:, c, :], o_t[:, c, :], ALU.add).then_inc(out_ready, 1)

        @block.gpsimd
        def _(pool):
            steps = [0]

            def link(ins):
                steps[0] += 1
                ins.then_inc(pool_step, 1)
                pool.wait_ge(pool_step, steps[0])

            tt, ts = nc.gpsimd.tensor_tensor, nc.gpsimd.tensor_scalar
            nc.gpsimd.memset(zero[:, :], 0.0)
            nc.gpsimd.memset(d_pad[:, :], 0.0)
            nc.gpsimd.memset(hot[:, :], 1.0)
            link(nc.gpsimd.memset(ident[:, :], 0.0))
            nc.gpsimd.affine_select(out=hot[:, :].rearrange("p (a b) -> p a b", b=4),
                                    in_=hot[:, :].rearrange("p (a b) -> p a b", b=4), compare_op=ALU.is_equal,
                                    fill=0.0, base=0, pattern=[[0, P // 4], [1, 4]], channel_multiplier=-1)
            nc.gpsimd.affine_select(out=ident[:, :], in_=ident[:, :], compare_op=ALU.not_equal, fill=1.0, base=0,
                                    pattern=[[-1, P]], channel_multiplier=1).then_inc(const, 1)
            for h in range(2):
                pool.dma_start(k_d[512 * h:512 * h + 512, 0:(L - 1) * CH].rearrange("(a p) n -> p a n", p=P),
                               zero[:, :].rearrange("p (a n) -> p a n", a=4)).then_inc(zero_stored, 16)

            pool.wait_ge(par_dve, 3)
            pool.wait_ge(b_in, 256)
            q16 = [prm[:, i, :].unsqueeze(2).broadcast_to([P, HG, CH]) for i in (15, 16)]
            tmp = [ptmp[:, i, 0:HG * CH].rearrange("p (g c) -> p g c", c=CH) for i in range(2)]
            for ri, (s0, s1, op) in enumerate(((0, 1, ALU.subtract), (1, 0, ALU.add))):
                tt(tmp[0], q16[0], b_raw[:, s0, :, :], ALU.mult)
                link(tt(tmp[1], q16[1], b_raw[:, s1, :, :], ALU.mult))
                link(tt(b_bar[:, ri, :, :], tmp[0], tmp[1], op))

            def power(lo, n, src):
                shape = [P, n, HG]
                ar, ai = (lam[:, lo:lo + 1, j, :].broadcast_to(shape) for j in range(2))
                br, bi = (lam[:, 1:1 + n, j, :] for j in range(2))
                t0, t1 = (ptmp[:, j, 0:n * HG].rearrange("p (n g) -> p n g", g=HG) for j in range(2))
                for ri, (x, y, op) in enumerate(((br, bi, ALU.subtract), (bi, br, ALU.add))):
                    tt(t0, ar, x, ALU.mult)
                    link(tt(t1, ai, y, ALU.mult))
                    link(tt(lam[:, lo + 1:lo + 1 + n, ri, :], t0, t1, op))

            power(1, 1, 1)
            power(2, 2, 1)
            power(4, 4, 1)
            for s in range(L):
                nc.gpsimd.tensor_copy(lam_r[:, s, :, :], lam[:, L - 1 - s, :, :])
            for j in range(2):
                nc.gpsimd.tensor_copy(scan_a[:, 0, :, j], lam[:, L, 0, :])
            ts(scan_a[:, 1, :, 0], lam[:, L, 1, :], -1.0, None, ALU.mult)
            link(nc.gpsimd.tensor_copy(scan_a[:, 1, :, 1], lam[:, L, 1, :]))

            def tables(half):
                for q in range(4):
                    b = 4 * half + q
                    g0 = OG * b
                    if half and q == 0:
                        pool.wait_ge(k_made, 4)
                        pool.wait_ge(g_made, 4)
                        pool.wait_ge(h_stored, 16 * 4)
                    gs = slice(g0, g0 + OG)
                    for dst, pw, src, n, signs in ((bl, lam_r, b_bar, L, (ALU.subtract, ALU.add)),
                                                   (hc, lam, c_t, L + 1, (ALU.add, ALU.subtract))):
                        shape = [P, OG, n, CH]
                        lr, li = (pw[:, 0:n, j, gs].rearrange("p n e -> p e n").unsqueeze(3).broadcast_to(shape)
                                  for j in range(2))
                        xr, xi = (src[:, j, gs, :].unsqueeze(2).broadcast_to(shape) for j in range(2))
                        t0, t1 = (ptmp[:, j, 0:OG * n * CH].rearrange("p (e n c) -> p e n c", e=OG, c=CH)
                                  for j in range(2))
                        for ri, (x, y) in enumerate(((xr, xi), (xi, xr))):
                            tt(t0, lr, x, ALU.mult)
                            link(tt(t1, li, y, ALU.mult))
                            last = tt(dst[:, q, :, ri, :, :], t0, t1, signs[ri])
                            if dst is hc and ri:
                                last.then_inc(tab_ready, 1)
                                pool.wait_ge(tab_ready, b + 1)
                            else:
                                link(last)
                    pool.dma_start(h_d[b], hc[:, q, :, :, :, :].rearrange("p e r k o -> p (e r) (k o)")
                                   ).then_inc(h_stored, 16)
            tables(0)
            tables(1)

            def biases(pr):
                for h in range(2):
                    if pr:
                        pool.wait_ge(biased, 8)
                    u7, u2 = bias[:, h, 0:7, :], bias[:, h, 7:9, :]
                    nc.gpsimd.iota(u7, pattern=[[-1, 7], [-CLS, P]], base=3, channel_multiplier=CLS,
                                   allow_small_or_imprecise_dtypes=True)
                    link(nc.gpsimd.iota(u2, pattern=[[0, 2], [-CLS, P]], base=0, channel_multiplier=CLS,
                                        allow_small_or_imprecise_dtypes=True))
                    nc.gpsimd.affine_select(out=u2, in_=u2, compare_op=ALU.is_ge, fill=BIG, base=0,
                                            pattern=[[0, 2], [-CLS, P]], channel_multiplier=CLS)
                    link(nc.gpsimd.affine_select(out=u7, in_=u7, compare_op=ALU.is_ge, fill=BIG, base=3,
                                                 pattern=[[-1, 7], [-CLS, P]], channel_multiplier=CLS))
                    link(nc.gpsimd.affine_select(out=u7, in_=u7, compare_op=ALU.is_ge, fill=BIG, base=WINDOW0 - 3,
                                                 pattern=[[1, 7], [CLS, P]], channel_multiplier=-CLS))
                    link(tt(bias[:, h, 8, :], bias[:, h, 8, :], pen[:, :], ALU.add))
                    ts(u7, u7, -slope(2 * pr + h) / SCALE, None, ALU.mult)
                    ts(bias[:, h, 7, :], bias[:, h, 7, :], -slope(HEADS + 2 * pr + h) / SCALE, None, ALU.mult)
                    ts(bias[:, h, 8, :], bias[:, h, 8, :], -slope(2 * HEADS + 2 * pr + h) / SCALE, None, ALU.mult
                       ).then_inc(bias_ready, 1)

            biases(0)
            pool.wait_ge(u_stored[0], 64)
            pool.wait_ge(u_stored[1], 64)
            pool.wait_ge(g_stored, 16 * OCT)
            pool.wait_ge(k_stored, 16 * 2 * OG)
            pool.wait_ge(h_stored, 16 * OCT)
            for s in range(L):
                pool.dma_start(u_all[CH * s:CH * s + CH, :, :], u_d[s].rearrange("(g i) n -> i g n", i=CH)
                               ).then_inc(u_in, 16)
            pool.wait_ge(heads_lo, 8)
            for b in range(OCT):
                s = b % 2
                if b >= 2:
                    pool.wait_ge(s_made, b - 1)
                pool.dma_start(g_r[:, s, :, :, :].rearrange("p e r n -> p (e r n)"), g_d[b]).then_inc(g_in[s], 16)
            pool.wait_ge(s_copied, OCT)
            with pool.Fori(0, NCH - 1) as n:
                prev = s_t[:, :, :, bass.ds(n, 1)].rearrange("p g r n -> p g (r n)")
                tt(scan_t[:, 0, :, :], prev, scan_a[:, 0, :, :], ALU.mult)
                for r in range(2):
                    other = s_t[:, :, 1 - r, bass.ds(n, 1)].rearrange("p g n -> p (g n)")
                    last = tt(scan_t[:, 1, :, r], other, scan_a[:, 1, :, r], ALU.mult)
                last.then_inc(scan_step, 1)
                pool.wait_ge(scan_step, 3 * n + 1)
                tt(scan_t[:, 0, :, :], scan_t[:, 0, :, :], scan_t[:, 1, :, :], ALU.add).then_inc(scan_step, 1)
                pool.wait_ge(scan_step, 3 * n + 2)
                cur = s_t[:, :, :, bass.ds(n + 1, 1)].rearrange("p g r n -> p g (r n)")
                tt(cur, cur, scan_t[:, 0, :, :], ALU.add).then_inc(scan_step, 1)
                pool.wait_ge(scan_step, 3 * n + 3)
            biases(1)
            pool.wait_ge(zero_stored, 32)

            def lag_tables(q):
                for s in range(L):
                    src = bass.AP(tensor=k_d.tensor, offset=16 * q * CH * KPAD + (L - 1 - s) * CH,
                                  ap=[[KPAD, CH], [CH * KPAD, 16], [1, P]])
                    pool.dma_start(t_q[q][CH * s:CH * s + CH, :, :], src).then_inc(t_in[q], 16)

            def state_tables(b):
                pool.dma_start(h_r[b % 2][:, :, :, :].rearrange("p e r n -> p (e r) n"), h_d[b, :, :, CH:]
                               ).then_inc(h_in[b % 2], 16)

            pool.wait_ge(heads_lo, 16)
            for b in range(2):
                state_tables(b)
            for q in range(2):
                lag_tables(q)
            pool.wait_ge(piece_done, B_MRG)
            for q in range(2, 4):
                lag_tables(q)
            for b in range(2, OCT):
                pool.wait_ge(y_made, b - 1)
                state_tables(b)
            pool.wait_ge(y_copied, OCT)
            for s in range(L):
                pool.dma_start(y_d[s].rearrange("(g o) n -> o g n", o=CH), u_all[CH * s:CH * s + CH, :, :]
                               ).then_inc(y_stored, 16)
            pool.wait_ge(y_stored, 16 * L)
            for t in range(SSM // P):
                if t >= 2:
                    pool.wait_ge(gelu, t - 1)
                pool.dma_start(y_in[:, t % 2, :].rearrange("p (s n) -> p s n", s=L),
                               y_d[:, t * P:t * P + P, :].rearrange("s p n -> p s n")).then_inc(y_back[t % 2], 16)
            pool.wait_ge(turned, 2 * KT)
            nc.gpsimd.memset(o_t[:, :, :].rearrange("p c d -> p (c d)"), 0.0).then_inc(acc_zero, 1)


_INS = ["x", "norm_mix_pre", "w_in", "w_attn_up", "ssm_a_re", "ssm_a_im", "ssm_log_dt", "ssm_b_re", "ssm_b_im",
        "ssm_c_re", "ssm_c_im", "ssm_d", "w_glu_v", "w_glu_g", "w_out", "norm_mix_post", "norm_ffn_pre",
        "w_ffn_gate", "w_ffn_up", "w_ffn_down", "norm_ffn_post"]


def kernel(**inputs):
    import numpy as _np
    import concourse.bacc as _bacc
    from concourse import mybir as _mybir
    from concourse.bass_utils import run_bass_kernel_spmd as _run

    nc = _bacc.Bacc("TRN2", target_bir_lowering=False, num_devices=1)
    arrays, aps = {}, {}
    for name in _INS:
        a = _np.ascontiguousarray(inputs[name])
        arrays[f"in_{name}"] = a
        aps[name] = nc.dram_tensor(f"in_{name}", a.shape, _mybir.dt.from_np(a.dtype), kind="ExternalInput").ap()
    out = nc.dram_tensor("out_0", (1, SEQ, D), _mybir.dt.float32, kind="ExternalOutput").ap()
    build(nc, aps, out)
    r = _run(nc, [arrays], core_ids=[0])
    return r.results[0]["out_0"]
```

```python
from contextlib import ExitStack
import math

import concourse.bass as bass
from concourse import mybir

F32 = mybir.dt.float32
F32R = mybir.dt.float32r
ALU = mybir.AluOpType
ACT = mybir.ActivationFunctionType
AX = mybir.AxisListType.X

P = 128
SEQ = 512
D = 2048
CLS = SEQ // P
KT = D // P
EPS = 1e-6
HEADS = 4
GROUPS = 3
HQ = HEADS * GROUPS * P
SCALE = float(P) ** -0.5
WINDOW0 = 128
BIG = 1e30
SSM = 1024
CH = 16
HG = SSM // CH // 2
NST = 64
L = 8
NCH = SEQ // L
OCT = 8
OG = HG // OCT
KPAD = (2 * L - 1) * CH
FF = 5632
FFG = FF // SEQ
U_COL = 3 * HQ
GA_COL = U_COL + SSM
GS_COL = GA_COL + D
TWO_PI = 2 * math.pi
PI_A = 6.28125
PI_B = 0.0019340515136718750
PI_C = TWO_PI - PI_A - PI_B
ROUND = 12582912.0

N_QKV = GROUPS * 12
B_U = 0
B_QKV = (16, 16 + N_QKV)
B_G0 = B_QKV[1] + N_QKV
B_AU = B_G0 + 8
B_Y0 = B_AU + 8
B_MRG = B_Y0 + 4
B_WO = B_MRG + 7 * 12
B_FF = B_WO + 32


START = 1


def group(b, gh, e):
    return 16 * (b // 2) + 8 * gh + OG * (b % 2) + e


def slope(head):
    return 2.0 ** (-8.0 * (head + 1) / (HEADS * GROUPS))


def build(nc, A, out):
    ctx = ExitStack()
    with ctx:
        def sem(name):
            return ctx.enter_context(nc.semaphore(name))

        base = 16512

        def at_kb(name, kb, shape, dt=F32):
            return nc.alloc_sbuf_tensor_at(name, shape, dt, offset=base + int(kb * 1024))

        a_hi = at_kb("a_hi", 0, [P, KT, SEQ], F32R)
        a_lo = at_kb("a_lo", 32, [P, KT, SEQ], F32R)
        raw = at_kb("raw", 64, [P, 4, 1024])
        w_hi = at_kb("w_hi", 80, [P, 2, 1024], F32R)
        w_lo = at_kb("w_lo", 88, [P, 2, 1024], F32R)
        ident = at_kb("ident", 96, [P, P])
        pen = at_kb("pen", 96.5, [P, P])
        scan_a = at_kb("scan_a", 97, [P, 2, HG, 2])
        scan_t = at_kb("scan_t", 97.5, [P, 2, HG, 2])
        hot = at_kb("hot", 98, [4, P])
        gain_t = at_kb("gain_t", 98.5, [P, 2, KT])
        stat = at_kb("stat", 98.75, [P, 3, CLS])
        smx = at_kb("smx", 98.875, [P, 3, 5])
        gain_rows = at_kb("gain_rows", 99, [2 * KT, P])
        sq_part = at_kb("sq_part", 99, [P, 4, CLS])
        x_tok = at_kb("x_tok", 100, [P, CLS, D])
        x_sq = at_kb("x_sq", 132, [P, D])
        u_st = at_kb("u_st", 100, [P, 2, 2, SEQ])
        q_t = at_kb("q_t", 99, [P, GROUPS, 2, SEQ])
        k_t = at_kb("k_t", 111, [P, GROUPS, 2, SEQ])
        v_t = at_kb("v_t", 123, [P, GROUPS, CLS, 2 * P])
        bias = at_kb("bias", 135, [P, 2, 9, P])
        at_hi = at_kb("at_hi", 144, [P, HEADS, SEQ], F32R)
        at_lo = at_kb("at_lo", 152, [P, HEADS, SEQ], F32R)
        s_t = at_kb("s_t", 160, [P, HG, 2, NCH])
        sc = at_kb("sc", 176, [P, 3, 768])
        p_t = at_kb("p_t", 185, [P, 2, 768])
        a_raw = at_kb("a_raw", 140, [HG, 2, 2 * NST])
        b_raw = at_kb("b_raw", 141, [P, 2, HG, CH])
        bl = at_kb("bl", 145, [P, 4, OG, 2, L, CH])
        hc = at_kb("hc", 161, [P, 4, OG, 2, L + 1, CH])
        g_st = at_kb("g_st", 179, [P, OG, 2, P])
        c_raw = at_kb("c_raw", 179, [P, 2, 4, 2, NST])
        b_bar = at_kb("b_bar", 183, [P, 2, HG, CH])
        c_t = at_kb("c_t", 187, [P, 2, HG, CH])
        lam = at_kb("lam", 191, [P, L + 1, 2, HG])
        lam_r = at_kb("lam_r", 193.25, [P, L, 2, HG])
        k_st = at_kb("k_st", 195.5, [P, 2, 2, 2, P])
        prm = at_kb("prm", 195.5, [P, 24, HG])
        ptmp = at_kb("ptmp", 199.5, [P, 2, OG * (L + 1) * CH])
        d_blk = at_kb("d_blk", 204, [P, 2 * OCT, CH])
        e16 = at_kb("e16", 205, [P, CH])
        d_pad = at_kb("d_pad", 205.125, [P, 2 * OCT])
        zero = at_kb("zero", 205.25, [P, 4 * (L - 1) * CH])
        g_r = at_kb("g_r", 177, [P, 2, OG, 2, P])
        u_all = at_kb("u_all", 191.75, [P, 2 * HG, NCH])
        t_q = [at_kb(f"t_q{q}", kb, [P, 16, P]) for q, kb in enumerate((177, 116, 100, 108))]
        h_r = [at_kb(f"h_r{s}", kb, [P, OG, 2, P]) for s, kb in enumerate((185, 140, 124, 128))]
        mrg = at_kb("mrg", 100, [P, KT, SEQ])
        sig_a = at_kb("sig_a", 132, [P, 1024])
        sig_s = at_kb("sig_s", 136, [P, 1024])
        sig_g = at_kb("sig_g", 140, [P, 1024])
        y_hi = at_kb("y_hi", 161, [P, SSM // P, SEQ], F32R)
        y_lo = at_kb("y_lo", 191.75, [P, SSM // P, SEQ], F32R)
        y_in = at_kb("y_in", 177, [P, 4, SEQ])
        y_act = at_kb("y_act", 185, [P, 2, SEQ])
        o_t = at_kb("o_t", 132, [P, CLS, D])
        x2 = at_kb("x2", 164, [P, CLS, D])
        gain_b = at_kb("gain_b", 196, [P, D])
        f_hi = at_kb("f_hi", 100, [P, 4, SEQ], F32R)
        f_lo = at_kb("f_lo", 108, [P, 4, SEQ], F32R)
        f_sg = at_kb("f_sg", 116, [P, 1024])
        f_t = at_kb("f_t", 120, [P, 1024])
        sq_t = at_kb("sq_t", 124, [P, D])
        o_gain = at_kb("o_gain", 0, [P, CLS, D])

        ps = ctx.enter_context(nc.psum_tensor("ps", [P, 8, 512], F32))

        def pair(p):
            return ps[:, 2 * p:2 * p + 2, :].rearrange("p b n -> p (b n)")

        u_d = nc.dram_tensor("u_d", [L, SSM, NCH], F32, kind="Internal").ap()
        y_d = nc.dram_tensor("y_d", [L, SSM, NCH], F32, kind="Internal").ap()
        g_d = nc.dram_tensor("g_d", [OCT, P, OG * 2 * P], F32, kind="Internal").ap()
        h_d = nc.dram_tensor("h_d", [OCT, P, OG * 2, (L + 1) * CH], F32, kind="Internal").ap()
        k_d = nc.dram_tensor("k_d", [SSM, KPAD], F32, kind="Internal").ap()

        landed = [sem(f"landed{s}") for s in range(4)]
        hi_ready = sem("hi_ready")
        lo_ready = sem("lo_ready")
        piece_done = sem("piece_done")
        x_in = [sem(f"x_in{c}") for c in range(CLS)]
        par_in = sem("par_in")
        c_in = sem("c_in")
        gain_in = sem("gain_in")
        b_in = sem("b_in")
        dp_in = sem("dp_in")
        skip_in = sem("skip_in")
        mix_sq = sem("mix_sq")
        ffn_sq = sem("ffn_sq")
        o_gained = sem("o_gained")
        const = sem("const")
        pool_step = sem("pool_step")
        dve_step = sem("dve_step")
        act_step = sem("act_step")
        par_tr = sem("par_tr")
        par_banks = sem("par_banks")
        par_act = sem("par_act")
        par_dve = sem("par_dve")
        sq_done = sem("sq_done")
        rstd_in = sem("rstd_in")
        rstd_sqrt = sem("rstd_sqrt")
        scaled = sem("scaled")
        turned = sem("turned")
        turned_hi = sem("turned_hi")
        turned_lo = sem("turned_lo")
        u_copied = sem("u_copied")
        u_stored = [sem(f"u_stored{s}") for s in range(2)]
        tab_ready = sem("tab_ready")
        h_stored = sem("h_stored")
        zero_stored = sem("zero_stored")
        k_bank = sem("k_bank")
        k_made = sem("k_made")
        k_copied = sem("k_copied")
        k_stored = sem("k_stored")
        g_made = sem("g_made")
        g_copied = sem("g_copied")
        g_stored = sem("g_stored")
        q_copied = sem("q_copied")
        k_act = sem("k_act")
        v_copied = sem("v_copied")
        bias_ready = sem("bias_ready")
        scores = sem("scores")
        biased = sem("biased")
        negmax = sem("negmax")
        exped = sem("exped")
        normed = sem("normed")
        probs_t = sem("probs_t")
        probs_copied = sem("probs_copied")
        heads = sem("heads")
        heads_hi = sem("heads_hi")
        heads_lo = sem("heads_lo")
        g_in = [sem(f"g_in{s}") for s in range(2)]
        u_in = sem("u_in")
        s_made = sem("s_made")
        s_copied = sem("s_copied")
        scan_step = sem("scan_step")
        h_in = [sem(f"h_in{s}") for s in range(4)]
        t_in = [sem(f"t_in{q}") for q in range(4)]
        y_made = sem("y_made")
        y_copied = sem("y_copied")
        y_stored = [sem(f"y_stored{h}") for h in range(2)]
        y_back = [sem(f"y_back{s}") for s in range(4)]
        gelu = sem("gelu")
        gelu_hi = sem("gelu_hi")
        gelu_lo = sem("gelu_lo")
        au_copied = sem("au_copied")
        gated = sem("gated")
        merge_step = sem("merge_step")
        mrg_hi = sem("mrg_hi")
        mrg_lo = sem("mrg_lo")
        o_copied = sem("o_copied")
        x_again = sem("x_again")
        gb_in = [sem(f"gb_in{s}") for s in range(2)]
        x2_ready = sem("x2_ready")
        acc_zero = sem("acc_zero")
        silu = sem("silu")
        f_made = sem("f_made")
        f_hi_ready = sem("f_hi_ready")
        f_lo_ready = sem("f_lo_ready")
        down = sem("down")
        down_added = sem("down_added")
        out_ready = sem("out_ready")
        stored = sem("stored")

        def load(sp, m, quads, w, row_tiles, rows0, cols0, n):
            if not isinstance(rows0, int):
                rows0 = sp.snap(rows0)
            if not isinstance(cols0, int):
                cols0 = sp.snap(cols0)
            src = w_tiles(w, row_tiles, rows0, cols0, n)
            if m >= 4:
                sp.wait_ge(lo_ready, m - 3 + 4 * quads)
            sp.dma_start(raw[:, m % 4, :].rearrange("p (k n) -> p k n", n=src.shape[-1]), src
                         ).then_inc(landed[m % 4], 16)

        def split_hi(act, m, quads):
            act.wait_ge(landed[m % 4], 16 * (m // 4 + 1) + 16 * quads)
            if m >= 2:
                act.wait_ge(piece_done, m - 1 + 4 * quads)
            nc.scalar.activation(w_hi[:, m % 2, :], raw[:, m % 4, :], ACT.Copy).then_inc(hi_ready, 1)

        def split_lo(dve, m, quads):
            dve.wait_ge(hi_ready, m + 1 + 4 * quads)
            nc.vector.tensor_tensor(w_lo[:, m % 2, :], raw[:, m % 4, :], w_hi[:, m % 2, :].bitcast(F32),
                                    ALU.subtract).then_inc(lo_ready, 1)

        def piece_f(pe, m, quads, banks, x_hi, x_lo, kt0, first, last):
            pe.wait_ge(lo_ready, m + 1 + 4 * quads)
            wh = w_hi[:, m % 2, :].rearrange("p (k n) -> p k n", n=256)
            wl = w_lo[:, m % 2, :].rearrange("p (k n) -> p k n", n=256)
            for k in range(4):
                for f in range(2):
                    cols = slice(f * P, f * P + P)
                    o = ps[:, 2 * banks + f, :]
                    nc.tensor.matmul(o, wh[:, k, cols], x_hi[:, kt0 + k, :], start=first and k == 0, stop=False)
                    nc.tensor.matmul(o, wh[:, k, cols], x_lo[:, kt0 + k, :], start=False, stop=False)
                    mm = nc.tensor.matmul(o, wl[:, k, cols], x_hi[:, kt0 + k, :], start=False,
                                          stop=last and k == 3)
            mm.then_inc(piece_done, 1)

        def piece_v(pe, m, quads, banks, kt0, first, last):
            pe.wait_ge(lo_ready, m + 1 + 4 * quads)
            wh = w_hi[:, m % 2, :].rearrange("p (k n) -> p k n", n=256)
            wl = w_lo[:, m % 2, :].rearrange("p (k n) -> p k n", n=256)
            for k in range(4):
                for c in range(CLS):
                    o = ps[:, 2 * banks + c // 2, 256 * (c % 2):256 * (c % 2) + 256]
                    toks = slice(c * P, c * P + P)
                    nc.tensor.matmul(o, a_hi[:, kt0 + k, toks], wh[:, k, :], start=first and k == 0 and c % 2 == 0,
                                     stop=False, skip_group_check=True)
                    nc.tensor.matmul(o, a_hi[:, kt0 + k, toks], wl[:, k, :], start=False, stop=False,
                                     skip_group_check=True)
                    mm = nc.tensor.matmul(o, a_lo[:, kt0 + k, toks], wh[:, k, :], start=False,
                                          stop=last and k == 3, skip_group_check=True)
            mm.then_inc(piece_done, 1)

        def piece_t(pe, m, quads, bank0, x_hi, x_lo, kt0, first, last, before=None, done=None):
            pe.wait_ge(lo_ready, m + 1 + 4 * quads)
            wh = w_hi[:, m % 2, :].rearrange("p (k n) -> p k n", n=512)
            wl = w_lo[:, m % 2, :].rearrange("p (k n) -> p k n", n=512)
            for c in range(CLS):
                if before:
                    before(c)
                toks = slice(c * P, c * P + P)
                o = ps[:, bank0 + c, :]
                for k in range(2):
                    nc.tensor.matmul(o, x_hi[:, kt0 + k, toks], wh[:, k, :], start=first and k == 0, stop=False)
                    nc.tensor.matmul(o, x_hi[:, kt0 + k, toks], wl[:, k, :], start=False, stop=False)
                    mm = nc.tensor.matmul(o, x_lo[:, kt0 + k, toks], wh[:, k, :], start=False,
                                          stop=last and k == 1)
                if done is not None and c < CLS - 1:
                    mm.then_inc(done, 1)
            mm.then_inc(piece_done, 1)

        def w_tiles(w, row_tiles, rows0, cols0, n):
            return w[bass.ds(rows0, row_tiles * P), bass.ds(cols0, n)].rearrange("(k p) n -> p k n", p=P)

        w_in, w_up = A["w_in"][0], A["w_attn_up"][0]
        w_gv, w_gg, w_out = A["w_glu_v"][0], A["w_glu_g"][0], A["w_out"][0]
        w_fg, w_fu, w_fd = A["w_ffn_gate"][0], A["w_ffn_up"][0], A["w_ffn_down"][0]
        x_cls = A["x"][0].rearrange("(j c) d -> c j d", c=CLS)
        out_cls = out[0].rearrange("(j c) d -> c j d", c=CLS)

        block = ctx.enter_context(nc.Block())

        @block.sync
        def _(sp):
            for gh in range(2):
                sp.dma_start(a_raw[:, 1, NST * gh:NST * gh + NST],
                             A["ssm_a_im"][0].rearrange("(q a e) p -> a q e p", q=4, a=2)[gh]).then_inc(par_in, 16)
            for c in range(CLS):
                sp.dma_start(x_tok[:, c, :], x_cls[c]).then_inc(x_in[c], 16)
            for k in range(16):
                load(sp, B_U + k, 0, w_in, 4, 4 * P * (k % 4), U_COL + 256 * (k // 4), 256)
            for pr in range(2):
                with sp.Fori(0, GROUPS) as g:
                    for k in range(12):
                        col = HQ * (k // 4) + 256 * pr
                        load(sp, B_QKV[pr] + k, 3 * g, w_in, 4, 4 * P * (k % 4), 512 * g + col, 256)
            for k in range(8):
                load(sp, B_G0 + k, 0, w_in, 4, 4 * P * (k % 4), (GA_COL, GS_COL)[k // 4], 256)
            for k in range(8):
                load(sp, B_AU + k, 0, w_up, 4, 0, 256 * k, 256)
            for k in range(4):
                load(sp, B_Y0 + k, 0, (w_gv, w_gg)[k // 2], 4, 4 * P * (k % 2), 0, 256)
            with sp.Fori(2, 9) as it:
                for k in range(12):
                    if k < 8:
                        src = (w_in, 4, 4 * P * (k % 4), 256 * it + (GA_COL, GS_COL)[k // 4] - 256, 256)
                    else:
                        src = ((w_gv, w_gg)[k // 2 - 4], 4, 4 * P * (k % 2), 256 * it - 256, 256)
                    load(sp, B_MRG + k - 24, 3 * it, *src)
            with sp.Fori(0, 2) as it:
                for k in range(16):
                    load(sp, B_WO + k, 4 * it, w_out, 2, 2 * P * (k % 8), 1024 * it + 512 * (k // 8), 512)
            with sp.Fori(0, FFG) as g:
                for k in range(24):
                    if k < 16:
                        src = ((w_fg, w_fu)[k // 4 % 2], 4, 4 * P * (k % 4), 512 * g + 256 * (k // 8), 256)
                    else:
                        src = (w_fd, 2, 512 * g + 2 * P * (k % 2), 512 * ((k - 16) // 2), 512)
                    load(sp, B_FF + k, 6 * g, *src)
            for c in range(CLS):
                sp.wait_ge(out_ready, c + 1)
                sp.dma_start(out_cls[c], x2[:, c, :]).then_inc(stored, 16)
            sp.wait_ge(stored, 16 * CLS)

        k_banks = (4, 0)

        def pe_turn(pe, src, first):
            for kt in range(KT):
                n = KT * first + kt
                if kt >= 8:
                    pe.wait_ge(turned_lo, n - 7)
                for c in range(CLS):
                    if kt == 0:
                        pe.wait_ge(scaled, CLS * first + c + 1)
                    mm = nc.tensor.transpose(ps[:, kt % 8, c * P:c * P + P], src[:, c, kt * P:kt * P + P], ident[:, :])
                mm.then_inc(turned, 1)

        def pe_tables(pe, half):
            for q in range(4):
                b = 4 * half + q
                pe.wait_ge(tab_ready, b + 1)
                if b == 0:
                    pe.wait_ge(k_bank, 1)
                if b == 1:
                    pe.wait_ge(u_copied, START + 3)
                if b == 5:
                    pe.wait_ge(q_copied, START + 3)
                if b >= 2:
                    pe.wait_ge(k_copied, b - 1)
                for gh in range(2):
                    ph = slice(NST * gh, NST * gh + NST)
                    for e in range(OG):
                        for ri in range(2):
                            mm = nc.tensor.matmul(
                                ps[32 * e:32 * e + CH, k_banks[b % 2] + gh, 0:P],
                                b_bar[ph, ri, OG * b + e, :],
                                hc[ph, q, e, ri, 0:L, :].rearrange("p k o -> p (k o)"),
                                start=ri == 0, stop=ri == 1)
                mm.then_inc(k_made, 1)
                if b >= 1:
                    pe.wait_ge(g_copied, b)
                for e in range(OG):
                    for ri in range(2):
                        mm = nc.tensor.transpose(
                            pair(3)[:, (2 * e + ri) * P:(2 * e + ri) * P + P],
                            bl[:, q, e, ri, :, :].rearrange("p s i -> p (s i)"), ident[:, :])
                mm.then_inc(g_made, 1)

        def pe_qkv(pe, pr, g, between=None):
            for k in range(12):
                m, quads, kt0, first, last = B_QKV[pr] + k, 3 * g, 4 * (k % 4), k % 4 == 0, k % 4 == 3
                if k == 0:
                    pe.wait_ge(q_copied, START + 3 * pr + g)
                if k == 4:
                    pe.wait_ge(k_act, START + 3 * pr + g)
                if k == 8:
                    pe.wait_ge(v_copied, START + 3 * pr + g)
                if k < 8:
                    piece_f(pe, m, quads, k // 4, a_hi, a_lo, kt0, first, last)
                else:
                    piece_v(pe, m, quads, 2, kt0, first, last)
                if between:
                    between(k)

        def pe_attention(pe, pr):
            n0 = 8 * pr
            pe.wait_ge(q_copied, START + 3 * pr + 3)
            pe.wait_ge(k_act, START + 3 * pr + 3)
            pe.wait_ge(v_copied, START + 3 * pr + 3)
            for t in range(8 + 3):
                if t < 8:
                    h, c, n = t // CLS, t % CLS, n0 + t
                    if n >= 2:
                        pe.wait_ge(biased, n - 1)
                    qs = slice(c * P, c * P + P)
                    s2 = pair(t % 2)
                    nc.tensor.matmul(s2[:, 0:512], q_t[:, 0, h, qs], k_t[:, 0, h, :], start=True, stop=True)
                    nc.tensor.matmul(s2[:, 512:640], q_t[:, 1, h, qs], k_t[:, 1, h, qs], start=True, stop=True)
                    nc.tensor.matmul(s2[:, 640:768], q_t[:, 2, h, qs], k_t[:, 2, h, qs], start=True,
                                     stop=True).then_inc(scores, 1)
                if 2 <= t < 10:
                    n = n0 + t - 2
                    pe.wait_ge(normed, n + 1)
                    if n >= 1:
                        pe.wait_ge(probs_copied, n)
                    for k in range(6):
                        mm = nc.tensor.transpose(pair(2)[:, k * P:k * P + P], sc[:, (t - 2) % 3, k * P:k * P + P],
                                                 ident[:, :])
                    mm.then_inc(probs_t, 1)
                if t >= 3:
                    h, c, n = (t - 3) // CLS, (t - 3) % CLS, n0 + t - 3
                    pe.wait_ge(probs_copied, n + 1)
                    if n >= 2:
                        pe.wait_ge(heads_lo, n - 1)
                    es = slice(h * P, h * P + P)
                    for k in range(6):
                        v = v_t[:, 0, k, es] if k < CLS else v_t[:, k - 3, c, es]
                        mm = nc.tensor.matmul(ps[:, 6 + (t - 3) % 2, 0:P], v, p_t[:, (t - 3) % 2, k * P:k * P + P],
                                              start=k == 0, stop=k == 5)
                    mm.then_inc(heads, 1)

        def pe_chunk_inputs(pe, b):
            pe.wait_ge(g_in[b % 2], 16 * (b // 2 + 1))
            if b == 0:
                pe.wait_ge(u_in, 16 * L)
                pe.wait_ge(heads_lo, 8)
            if b >= 2:
                pe.wait_ge(s_copied, b - 1)
            for gh in range(2):
                for e in range(OG):
                    for ri in range(2):
                        col = (2 * e + ri) * NCH
                        mm = nc.tensor.matmul(
                            ps[NST * gh:NST * gh + NST, 6 + b % 2, col:col + NCH],
                            g_r[:, b % 2, e, ri, NST * gh:NST * gh + NST], u_all[:, group(b, gh, e), :],
                            start=True, stop=True)
            mm.then_inc(s_made, 1)

        def pe_outputs(pe, b):
            if b == 0:
                pe.wait_ge(scan_step, 3 * (NCH - 1))
            pe.wait_ge(h_in[b % 4], 16 * (b // 4 + 1))
            pe.wait_ge(t_in[b // 2], 16 * L)
            if b >= 2:
                pe.wait_ge(y_copied, b - 1)
            for gh in range(2):
                ph = slice(NST * gh, NST * gh + NST)
                for e in range(OG):
                    col, bank = e * NCH, 4 + 2 * (b % 2) + gh
                    g = group(b, gh, e)
                    nc.tensor.matmul(ps[:, bank, col:col + NCH], t_q[b // 2][:, g % 16, :], u_all[:, g, :],
                                     start=True, stop=True)
                    for ri in range(2):
                        mm = nc.tensor.matmul(ps[:, bank, col + 1:col + NCH], h_r[b % 4][ph, e, ri, :],
                                              s_t[ph, OG * b + e, ri, 0:NCH - 1], start=False, stop=True,
                                              skip_group_check=True)
            mm.then_inc(y_made, 1)

        @block.tensor
        def _(pe):
            pe.wait_ge(const, 1)
            pe.wait_ge(par_in, 64)
            for ri in range(2):
                nc.tensor.transpose(ps[:, 0, ri * HG:ri * HG + HG], a_raw[:, ri, :], ident[0:HG, 0:HG])
            nc.tensor.matmul(ps[:, 3, 0:P], hot[:, :], hot[:, :], start=True, stop=True).then_inc(par_tr, 1)
            pe.wait_ge(gain_in, 32)
            nc.tensor.transpose(ps[:, 4, 0:2 * KT], gain_rows[:, :], ident[0:2 * KT, 0:2 * KT])
            pe.wait_ge(c_in, 32)
            for ri in range(2):
                for k in range(4):
                    mm = nc.tensor.transpose(ps[:, 1 + ri, k * P:k * P + P],
                                             c_raw[:, ri, k, :, :].rearrange("p a b -> p (a b)"), ident[:, :])
            mm.then_inc(par_tr, 1)
            pe.wait_ge(par_banks, 1)
            pe_turn(pe, x_tok, 0)
            pe.wait_ge(turned_lo, KT)
            with pe.Fori(0, 2) as it:
                for k in range(8):
                    if k % 4 == 0:
                        pe.wait_ge(u_copied, START + 2 * it + k // 4)
                    piece_f(pe, B_U + k, 2 * it, k // 4, a_hi, a_lo, 4 * (k % 4), k % 4 == 0, k % 4 == 3)
            pe_tables(pe, 0)
            pe.wait_ge(u_copied, START + 4)
            pe.wait_ge(k_copied, 4)
            with pe.Fori(0, GROUPS) as g:
                pe_qkv(pe, 0, g)
            pe.wait_ge(v_copied, START + 3)
            pe_tables(pe, 1)
            pe.wait_ge(q_copied, START + 3)
            pe.wait_ge(k_copied, 8)
            pe.wait_ge(g_copied, 8)
            pe_attention(pe, 0)
            pe_qkv(pe, 1, 0, lambda k: pe_chunk_inputs(pe, k - 2) if 2 <= k < 2 + OCT else None)
            with pe.Fori(1, GROUPS) as g:
                pe_qkv(pe, 1, g)
            pe.wait_ge(s_copied, OCT)
            pe_attention(pe, 1)
            pe.wait_ge(heads_lo, 16)
            for k in range(8):
                piece_f(pe, B_G0 + k, 0, k // 4, a_hi, a_lo, 4 * (k % 4), k % 4 == 0, k % 4 == 3)
                if k >= 2:
                    pe_outputs(pe, k - 2)
            pe_outputs(pe, 6)
            pe_outputs(pe, 7)
            for k in range(8):
                if k < 2:
                    pe.wait_ge(gated, START + k + 1)
                if k == 2:
                    pe.wait_ge(y_copied, OCT)
                if k >= 4:
                    pe.wait_ge(au_copied, k - 3)
                piece_f(pe, B_AU + k, 0, k % 4, at_hi, at_lo, 0, True, True)
            pe.wait_ge(au_copied, 8)
            pe.wait_ge(gelu_lo, SSM // P)
            for k in range(4):
                piece_f(pe, B_Y0 + k, 0, k // 2 + 2, y_hi, y_lo, 4 * (k % 2), k % 2 == 0, k % 2 == 1)
            with pe.Fori(1, 8) as it:
                for k in range(12):
                    if k < 8:
                        if k == 0:
                            pe.wait_ge(gated, START + 3 * it)
                        piece_f(pe, B_MRG + k - 12, 3 * it, k // 4, a_hi, a_lo, 4 * (k % 4), k % 4 == 0, k % 4 == 3)
                    else:
                        if k % 2 == 0:
                            pe.wait_ge(merge_step, START + 4 * it)
                        piece_f(pe, B_MRG + k - 12, 3 * it, k // 2 - 2, y_hi, y_lo, 4 * (k % 2), k % 2 == 0, k % 2 == 1)
            pe.wait_ge(merge_step, START + 32)
            with pe.Fori(0, 2) as it:
                for k in range(16):
                    if k % 2 == 0 and k < 8:
                        pe.wait_ge(mrg_lo, k // 2 + 1)
                    if k % 8 == 0:
                        pe.wait_ge(o_copied, START + 2 * it + k // 8)
                    piece_t(pe, B_WO + k, 4 * it, 4 * (k // 8), a_hi, a_lo, 2 * (k % 8), k % 8 == 0, k % 8 == 7)
            pe.wait_ge(o_copied, START + 4)
            pe_turn(pe, o_t, 1)
            pe.wait_ge(turned_lo, 2 * KT)
            with pe.Fori(0, FFG) as g:
                for k in range(24):
                    m = B_FF + k
                    if k < 16:
                        if k % 8 == 0:
                            pe.wait_ge(silu, START + 2 * g + k // 8)
                        if k % 8 == 4:
                            pe.wait_ge(f_made, START + 2 * g + k // 8)
                        piece_f(pe, m, 6 * g, k // 4 % 2, a_hi, a_lo, 4 * (k % 4), k % 4 == 0, k % 4 == 3)
                    else:
                        d = (k - 16) // 2
                        if k < 18:
                            pe.wait_ge(f_lo_ready, 2 * g + k - 15)

                        def bank_free(c, d=d, k=k, g=g):
                            if k % 2 == 0:
                                if d == 0:
                                    if c == 0:
                                        pe.wait_ge(down_added, START + 16 * g)
                                else:
                                    pe.wait_ge(down_added, START + 16 * g + 4 * d + c - 3)

                        piece_t(pe, m, 6 * g, 4, f_hi, f_lo, 2 * (k % 2), k % 2 == 0, k % 2 == 1,
                                before=bank_free, done=down if k % 2 else None)

        def act_turn(act, first):
            for kt in range(KT):
                act.wait_ge(turned, KT * first + kt + 1)
                nc.scalar.activation(a_hi[:, kt, :], ps[:, kt % 8, :], ACT.Copy,
                                     scale=gain_t[:, first, kt:kt + 1]).then_inc(turned_hi, 1)

        def act_stats(act, src, scratch, waits, turn, between=None):
            for c in range(CLS):
                waits(c)
                if c:
                    act.wait_ge(sq_done, CLS * turn + c)
                nc.scalar.activation(scratch[:, :], src[:, c, :], ACT.Square,
                                     accum_out=stat[:, 0, c:c + 1]).then_inc(sq_done, 1)
                if between:
                    between(c)
            act_root(act, 2 * turn)

        def act_root(act, n):
            act.wait_ge(rstd_in, n + 1)
            nc.scalar.activation(stat[:, 1, :], stat[:, 1, :], ACT.Sqrt).then_inc(rstd_sqrt, 1)

        def act_tables(act, half):
            for q in range(4):
                b = 4 * half + q
                act.wait_ge(g_made, b + 1)
                if b >= 1:
                    act.wait_ge(g_stored, 16 * b)
                nc.scalar.activation(g_st[:, :, :, :].rearrange("p a b n -> p (a b n)"), pair(3),
                                     ACT.Copy).then_inc(g_copied, 1)
                act.wait_ge(g_copied, b + 1)
                act.dma_start(g_d[b], g_st[:, :, :, :].rearrange("p a b n -> p (a b n)")).then_inc(g_stored, 16)
            act.wait_ge(k_copied, 4 * half + 4)
            for e in range(OG):
                dst = bass.AP(tensor=k_d.tensor, offset=(group(4 * half, 0, e) * CH) * KPAD + (L - 1) * CH,
                              ap=[[KPAD, CH], [OG * CH * KPAD, 8], [1, P]])
                act.dma_start(dst, k_st[32 * e:32 * e + CH, :, :, :, :].rearrange("p q a b n -> p (q a b) n")
                              ).then_inc(k_stored, 16)

        def act_qkv(act, pr):
            with act.Fori(0, GROUPS) as g:
                for k in range(1, 13):
                    split_hi(act, B_QKV[pr] + k, 3 * g)
                    if k == 5:
                        nc.scalar.activation(q_t[:, bass.ds(g, 1), :, :].rearrange("p g h n -> p (g h n)"), pair(0),
                                             ACT.Copy).then_inc(q_copied, 1)
                act.wait_ge(piece_done, B_QKV[pr] + 12 + 12 * g)
                nc.scalar.activation(v_t[:, bass.ds(g, 1), :, :].rearrange("p g c n -> p (g c n)"), pair(2),
                                     ACT.Copy).then_inc(v_copied, 1)

        def act_attention(act, pr):
            n0 = 8 * pr
            for t in range(8 + 4):
                if t < 8:
                    n = n0 + t
                    act.wait_ge(negmax, n + 1)
                    nc.scalar.activation(sc[:, t % 3, :], sc[:, t % 3, :], ACT.Exp, bias=smx[:, t % 3, 2:3],
                                         scale=SCALE, accum_out=smx[:, t % 3, 3:4]).then_inc(exped, 1)
                if 2 <= t < 10:
                    n = n0 + t - 2
                    act.wait_ge(probs_t, n + 1)
                    if n >= 2:
                        act.wait_ge(heads, n - 1)
                    nc.scalar.activation(p_t[:, t % 2, :], pair(2)[:, 0:768], ACT.Copy).then_inc(probs_copied, 1)
                if t >= 4:
                    h, c, n = (t - 4) // CLS, (t - 4) % CLS, n0 + t - 4
                    act.wait_ge(heads, n + 1)
                    nc.scalar.activation(at_hi[:, 2 * pr + h, c * P:c * P + P], ps[:, 6 + t % 2, 0:P], ACT.Copy
                                         ).then_inc(heads_hi, 1)

        @block.scalar
        def _(act):
            for gh in range(2):
                act.dma_start(a_raw[:, 0, NST * gh:NST * gh + NST],
                              A["ssm_a_re"][0].rearrange("(q a e) p -> a q e p", q=4, a=2)[gh]).then_inc(par_in, 16)
            for gh in range(2):
                act.dma_start(prm[NST * gh:NST * gh + NST, 0, :].rearrange("p (q e) -> p q e", q=4),
                              bass.AP(tensor=A["ssm_log_dt"].tensor, offset=8 * gh, ap=[[0, NST], [16, 4], [1, 8]])
                              ).then_inc(dp_in, 16)
            for i, name in enumerate(("norm_mix_pre", "norm_ffn_pre")):
                act.dma_start(gain_rows[KT * i:KT * i + KT, :], A[name][0].rearrange("(k p) -> k p", p=P)
                              ).then_inc(gain_in, 16)
            for ri, name in enumerate(("ssm_c_re", "ssm_c_im")):
                act.dma_start(c_raw[:, ri, :, :, :].rearrange("p k a n -> p (k a) n"),
                              A[name][0].rearrange("(k e) c p -> (e c) k p", e=8)).then_inc(c_in, 16)
            for ri, name in enumerate(("ssm_b_re", "ssm_b_im")):
                for gh in range(2):
                    for q in range(4):
                        act.dma_start(b_raw[NST * gh:NST * gh + NST, ri, 8 * q:8 * q + 8, :],
                                      A[name][0, 16 * q + 8 * gh:16 * q + 8 * gh + 8].rearrange("g p c -> p g c")
                                      ).then_inc(b_in, 16)
            act.wait_ge(const, 1)
            d_src = A["ssm_d"][0].rearrange("(m e i) -> e i m", m=2 * OCT, e=OG)
            for e in range(OG):
                act.dma_start(d_pad[32 * e:32 * e + CH, :], d_src[e],
                              allow_slow_non_contiguous=True).then_inc(skip_in, 16)

            def between(c):
                if c == 0:
                    act.wait_ge(dp_in, 32)
                    nc.scalar.activation(prm[:, 1, :], prm[:, 0, :], ACT.Exp).then_inc(par_act, 1)
                if c == 1:
                    act.wait_ge(par_dve, 1)
                    nc.scalar.activation(prm[:, 6, :], prm[:, 4, :], ACT.Exp).then_inc(par_act, 1)
                if c == 2:
                    act.wait_ge(par_dve, 2)
                    nc.scalar.activation(prm[:, 9, :], prm[:, 7, :], ACT.Sin).then_inc(par_act, 1)
                    nc.scalar.activation(prm[:, 10, :], prm[:, 8, :], ACT.Sin).then_inc(par_act, 1)

            act_stats(act, x_tok, x_sq, lambda c: act.wait_ge(x_in[c], 16), 0, between)
            split_hi(act, 0, 0)
            act_turn(act, 0)

            with act.Fori(0, 2) as it:
                for k in range(1, 9):
                    split_hi(act, B_U + k, 2 * it)
                    if k % 4 == 0:
                        s = k // 4 - 1
                        act.wait_ge(piece_done, k + 8 * it)
                        act.wait_ge(u_stored[s], START + 32 * it)
                        for f in range(2):
                            mm = nc.scalar.activation(
                                u_st[:, s, f, :].rearrange("p (b c n) -> p b c n", b=2, c=CLS),
                                ps[:, 2 * s + f, :].rearrange("p (c n b) -> p b c n", b=2, c=CLS), ACT.Copy)
                        mm.then_inc(u_copied, 1)
                        act.wait_ge(u_copied, START + 2 * it + s + 1)
                        for f in range(2):
                            act.dma_start(u_d[:, bass.ds(512 * it + 256 * s + P * f, P), :].rearrange("s p n -> p s n"),
                                          u_st[:, s, f, :].rearrange("p (s n) -> p s n", s=L)
                                          ).then_inc(u_stored[s], 16)
            act_tables(act, 0)
            act.wait_ge(u_stored[0], START + 64)
            act.wait_ge(u_stored[1], START + 64)
            act_qkv(act, 0)
            act_tables(act, 1)
            act_attention(act, 0)
            act_qkv(act, 1)
            act_attention(act, 1)
            for k in range(1, 9):
                split_hi(act, B_G0 + k, 0)
                if k % 4 == 0:
                    act.wait_ge(piece_done, B_G0 + k)
                    nc.scalar.activation((sig_a, sig_s)[k // 4 - 1][:, :], pair(k // 4 - 1), ACT.Sigmoid
                                         ).then_inc(gated, 1)

            def act_gelu(t):
                act.wait_ge(y_back[t % 4], 16 * (t // 4 + 1))
                if t >= 2:
                    act.wait_ge(gelu_lo, t - 1)
                nc.scalar.activation(y_act[:, t % 2, :].rearrange("p (c n b) -> p b c n", b=2, c=CLS),
                                     y_in[:, t % 4, :].rearrange("p (b c n) -> p b c n", b=2, c=CLS),
                                     ACT.Gelu_apprx_tanh).then_inc(gelu, 1)
                act.wait_ge(gelu, t + 1)
                nc.scalar.activation(y_hi[:, t, :], y_act[:, t % 2, :], ACT.Copy).then_inc(gelu_hi, 1)

            for k in range(1, 9):
                split_hi(act, B_AU + k, 0)
                act.wait_ge(piece_done, B_AU + k)
                nc.scalar.activation(mrg[:, 2 * k - 2:2 * k, :].rearrange("p a n -> p (a n)"), pair((k - 1) % 4),
                                     ACT.Copy).then_inc(au_copied, 1)
                act_gelu(k - 1)

            def gate_glu(it, k):
                j = k // 4 - 1
                if j == 0:
                    act.wait_ge(merge_step, START + 4 * it)
                act.wait_ge(piece_done, B_MRG - 12 + k + 12 * it)
                nc.scalar.activation((sig_a, sig_s, sig_g)[j][:, :], pair((0, 1, 3)[j]), ACT.Sigmoid
                                     ).then_inc(gated, 1)

            for k in range(1, 5):
                split_hi(act, B_Y0 + k, 0)
            gate_glu(0, 12)
            with act.Fori(1, 8) as it:
                for k in range(1, 13):
                    split_hi(act, B_MRG - 12 + k, 3 * it)
                    if k % 4 == 0:
                        gate_glu(it, k)
            act.wait_ge(merge_step, START + 32)
            for q in range(4):
                nc.scalar.activation(a_hi[:, 4 * q:4 * q + 4, :], mrg[:, 4 * q:4 * q + 4, :], ACT.Copy
                                     ).then_inc(mrg_hi, 1)
            with act.Fori(0, 2) as it:
                for k in range(1, 17):
                    split_hi(act, B_WO + k, 4 * it)
                    if k in (9, 16):
                        b = (k - 1) // 8 - (k == 9)
                        act.wait_ge(piece_done, B_WO + 8 * b + 8 + 16 * it)
                        for c in range(CLS):
                            sq = nc.scalar.activation(
                                sq_t[:, 512 * c:512 * c + 512], ps[:, 4 * b + c, :], ACT.Square,
                                accum_out=sq_part[:, bass.ds(2 * it + b, 1), c:c + 1].rearrange("p a c -> p (a c)"))
                        sq.then_inc(mix_sq, 1)
            act_root(act, 1)
            act_stats(act, x2, sq_t, lambda c: act.wait_ge(x2_ready, c + 1), 1)
            act_turn(act, 1)

            def ffn(g, last, squares=None):
                for k in range(1, 25):
                    if not (last and k == 24):
                        split_hi(act, B_FF + k, 6 * g)
                    if squares and k >= 20 and k % 2 == 0:
                        squares((k - 20) // 2)
                    if k in (4, 12):
                        act.wait_ge(piece_done, B_FF + k + 24 * g)
                        act.wait_ge(f_made, START + 2 * g + k // 8)
                        nc.scalar.activation(f_sg[:, :], pair(0), ACT.Silu).then_inc(silu, 1)
                    if k in (8, 16):
                        a = k // 8 - 1
                        act.wait_ge(f_made, START + 2 * g + a + 1)
                        nc.scalar.activation(f_hi[:, 2 * a:2 * a + 2, :].rearrange("p a n -> p (a n)"), f_t[:, :],
                                             ACT.Copy).then_inc(f_hi_ready, 1)
                if squares:
                    squares(3)

            with act.Fori(0, FFG - 1) as g:
                ffn(g, False)

            def last_squares(d):
                for c in range(CLS):
                    act.wait_ge(down_added, START + 16 * (FFG - 1) + 4 * d + c + 1)
                    if d:
                        act.wait_ge(ffn_sq, CLS * (d - 1) + c + 1)
                    nc.scalar.activation(sq_t[:, 512 * c:512 * c + 512], o_t[:, c, 512 * d:512 * d + 512], ACT.Square,
                                         accum_out=sq_part[:, d, c:c + 1]).then_inc(ffn_sq, 1)

            ffn(FFG - 1, True, last_squares)
            act_root(act, 3)

        chain = [0]

        @block.vector
        def _(dve):
            def link(ins):
                chain[0] += 1
                ins.then_inc(dve_step, 1)
                dve.wait_ge(dve_step, chain[0])

            tt, ts, stt = nc.vector.tensor_tensor, nc.vector.tensor_scalar, nc.vector.scalar_tensor_tensor

            def dve_turn(first):
                for kt in range(KT):
                    dve.wait_ge(turned_hi, KT * first + kt + 1)
                    stt(a_lo[:, kt, :], ps[:, kt % 8, :], gain_t[:, first, kt:kt + 1], a_hi[:, kt, :].bitcast(F32),
                        ALU.mult, ALU.subtract).then_inc(turned_lo, 1)

            def dve_rstd(n, turn=None):
                if turn is None:
                    link(nc.vector.tensor_reduce(stat[:, 0, :], sq_part[:, :, :].rearrange("p d c -> p c d"), AX,
                                                 ALU.add))
                else:
                    dve.wait_ge(sq_done, CLS * (turn + 1))
                ts(stat[:, 1, :], stat[:, 0, :], 1.0 / D, EPS, ALU.mult, ALU.add).then_inc(rstd_in, 1)
                dve.wait_ge(rstd_sqrt, n + 1)
                link(nc.vector.reciprocal(stat[:, 2, :], stat[:, 1, :]))

            def dve_tables(half):
                for q in range(4):
                    b = 4 * half + q
                    dve.wait_ge(k_made, b + 1)
                    if b == 4:
                        dve.wait_ge(k_stored, 16 * OG)
                    st = k_st[:, q // 2, :, q % 2, :]
                    link(nc.vector.tensor_copy(st, ps[:, k_banks[b % 2]:k_banks[b % 2] + 2, 0:P]))
                    i = 4 * (b // 2) + b % 2
                    tt(st[:, :, 0:CH], st[:, :, 0:CH], d_blk[:, i:i + 3:2, :], ALU.add).then_inc(k_copied, 1)

            def dve_qkv(pr, g, between=None):
                for k in range(1, 13):
                    split_lo(dve, B_QKV[pr] + k, 3 * g)
                    if k == 9:
                        nc.vector.tensor_copy(k_t[:, bass.ds(g, 1), :, :].rearrange("p g h n -> p (g h n)"),
                                              pair(1)).then_inc(k_act, 1)
                    if between:
                        between(k)

            def dve_attention(pr):
                n0 = 8 * pr
                for t in range(8 + 4):
                    if t < 8:
                        h, c, n = t // CLS, t % CLS, n0 + t
                        s = t % 3
                        dve.wait_ge(scores, n + 1)
                        if t % CLS == 0:
                            dve.wait_ge(bias_ready, 2 * pr + h + 1)
                        if t >= 3 or pr:
                            dve.wait_ge(probs_t, n - 2 if t >= 3 else n0)
                        link(nc.vector.tensor_tensor_reduce(
                            out=sc[:, s, 0:512], in0=pair(t % 2)[:, 0:512],
                            in1=bias[:, h, 3 - c:7 - c, :].rearrange("p a b -> p (a b)"), scale=1.0, scalar=-3e38,
                            op0=ALU.add, op1=ALU.max, accum_out=smx[:, s, 0:1]))
                        nc.vector.tensor_tensor_reduce(
                            out=sc[:, s, 512:768], in0=pair(t % 2)[:, 512:768],
                            in1=bias[:, h, 7:9, :].rearrange("p a b -> p (a b)"), scale=1.0, scalar=smx[:, s, 0:1],
                            op0=ALU.add, op1=ALU.max, accum_out=smx[:, s, 1:2]).then_inc(biased, 1)
                        dve.wait_ge(biased, n + 1)
                        ts(smx[:, s, 2:3], smx[:, s, 1:2], -SCALE, None, ALU.mult).then_inc(negmax, 1)
                    if 1 <= t < 9:
                        n, s = n0 + t - 1, (t - 1) % 3
                        dve.wait_ge(exped, n + 1)
                        link(nc.vector.reciprocal(smx[:, s, 4:5], smx[:, s, 3:4]))
                        ts(sc[:, s, :], sc[:, s, :], smx[:, s, 4:5], None, ALU.mult).then_inc(normed, 1)
                    if t >= 4:
                        h, c, n = (t - 4) // CLS, (t - 4) % CLS, n0 + t - 4
                        dve.wait_ge(heads_hi, n + 1)
                        qs = slice(c * P, c * P + P)
                        tt(at_lo[:, 2 * pr + h, qs], ps[:, 6 + t % 2, 0:P], at_hi[:, 2 * pr + h, qs].bitcast(F32),
                           ALU.subtract).then_inc(heads_lo, 1)

            def dve_gelu_lo(t):
                dve.wait_ge(gelu_hi, t + 1)
                tt(y_lo[:, t, :], y_act[:, t % 2, :], y_hi[:, t, :].bitcast(F32), ALU.subtract).then_inc(gelu_lo, 1)

            DT, ARE, AIM, RE, TH, ER, ANG, CANG, SIN, COS, T0, T1, T2, T3, QR, QI = (
                1, 2, 3, 4, 5, 6, 7, 8, 9, 10, 11, 12, 13, 14, 15, 16)

            def r(i):
                return prm[:, i, :]

            for free in (u_copied, u_stored[0], u_stored[1], q_copied, k_act, v_copied, gated, merge_step,
                         o_copied, silu, f_made, down_added):
                dve.sem_inc(free, START)
            dve.wait_ge(par_tr, 1)
            dve.wait_ge(par_act, 1)
            nc.vector.tensor_copy(prm[:, ARE:AIM + 1, :], ps[:, 0, 0:2 * HG].rearrange("p (a g) -> p a g", a=2))
            link(ts(pen[:, :], ps[:, 3, 0:P], -BIG, BIG, ALU.mult, ALU.add))
            tt(r(RE), r(ARE), r(DT), ALU.mult).then_inc(par_dve, 1)
            link(tt(r(TH), r(AIM), r(DT), ALU.mult))
            link(ts(r(T0), r(TH), 1.0 / TWO_PI, ROUND, ALU.mult, ALU.add))
            link(ts(r(T1), r(T0), ROUND, None, ALU.subtract))
            link(stt(r(T2), r(T1), -PI_A, r(TH), ALU.mult, ALU.add))
            link(stt(r(T3), r(T1), -PI_B, r(T2), ALU.mult, ALU.add))
            link(stt(r(T2), r(T1), -PI_C, r(T3), ALU.mult, ALU.add))
            link(ts(r(ANG), r(T2), 3.1415925, -3.1415925, ALU.min, ALU.max))
            link(ts(r(T3), r(ANG), -1.0, None, ALU.mult))
            link(tt(r(T3), r(T3), r(ANG), ALU.max))
            ts(r(CANG), r(T3), -1.0, math.pi / 2, ALU.mult, ALU.add).then_inc(par_dve, 1)
            link(tt(r(T0), r(ARE), r(ARE), ALU.mult))
            link(tt(r(T1), r(AIM), r(AIM), ALU.mult))
            link(tt(r(T0), r(T0), r(T1), ALU.add))
            link(nc.vector.reciprocal(r(T1), r(T0)))
            dve.wait_ge(par_act, 4)
            link(nc.vector.memset(lam[:, 0, 0, :], 1.0))
            link(nc.vector.memset(lam[:, 0, 1, :], 0.0))
            link(tt(lam[:, 1, 0, :], r(ER), r(COS), ALU.mult))
            link(tt(lam[:, 1, 1, :], r(ER), r(SIN), ALU.mult))
            link(ts(r(T0), lam[:, 1, 0, :], -1.0, None, ALU.add))
            link(tt(r(T2), r(T0), r(ARE), ALU.mult))
            link(tt(r(T3), lam[:, 1, 1, :], r(AIM), ALU.mult))
            link(tt(r(T2), r(T2), r(T3), ALU.add))
            link(tt(r(QR), r(T2), r(T1), ALU.mult))
            link(tt(r(T2), lam[:, 1, 1, :], r(ARE), ALU.mult))
            link(tt(r(T3), r(T0), r(AIM), ALU.mult))
            link(tt(r(T2), r(T2), r(T3), ALU.subtract))
            tt(r(QI), r(T2), r(T1), ALU.mult).then_inc(par_dve, 1)
            dve.wait_ge(par_tr, 2)
            nc.vector.tensor_copy(gain_t[:, :, :].rearrange("p a k -> p (a k)"), ps[:, 4, 0:2 * KT])
            nc.vector.tensor_copy(c_t[:, 0, :, :].rearrange("p g c -> p (g c)"), ps[:, 1, :])
            ts(c_t[:, 1, :, :].rearrange("p g c -> p (g c)"), ps[:, 2, :], -1.0, None, ALU.mult).then_inc(par_banks, 1)

            dve_rstd(0, 0)
            for c in range(CLS):
                ts(x_tok[:, c, :], x_tok[:, c, :], stat[:, 2, c:c + 1], None, ALU.mult).then_inc(scaled, 1)
            split_lo(dve, 0, 0)
            dve_turn(0)
            dve.wait_ge(const, 1)
            dve.wait_ge(skip_in, 16 * OG)
            link(nc.vector.tensor_reduce(e16[:, :], ident[:, :].rearrange("p (j o) -> p o j", j=4)[:, 0:CH, :],
                                         AX, ALU.add))
            tt(d_blk[:, :, :],
               e16[:, :].unsqueeze(1).broadcast_to([P, 2 * OCT, CH]),
               d_pad[:, :].unsqueeze(2).broadcast_to([P, 2 * OCT, CH]), ALU.mult)
            nc.vector.memset(ps[:, 4:6, 0:256], 0.0).then_inc(k_bank, 1)
            with dve.Fori(0, 2) as it:
                for k in range(1, 9):
                    split_lo(dve, B_U + k, 2 * it)
            dve_tables(0)
            with dve.Fori(0, GROUPS) as g:
                dve_qkv(0, g)
            dve_tables(1)
            dve.wait_ge(h_stored, 16 * OCT)
            dve.wait_ge(g_stored, 16 * OCT)
            dve_attention(0)

            def dve_chunk_inputs(b):
                dve.wait_ge(s_made, b + 1)
                nc.vector.tensor_copy(s_t[:, OG * b:OG * b + OG, :, :].rearrange("p e r n -> p (e r n)"),
                                      ps[:, 6 + b % 2, :]).then_inc(s_copied, 1)

            dve_qkv(1, 0, lambda k: dve_chunk_inputs(k - 3) if 3 <= k < 3 + OCT else None)
            with dve.Fori(1, GROUPS) as g:
                dve_qkv(1, g)
            dve_attention(1)
            def dve_outputs(b):
                dve.wait_ge(y_made, b + 1)
                for gh in range(2):
                    g = group(b, gh, 0)
                    ins = nc.vector.tensor_copy(u_all[:, g:g + OG, :].rearrange("p e n -> p (e n)"),
                                                ps[:, 4 + 2 * (b % 2) + gh, 0:OG * NCH])
                ins.then_inc(y_copied, 1)

            for k in range(1, 9):
                split_lo(dve, B_G0 + k, 0)
                if k >= 4:
                    dve_outputs(k - 4)
            for b in range(5, OCT):
                dve_outputs(b)
            for k in range(1, 9):
                split_lo(dve, B_AU + k, 0)
                dve_gelu_lo(k - 1)

            def merge(it):
                m2 = mrg[:, bass.ds(2 * it, 2), :].rearrange("p a n -> p (a n)")
                dve.wait_ge(gated, START + 3 * it + 3)
                tt(sig_g[:, :], pair(2), sig_g[:, :], ALU.mult).then_inc(merge_step, 1)
                dve.wait_ge(merge_step, START + 4 * it + 2)
                tt(sig_g[:, :], sig_g[:, :], sig_s[:, :], ALU.mult).then_inc(merge_step, 1)
                dve.wait_ge(merge_step, START + 4 * it + 3)
                tt(m2, m2, sig_g[:, :], ALU.add).then_inc(merge_step, 1)

            def merge_attention(it):
                m2 = mrg[:, bass.ds(2 * it, 2), :].rearrange("p a n -> p (a n)")
                dve.wait_ge(gated, START + 3 * it + 2)
                tt(m2, m2, sig_a[:, :], ALU.mult).then_inc(merge_step, 1)

            for k in range(1, 5):
                split_lo(dve, B_Y0 + k, 0)
            dve.wait_ge(au_copied, 1)
            merge_attention(0)
            merge(0)
            with dve.Fori(1, 8) as it:
                for k in range(1, 13):
                    split_lo(dve, B_MRG - 12 + k, 3 * it)
                    if k == 8:
                        merge_attention(it)
                merge(it)
            for q in range(4):
                dve.wait_ge(mrg_hi, q + 1)
                tt(a_lo[:, 4 * q:4 * q + 4, :], mrg[:, 4 * q:4 * q + 4, :], a_hi[:, 4 * q:4 * q + 4, :].bitcast(F32),
                   ALU.subtract).then_inc(mrg_lo, 1)
            with dve.Fori(0, 2) as it:
                for k in range(1, 17):
                    split_lo(dve, B_WO + k, 4 * it)
                    if k in (9, 16):
                        b = (k - 1) // 8 - (k == 9)
                        dve.wait_ge(mix_sq, 2 * it + b + 1)
                        if k == 9:
                            dve.wait_ge(gb_in[0], 16)
                        cols = bass.ds(1024 * it + 512 * b, 512)
                        tt(o_t[:, :, cols], ps[:, 4 * b:4 * b + 4, :],
                           gain_b[:, cols].unsqueeze(1).broadcast_to([P, CLS, 512]), ALU.mult).then_inc(o_copied, 1)
            dve_rstd(1)
            dve.wait_ge(o_copied, START + 4)
            dve.wait_ge(x_again, 16)
            for c in range(CLS):
                stt(x2[:, c, :], o_t[:, c, :], stat[:, 2, c:c + 1], x2[:, c, :], ALU.mult, ALU.add
                    ).then_inc(x2_ready, 1)
            dve_rstd(2, 1)
            dve.wait_ge(x2_ready, CLS)
            for c in range(CLS):
                ts(o_t[:, c, :], x2[:, c, :], stat[:, 2, c:c + 1], None, ALU.mult).then_inc(scaled, 1)
            dve_turn(1)

            def ffn(g, last):
                if last:
                    dve.wait_ge(gb_in[1], 16)
                for k in range(1, 25):
                    if not (last and k == 24):
                        split_lo(dve, B_FF + k, 6 * g)
                    if k in (8, 16):
                        a = k // 8 - 1
                        dve.wait_ge(piece_done, B_FF + k + 24 * g)
                        dve.wait_ge(silu, START + 2 * g + a + 1)
                        tt(f_t[:, :], pair(1), f_sg[:, :], ALU.mult).then_inc(f_made, 1)
                        dve.wait_ge(f_hi_ready, 2 * g + a + 1)
                        tt(f_lo[:, 2 * a:2 * a + 2, :].rearrange("p a n -> p (a n)"), f_t[:, :],
                           f_hi[:, 2 * a:2 * a + 2, :].rearrange("p a n -> p (a n)").bitcast(F32), ALU.subtract
                           ).then_inc(f_lo_ready, 1)
                    if k >= 18 and k % 2 == 0:
                        d = (k - 18) // 2
                        if d == 0:
                            dve.wait_ge(acc_zero, 1)
                        for c in range(CLS):
                            if c < CLS - 1:
                                dve.wait_ge(down, 12 * g + 3 * d + c + 1)
                            else:
                                dve.wait_ge(piece_done, B_FF + k + 24 * g)
                            o = o_t[:, c, 512 * d:512 * d + 512]
                            tt(o, o, ps[:, 4 + c, :], ALU.add).then_inc(down_added, 1)
                            if last:
                                dve.wait_ge(down_added, START + 16 * g + 4 * d + c + 1)
                                cols = slice(512 * d, 512 * d + 512)
                                tt(o_gain[:, c, cols], o, gain_b[:, cols], ALU.mult).then_inc(o_gained, 1)

            with dve.Fori(0, FFG - 1) as g:
                ffn(g, False)
            ffn(FFG - 1, True)
            dve.wait_ge(ffn_sq, 4 * CLS)
            dve_rstd(3)
            dve.wait_ge(o_gained, 4 * CLS)
            for c in range(CLS):
                stt(x2[:, c, :], o_gain[:, c, :], stat[:, 2, c:c + 1], x2[:, c, :], ALU.mult, ALU.add
                    ).then_inc(out_ready, 1)

        @block.gpsimd
        def _(pool):
            steps = [0]

            def link(ins):
                steps[0] += 1
                ins.then_inc(pool_step, 1)
                pool.wait_ge(pool_step, steps[0])

            tt, ts = nc.gpsimd.tensor_tensor, nc.gpsimd.tensor_scalar
            nc.gpsimd.memset(zero[:, :], 0.0)
            nc.gpsimd.memset(d_pad[:, :], 0.0)
            nc.gpsimd.memset(hot[:, :], 1.0)
            link(nc.gpsimd.memset(ident[:, :], 0.0))
            nc.gpsimd.affine_select(out=hot[:, :].rearrange("p (a b) -> p a b", b=4),
                                    in_=hot[:, :].rearrange("p (a b) -> p a b", b=4), compare_op=ALU.is_equal,
                                    fill=0.0, base=0, pattern=[[0, P // 4], [1, 4]], channel_multiplier=-1)
            nc.gpsimd.affine_select(out=ident[:, :], in_=ident[:, :], compare_op=ALU.not_equal, fill=1.0, base=0,
                                    pattern=[[-1, P]], channel_multiplier=1).then_inc(const, 1)
            pool.wait_ge(par_dve, 3)
            pool.wait_ge(b_in, 256)
            q16 = [prm[:, i, :].unsqueeze(2).broadcast_to([P, HG, CH]) for i in (15, 16)]
            tmp = [ptmp[:, i, 0:HG * CH].rearrange("p (g c) -> p g c", c=CH) for i in range(2)]
            for ri, (s0, s1, op) in enumerate(((0, 1, ALU.subtract), (1, 0, ALU.add))):
                tt(tmp[0], q16[0], b_raw[:, s0, :, :], ALU.mult)
                link(tt(tmp[1], q16[1], b_raw[:, s1, :, :], ALU.mult))
                link(tt(b_bar[:, ri, :, :], tmp[0], tmp[1], op))

            def power(lo, n, src):
                shape = [P, n, HG]
                ar, ai = (lam[:, lo:lo + 1, j, :].broadcast_to(shape) for j in range(2))
                br, bi = (lam[:, 1:1 + n, j, :] for j in range(2))
                t0, t1 = (ptmp[:, j, 0:n * HG].rearrange("p (n g) -> p n g", g=HG) for j in range(2))
                for ri, (x, y, op) in enumerate(((br, bi, ALU.subtract), (bi, br, ALU.add))):
                    tt(t0, ar, x, ALU.mult)
                    link(tt(t1, ai, y, ALU.mult))
                    link(tt(lam[:, lo + 1:lo + 1 + n, ri, :], t0, t1, op))

            power(1, 1, 1)
            power(2, 2, 1)
            power(4, 4, 1)
            for s in range(L):
                nc.gpsimd.tensor_copy(lam_r[:, s, :, :], lam[:, L - 1 - s, :, :])
            for j in range(2):
                nc.gpsimd.tensor_copy(scan_a[:, 0, :, j], lam[:, L, 0, :])
            ts(scan_a[:, 1, :, 0], lam[:, L, 1, :], -1.0, None, ALU.mult)
            link(nc.gpsimd.tensor_copy(scan_a[:, 1, :, 1], lam[:, L, 1, :]))

            def tables(half):
                for q in range(4):
                    b = 4 * half + q
                    g0 = OG * b
                    if half and q == 0:
                        pool.wait_ge(k_made, 4)
                        pool.wait_ge(g_made, 4)
                        pool.wait_ge(h_stored, 16 * 4)
                    gs = slice(g0, g0 + OG)
                    for dst, pw, src, n, signs in ((bl, lam_r, b_bar, L, (ALU.subtract, ALU.add)),
                                                   (hc, lam, c_t, L + 1, (ALU.add, ALU.subtract))):
                        shape = [P, OG, n, CH]
                        lr, li = (pw[:, 0:n, j, gs].rearrange("p n e -> p e n").unsqueeze(3).broadcast_to(shape)
                                  for j in range(2))
                        xr, xi = (src[:, j, gs, :].unsqueeze(2).broadcast_to(shape) for j in range(2))
                        t0, t1 = (ptmp[:, j, 0:OG * n * CH].rearrange("p (e n c) -> p e n c", e=OG, c=CH)
                                  for j in range(2))
                        for ri, (x, y) in enumerate(((xr, xi), (xi, xr))):
                            tt(t0, lr, x, ALU.mult)
                            link(tt(t1, li, y, ALU.mult))
                            last = tt(dst[:, q, :, ri, :, :], t0, t1, signs[ri])
                            if dst is hc and ri:
                                last.then_inc(tab_ready, 1)
                                pool.wait_ge(tab_ready, b + 1)
                            else:
                                link(last)
                    pool.dma_start(h_d[b], hc[:, q, :, :, :, :].rearrange("p e r k o -> p (e r) (k o)")
                                   ).then_inc(h_stored, 16)
            pool.wait_ge(par_banks, 1)
            tables(0)
            tables(1)
            for h in range(2):
                pool.dma_start(k_d[512 * h:512 * h + 512, 0:(L - 1) * CH].rearrange("(a p) n -> p a n", p=P),
                               zero[:, :].rearrange("p (a n) -> p a n", a=4)).then_inc(zero_stored, 16)

            def biases(pr):
                for h in range(2):
                    if pr:
                        pool.wait_ge(biased, 8)
                    u7, u2 = bias[:, h, 0:7, :], bias[:, h, 7:9, :]
                    nc.gpsimd.iota(u7, pattern=[[-1, 7], [-CLS, P]], base=3, channel_multiplier=CLS,
                                   allow_small_or_imprecise_dtypes=True)
                    link(nc.gpsimd.iota(u2, pattern=[[0, 2], [-CLS, P]], base=0, channel_multiplier=CLS,
                                        allow_small_or_imprecise_dtypes=True))
                    nc.gpsimd.affine_select(out=u2, in_=u2, compare_op=ALU.is_ge, fill=BIG, base=0,
                                            pattern=[[0, 2], [-CLS, P]], channel_multiplier=CLS)
                    link(nc.gpsimd.affine_select(out=u7, in_=u7, compare_op=ALU.is_ge, fill=BIG, base=3,
                                                 pattern=[[-1, 7], [-CLS, P]], channel_multiplier=CLS))
                    link(nc.gpsimd.affine_select(out=u7, in_=u7, compare_op=ALU.is_ge, fill=BIG, base=WINDOW0 - 3,
                                                 pattern=[[1, 7], [CLS, P]], channel_multiplier=-CLS))
                    link(tt(bias[:, h, 8, :], bias[:, h, 8, :], pen[:, :], ALU.add))
                    ts(u7, u7, -slope(2 * pr + h) / SCALE, None, ALU.mult)
                    ts(bias[:, h, 7, :], bias[:, h, 7, :], -slope(HEADS + 2 * pr + h) / SCALE, None, ALU.mult)
                    ts(bias[:, h, 8, :], bias[:, h, 8, :], -slope(2 * HEADS + 2 * pr + h) / SCALE, None, ALU.mult
                       ).then_inc(bias_ready, 1)

            biases(0)
            pool.wait_ge(u_stored[0], START + 64)
            pool.wait_ge(u_stored[1], START + 64)
            pool.wait_ge(g_stored, 16 * OCT)
            pool.wait_ge(k_stored, 16 * 2 * OG)
            pool.wait_ge(zero_stored, 32)
            pool.wait_ge(h_stored, 16 * OCT)
            for s in range(L):
                pool.dma_start(u_all[CH * s:CH * s + CH, :, :], u_d[s].rearrange("(g i) n -> i g n", i=CH)
                               ).then_inc(u_in, 16)
            pool.wait_ge(heads_lo, 8)
            for b in range(OCT):
                s = b % 2
                if b >= 2:
                    pool.wait_ge(s_made, b - 1)
                pool.dma_start(g_r[:, s, :, :, :].rearrange("p e r n -> p (e r n)"), g_d[b]).then_inc(g_in[s], 16)
            biases(1)
            pool.wait_ge(s_copied, OCT)
            with pool.Fori(0, NCH - 1) as n:
                prev = s_t[:, :, :, bass.ds(n, 1)].rearrange("p g r n -> p g (r n)")
                tt(scan_t[:, 0, :, :], prev, scan_a[:, 0, :, :], ALU.mult)
                for r in range(2):
                    other = s_t[:, :, 1 - r, bass.ds(n, 1)].rearrange("p g n -> p (g n)")
                    last = tt(scan_t[:, 1, :, r], other, scan_a[:, 1, :, r], ALU.mult)
                last.then_inc(scan_step, 1)
                pool.wait_ge(scan_step, 3 * n + 1)
                tt(scan_t[:, 0, :, :], scan_t[:, 0, :, :], scan_t[:, 1, :, :], ALU.add).then_inc(scan_step, 1)
                pool.wait_ge(scan_step, 3 * n + 2)
                cur = s_t[:, :, :, bass.ds(n + 1, 1)].rearrange("p g r n -> p g (r n)")
                tt(cur, cur, scan_t[:, 0, :, :], ALU.add).then_inc(scan_step, 1)
                pool.wait_ge(scan_step, 3 * n + 3)

            def lag_tables(q):
                for s in range(L):
                    src = bass.AP(tensor=k_d.tensor, offset=16 * q * CH * KPAD + (L - 1 - s) * CH,
                                  ap=[[KPAD, CH], [CH * KPAD, 16], [1, P]])
                    pool.dma_start(t_q[q][CH * s:CH * s + CH, :, :], src).then_inc(t_in[q], 16)

            def state_tables(b):
                pool.dma_start(h_r[b % 4][:, :, :, :].rearrange("p e r n -> p (e r) n"), h_d[b, :, :, CH:]
                               ).then_inc(h_in[b % 4], 16)

            pool.wait_ge(heads_lo, 16)
            for q in range(4):
                state_tables(q)
                lag_tables(q)
            for b in range(4, OCT):
                pool.wait_ge(y_made, b - 3)
                state_tables(b)
            for h in range(2):
                pool.wait_ge(y_copied, OCT // 2 * (h + 1))
                gs = slice(HG * h, HG * h + HG)
                for s in range(L):
                    pool.dma_start(y_d[s].rearrange("(g o) n -> o g n", o=CH)[:, gs], u_all[CH * s:CH * s + CH, gs, :]
                                   ).then_inc(y_stored[h], 16)
                pool.wait_ge(y_stored[h], 16 * L)
                for t in range(4 * h, 4 * h + 4):
                    if h:
                        pool.wait_ge(gelu, t - 3)
                    pool.dma_start(y_in[:, t % 4, :].rearrange("p (s n) -> p s n", s=L),
                                   y_d[:, t * P:t * P + P, :].rearrange("s p n -> p s n")
                                   ).then_inc(y_back[t % 4], 16)
            pool.wait_ge(mrg_lo, 4)
            pool.dma_start(gain_b[:, :], A["norm_mix_post"][0:1, :].partition_broadcast(P)).then_inc(gb_in[0], 16)
            pool.dma_start(x2[:, :, :], A["x"][0].rearrange("(j c) d -> j c d", c=CLS)).then_inc(x_again, 16)
            pool.wait_ge(o_copied, START + 4)
            pool.dma_start(gain_b[:, :], A["norm_ffn_post"][0:1, :].partition_broadcast(P)).then_inc(gb_in[1], 16)
            pool.wait_ge(turned, 2 * KT)
            nc.gpsimd.memset(o_t[:, :, :].rearrange("p c d -> p (c d)"), 0.0).then_inc(acc_zero, 1)


_INS = ["x", "norm_mix_pre", "w_in", "w_attn_up", "ssm_a_re", "ssm_a_im", "ssm_log_dt", "ssm_b_re", "ssm_b_im",
        "ssm_c_re", "ssm_c_im", "ssm_d", "w_glu_v", "w_glu_g", "w_out", "norm_mix_post", "norm_ffn_pre",
        "w_ffn_gate", "w_ffn_up", "w_ffn_down", "norm_ffn_post"]


def kernel(**inputs):
    import numpy as _np
    import concourse.bacc as _bacc
    from concourse import mybir as _mybir
    from concourse.bass_utils import run_bass_kernel_spmd as _run

    nc = _bacc.Bacc("TRN2", target_bir_lowering=False, num_devices=1)
    arrays, aps = {}, {}
    for name in _INS:
        a = _np.ascontiguousarray(inputs[name])
        arrays[f"in_{name}"] = a
        aps[name] = nc.dram_tensor(f"in_{name}", a.shape, _mybir.dt.from_np(a.dtype), kind="ExternalInput").ap()
    out = nc.dram_tensor("out_0", (1, SEQ, D), _mybir.dt.float32, kind="ExternalOutput").ap()
    build(nc, aps, out)
    r = _run(nc, [arrays], core_ids=[0])
    return r.results[0]["out_0"]
```

```python
from contextlib import ExitStack
import math

import concourse.bass as bass
from concourse import mybir

F32 = mybir.dt.float32
F32R = mybir.dt.float32r
ALU = mybir.AluOpType
ACT = mybir.ActivationFunctionType
AX = mybir.AxisListType.X

P = 128
SEQ = 512
D = 2048
CLS = SEQ // P
KT = D // P
EPS = 1e-6
HEADS = 4
GROUPS = 3
HQ = HEADS * GROUPS * P
SCALE = float(P) ** -0.5
WINDOW0 = 128
BIG = 1e30
SSM = 1024
CH = 16
HG = SSM // CH // 2
NST = 64
L = 8
NCH = SEQ // L
OCT = 8
OG = HG // OCT
KPAD = (2 * L - 1) * CH
FF = 5632
FFG = FF // SEQ
U_COL = 3 * HQ
GA_COL = U_COL + SSM
GS_COL = GA_COL + D
TWO_PI = 2 * math.pi
PI_A = 6.28125
PI_B = 0.0019340515136718750
PI_C = TWO_PI - PI_A - PI_B
ROUND = 12582912.0

N_QKV = GROUPS * 12
B_U = 0
B_QKV = (16, 16 + N_QKV)
B_G0 = B_QKV[1] + N_QKV
B_AU = B_G0 + 8
B_Y0 = B_AU + 8
B_MRG = B_Y0 + 4
B_WO = B_MRG + 7 * 12
B_FF = B_WO + 32

START = 2

GELU_AT = ((), (0,), (1, 2), (3,), (4,), (5,), (6, 7), ())
MRG_RUNS = ((0, 4), (4, 8), (8, 12), (12, 14), (14, 16))


def group(b, gh, e):
    return 16 * (b // 2) + 8 * gh + OG * (b % 2) + e


def slope(head):
    return 2.0 ** (-8.0 * (head + 1) / (HEADS * GROUPS))


def build(nc, A, out):
    ctx = ExitStack()
    with ctx:
        def sem(name):
            return ctx.enter_context(nc.semaphore(name))

        base = 16512

        def at_kb(name, kb, shape, dt=F32):
            return nc.alloc_sbuf_tensor_at(name, shape, dt, offset=base + int(kb * 1024))

        a_hi = at_kb("a_hi", 0, [P, KT, SEQ], F32R)
        a_lo = at_kb("a_lo", 32, [P, KT, SEQ], F32R)
        raw = at_kb("raw", 64, [P, 4, 1024])
        w_hi = at_kb("w_hi", 80, [P, 2, 1024], F32R)
        w_lo = at_kb("w_lo", 88, [P, 2, 1024], F32R)
        ident = at_kb("ident", 96, [P, P])
        pen = at_kb("pen", 96.5, [P, P])
        scan_a = at_kb("scan_a", 97, [P, 2, HG, 2])
        scan_t = at_kb("scan_t", 97.5, [P, 2, HG, 2])
        hot = at_kb("hot", 98, [4, P])
        gain_t = at_kb("gain_t", 98.5, [P, 2, KT])
        stat = at_kb("stat", 98.75, [P, 3, CLS])
        smx = at_kb("smx", 98.875, [P, 3, 5])
        gain_rows = at_kb("gain_rows", 99, [2 * KT, P])
        sq_part = at_kb("sq_part", 99, [P, 4, CLS])
        x_tok = at_kb("x_tok", 100, [P, CLS, D])
        x_sq = at_kb("x_sq", 132, [P, D])
        u_st = at_kb("u_st", 100, [P, 2, 2, SEQ])
        q_t = at_kb("q_t", 99, [P, GROUPS, 2, SEQ])
        k_t = at_kb("k_t", 111, [P, GROUPS, 2, SEQ])
        v_t = at_kb("v_t", 123, [P, GROUPS, CLS, 2 * P])
        bias = at_kb("bias", 135, [P, 2, 9, P])
        at_hi = at_kb("at_hi", 144, [P, HEADS, SEQ], F32R)
        at_lo = at_kb("at_lo", 152, [P, HEADS, SEQ], F32R)
        s_t = at_kb("s_t", 160, [P, HG, 2, NCH])
        sc = at_kb("sc", 176, [P, 3, 768])
        p_t = at_kb("p_t", 185, [P, 2, 768])
        a_raw = at_kb("a_raw", 140, [HG, 2, 2 * NST])
        b_raw = at_kb("b_raw", 141, [P, 2, HG, CH])
        bl = at_kb("bl", 145, [P, 4, OG, 2, L, CH])
        hc = at_kb("hc", 161, [P, 4, OG, 2, L + 1, CH])
        g_st = at_kb("g_st", 179, [P, OG, 2, P])
        c_raw = at_kb("c_raw", 179, [P, 2, 4, 2, NST])
        b_bar = at_kb("b_bar", 183, [P, 2, HG, CH])
        c_t = at_kb("c_t", 187, [P, 2, HG, CH])
        lam = at_kb("lam", 191, [P, L + 1, 2, HG])
        lam_r = at_kb("lam_r", 193.25, [P, L, 2, HG])
        k_st = at_kb("k_st", 195.5, [P, 2, 2, 2, P])
        prm = at_kb("prm", 195.5, [P, 24, HG])
        ptmp = at_kb("ptmp", 199.5, [P, 2, OG * (L + 1) * CH])
        d_blk = at_kb("d_blk", 204, [P, 2 * OCT, CH])
        e16 = at_kb("e16", 205, [P, CH])
        d_pad = at_kb("d_pad", 205.125, [P, 2 * OCT])
        zero = at_kb("zero", 205.25, [P, 4 * (L - 1) * CH])
        g_r = at_kb("g_r", 177, [P, 2, OG, 2, P])
        u_all = at_kb("u_all", 191.75, [P, 2 * HG, NCH])
        t_q = [at_kb(f"t_q{q}", kb, [P, 16, P]) for q, kb in enumerate((177, 116, 100, 108))]
        h_r = [at_kb(f"h_r{s}", kb, [P, OG, 2, P]) for s, kb in enumerate((185, 140, 124, 128))]
        mrg = at_kb("mrg", 100, [P, KT, SEQ])
        sig_a = at_kb("sig_a", 132, [P, 1024])
        sig_s = at_kb("sig_s", 136, [P, 1024])
        sig_g = at_kb("sig_g", 140, [P, 1024])
        y_hi = at_kb("y_hi", 161, [P, SSM // P, SEQ], F32R)
        y_lo = at_kb("y_lo", 191.75, [P, SSM // P, SEQ], F32R)
        y_in = at_kb("y_in", 177, [P, 4, SEQ])
        y_act = at_kb("y_act", 185, [P, 2, SEQ])
        o_t = at_kb("o_t", 132, [P, CLS, D])
        x2 = at_kb("x2", 164, [P, CLS, D])
        gain_b = at_kb("gain_b", 196, [P, D])
        f_hi = at_kb("f_hi", 100, [P, 4, SEQ], F32R)
        f_lo = at_kb("f_lo", 108, [P, 4, SEQ], F32R)
        f_sg = at_kb("f_sg", 116, [P, 1024])
        f_t = at_kb("f_t", 120, [P, 1024])
        sq_t = at_kb("sq_t", 124, [P, D])
        o_gain = at_kb("o_gain", 0, [P, CLS, D])

        ps = ctx.enter_context(nc.psum_tensor("ps", [P, 8, 512], F32))

        def pair(p):
            return ps[:, 2 * p:2 * p + 2, :].rearrange("p b n -> p (b n)")

        u_d = nc.dram_tensor("u_d", [L, SSM, NCH], F32, kind="Internal").ap()
        y_d = nc.dram_tensor("y_d", [L, SSM, NCH], F32, kind="Internal").ap()
        g_d = nc.dram_tensor("g_d", [OCT, P, OG * 2 * P], F32, kind="Internal").ap()
        h_d = nc.dram_tensor("h_d", [OCT, P, OG * 2, (L + 1) * CH], F32, kind="Internal").ap()
        k_d = nc.dram_tensor("k_d", [SSM, KPAD], F32, kind="Internal").ap()

        landed = [sem(f"landed{s}") for s in range(4)]
        hi_ready = sem("hi_ready")
        lo_ready = sem("lo_ready")
        piece_done = sem("piece_done")
        x_in = [sem(f"x_in{c}") for c in range(CLS)]
        par_in = sem("par_in")
        c_in = sem("c_in")
        gain_in = sem("gain_in")
        b_in = sem("b_in")
        dp_in = sem("dp_in")
        skip_in = sem("skip_in")
        mix_sq = sem("mix_sq")
        ffn_sq = sem("ffn_sq")
        o_gained = sem("o_gained")
        const = sem("const")
        pool_step = sem("pool_step")
        dve_step = sem("dve_step")
        par_tr = sem("par_tr")
        par_banks = sem("par_banks")
        par_act = sem("par_act")
        par_dve = sem("par_dve")
        sq_done = sem("sq_done")
        rstd_in = sem("rstd_in")
        rstd_sqrt = sem("rstd_sqrt")
        scaled = sem("scaled")
        turned = sem("turned")
        turned_hi = sem("turned_hi")
        turned_lo = sem("turned_lo")
        u_copied = sem("u_copied")
        u_stored = [sem(f"u_stored{s}") for s in range(2)]
        tab_ready = sem("tab_ready")
        h_stored = sem("h_stored")
        zero_stored = sem("zero_stored")
        k_bank = sem("k_bank")
        k_made = sem("k_made")
        k_copied = sem("k_copied")
        k_stored = sem("k_stored")
        g_made = sem("g_made")
        g_copied = sem("g_copied")
        g_stored = sem("g_stored")
        q_copied = sem("q_copied")
        k_act = sem("k_act")
        v_copied = sem("v_copied")
        bias_ready = sem("bias_ready")
        scores = sem("scores")
        biased = sem("biased")
        negmax = sem("negmax")
        exped = sem("exped")
        normed = sem("normed")
        probs_t = sem("probs_t")
        probs_copied = sem("probs_copied")
        heads = sem("heads")
        heads_hi = sem("heads_hi")
        heads_lo = sem("heads_lo")
        g_in = [sem(f"g_in{s}") for s in range(2)]
        u_in = sem("u_in")
        s_made = sem("s_made")
        s_copied = sem("s_copied")
        scan_step = sem("scan_step")
        h_in = [sem(f"h_in{s}") for s in range(4)]
        t_in = [sem(f"t_in{q}") for q in range(4)]
        y_made = sem("y_made")
        y_copied = sem("y_copied")
        y_stored = [sem(f"y_stored{h}") for h in range(2)]
        y_back = [sem(f"y_back{s}") for s in range(4)]
        gelu = sem("gelu")
        gelu_hi = sem("gelu_hi")
        gelu_lo = sem("gelu_lo")
        au_copied = sem("au_copied")
        gated = sem("gated")
        merge_step = sem("merge_step")
        mrg_hi = sem("mrg_hi")
        mrg_lo = sem("mrg_lo")
        o_copied = sem("o_copied")
        x_again = sem("x_again")
        gb_in = [sem(f"gb_in{s}") for s in range(2)]
        x2_ready = sem("x2_ready")
        acc_zero = sem("acc_zero")
        silu = sem("silu")
        f_made = sem("f_made")
        f_hi_ready = sem("f_hi_ready")
        f_lo_ready = sem("f_lo_ready")
        down = sem("down")
        down_added = sem("down_added")
        out_ready = sem("out_ready")
        stored = sem("stored")

        def load(sp, m, quads, w, row_tiles, rows0, cols0, n):
            if not isinstance(rows0, int):
                rows0 = sp.snap(rows0)
            if not isinstance(cols0, int):
                cols0 = sp.snap(cols0)
            src = w_tiles(w, row_tiles, rows0, cols0, n)
            if m >= 4:
                sp.wait_ge(lo_ready, m - 3 + 4 * quads)
            sp.dma_start(raw[:, m % 4, :].rearrange("p (k n) -> p k n", n=src.shape[-1]), src
                         ).then_inc(landed[m % 4], 16)

        def split_hi(act, m, quads):
            act.wait_ge(landed[m % 4], 16 * (m // 4 + 1) + 16 * quads)
            if m >= 2:
                act.wait_ge(piece_done, m - 1 + 4 * quads)
            nc.scalar.activation(w_hi[:, m % 2, :], raw[:, m % 4, :], ACT.Copy).then_inc(hi_ready, 1)

        def split_lo(dve, m, quads):
            dve.wait_ge(hi_ready, m + 1 + 4 * quads)
            nc.vector.tensor_tensor(w_lo[:, m % 2, :], raw[:, m % 4, :], w_hi[:, m % 2, :].bitcast(F32),
                                    ALU.subtract).then_inc(lo_ready, 1)

        def piece_f(pe, m, quads, banks, x_hi, x_lo, kt0, first, last, halfway=None):
            pe.wait_ge(lo_ready, m + 1 + 4 * quads)
            wh = w_hi[:, m % 2, :].rearrange("p (k n) -> p k n", n=256)
            wl = w_lo[:, m % 2, :].rearrange("p (k n) -> p k n", n=256)
            for k in range(4):
                for f in range(2):
                    cols = slice(f * P, f * P + P)
                    o = ps[:, 2 * banks + f, :]
                    nc.tensor.matmul(o, wh[:, k, cols], x_hi[:, kt0 + k, :], start=first and k == 0, stop=False)
                    nc.tensor.matmul(o, wh[:, k, cols], x_lo[:, kt0 + k, :], start=False, stop=False)
                    mm = nc.tensor.matmul(o, wl[:, k, cols], x_hi[:, kt0 + k, :], start=False,
                                          stop=last and k == 3)
                if halfway and k == 1:
                    halfway()
            mm.then_inc(piece_done, 1)

        def piece_v(pe, m, quads, banks, kt0, first, last):
            pe.wait_ge(lo_ready, m + 1 + 4 * quads)
            wh = w_hi[:, m % 2, :].rearrange("p (k n) -> p k n", n=256)
            wl = w_lo[:, m % 2, :].rearrange("p (k n) -> p k n", n=256)
            for k in range(4):
                for c in range(CLS):
                    o = ps[:, 2 * banks + c // 2, 256 * (c % 2):256 * (c % 2) + 256]
                    toks = slice(c * P, c * P + P)
                    nc.tensor.matmul(o, a_hi[:, kt0 + k, toks], wh[:, k, :], start=first and k == 0 and c % 2 == 0,
                                     stop=False, skip_group_check=True)
                    nc.tensor.matmul(o, a_hi[:, kt0 + k, toks], wl[:, k, :], start=False, stop=False,
                                     skip_group_check=True)
                    mm = nc.tensor.matmul(o, a_lo[:, kt0 + k, toks], wh[:, k, :], start=False,
                                          stop=last and k == 3, skip_group_check=True)
            mm.then_inc(piece_done, 1)

        def piece_t(pe, m, quads, bank0, x_hi, x_lo, kt0, first, last, before=None, done=None):
            pe.wait_ge(lo_ready, m + 1 + 4 * quads)
            wh = w_hi[:, m % 2, :].rearrange("p (k n) -> p k n", n=512)
            wl = w_lo[:, m % 2, :].rearrange("p (k n) -> p k n", n=512)
            for c in range(CLS):
                if before:
                    before(c)
                toks = slice(c * P, c * P + P)
                o = ps[:, bank0 + c, :]
                for k in range(2):
                    nc.tensor.matmul(o, x_hi[:, kt0 + k, toks], wh[:, k, :], start=first and k == 0, stop=False)
                    nc.tensor.matmul(o, x_hi[:, kt0 + k, toks], wl[:, k, :], start=False, stop=False)
                    mm = nc.tensor.matmul(o, x_lo[:, kt0 + k, toks], wh[:, k, :], start=False,
                                          stop=last and k == 1)
                if done is not None and c < CLS - 1:
                    mm.then_inc(done, 1)
            mm.then_inc(piece_done, 1)

        def w_tiles(w, row_tiles, rows0, cols0, n):
            return w[bass.ds(rows0, row_tiles * P), bass.ds(cols0, n)].rearrange("(k p) n -> p k n", p=P)

        w_in, w_up = A["w_in"][0], A["w_attn_up"][0]
        w_gv, w_gg, w_out = A["w_glu_v"][0], A["w_glu_g"][0], A["w_out"][0]
        w_fg, w_fu, w_fd = A["w_ffn_gate"][0], A["w_ffn_up"][0], A["w_ffn_down"][0]
        x_cls = A["x"][0].rearrange("(j c) d -> c j d", c=CLS)
        out_cls = out[0].rearrange("(j c) d -> c j d", c=CLS)

        def store_outputs(eng, h):
            gs = slice(HG * h, HG * h + HG)
            for s in range(L):
                eng.dma_start(y_d[s].rearrange("(g o) n -> o g n", o=CH)[:, gs], u_all[CH * s:CH * s + CH, gs, :]
                              ).then_inc(y_stored[h], 16)

        block = ctx.enter_context(nc.Block())

        @block.sync
        def _(sp):
            for gh in range(2):
                sp.dma_start(a_raw[:, 1, NST * gh:NST * gh + NST],
                             A["ssm_a_im"][0].rearrange("(q a e) p -> a q e p", q=4, a=2)[gh]).then_inc(par_in, 16)
            for c in range(CLS):
                sp.dma_start(x_tok[:, c, :], x_cls[c]).then_inc(x_in[c], 16)
            for i, name in enumerate(("norm_mix_pre", "norm_ffn_pre")):
                sp.dma_start(gain_rows[KT * i:KT * i + KT, :], A[name][0].rearrange("(k p) -> k p", p=P)
                              ).then_inc(gain_in, 16)
            for ri, name in enumerate(("ssm_c_re", "ssm_c_im")):
                sp.dma_start(c_raw[:, ri, :, :, :].rearrange("p k a n -> p (k a) n"),
                              A[name][0].rearrange("(k e) c p -> (e c) k p", e=8)).then_inc(c_in, 16)
            for k in range(16):
                load(sp, B_U + k, 0, w_in, 4, 4 * P * (k % 4), U_COL + 256 * (k // 4), 256)
            for pr in range(2):
                with sp.Fori(0, GROUPS) as g:
                    for k in range(12):
                        col = HQ * (k // 4) + 256 * pr
                        load(sp, B_QKV[pr] + k, 3 * g, w_in, 4, 4 * P * (k % 4), 512 * g + col, 256)
            for k in range(8):
                load(sp, B_G0 + k, 0, w_in, 4, 4 * P * (k % 4), (GA_COL, GS_COL)[k // 4], 256)
            for k in range(8):
                load(sp, B_AU + k, 0, w_up, 4, 0, 256 * k, 256)
                if k == 5:
                    sp.wait_ge(y_copied, OCT)
                    store_outputs(sp, 1)
            for k in range(4):
                load(sp, B_Y0 + k, 0, (w_gv, w_gg)[k // 2], 4, 4 * P * (k % 2), 0, 256)
            with sp.Fori(2, 9) as it:
                for k in range(12):
                    if k < 8:
                        src = (w_in, 4, 4 * P * (k % 4), 256 * it + (GA_COL, GS_COL)[k // 4] - 256, 256)
                    else:
                        src = ((w_gv, w_gg)[k // 2 - 4], 4, 4 * P * (k % 2), 256 * it - 256, 256)
                    load(sp, B_MRG + k - 24, 3 * it, *src)
            with sp.Fori(0, 2) as it:
                for k in range(16):
                    load(sp, B_WO + k, 4 * it, w_out, 2, 2 * P * (k % 8), 1024 * it + 512 * (k // 8), 512)
            with sp.Fori(0, FFG) as g:
                for k in range(24):
                    if k < 16:
                        src = ((w_fg, w_fu)[k // 4 % 2], 4, 4 * P * (k % 4), 512 * g + 256 * (k // 8), 256)
                    else:
                        src = (w_fd, 2, 512 * g + 2 * P * (k % 2), 512 * ((k - 16) // 2), 512)
                    load(sp, B_FF + k, 6 * g, *src)
            for c in range(CLS):
                for h in range(2):
                    cols = slice(D // 2 * h, D // 2 * (h + 1))
                    sp.wait_ge(out_ready, 2 * c + h + 1)
                    sp.dma_start(out_cls[c][:, cols], x2[:, c, cols]).then_inc(stored, 16)
            sp.wait_ge(stored, 2 * 16 * CLS)

        def pe_turn(pe, src, first):
            for kt in range(KT):
                n = KT * first + kt
                if kt >= 8:
                    pe.wait_ge(turned_lo, n - 7)
                for c in range(CLS):
                    if kt == 0:
                        pe.wait_ge(scaled, CLS * first + c + 1)
                    mm = nc.tensor.transpose(ps[:, kt % 8, c * P:c * P + P], src[:, c, kt * P:kt * P + P], ident[:, :])
                mm.then_inc(turned, 1)

        def pe_turned(pe, k, turn):
            if k in (0, 2, 3):
                pe.wait_ge(turned_lo, KT * turn + {0: 10, 2: 12, 3: KT}[k])

        def pe_lags(pe, b):
            pe.wait_ge(tab_ready, b + 1)
            if b == 0:
                pe.wait_ge(k_bank, 1)
            else:
                pe.wait_ge(g_copied, b)
            for gh in range(2):
                ph = slice(NST * gh, NST * gh + NST)
                for e in range(OG):
                    for ri in range(2):
                        mm = nc.tensor.matmul(
                            ps[32 * e:32 * e + CH, 6 + gh, 0:P],
                            b_bar[ph, ri, OG * b + e, :],
                            hc[ph, b % 4, e, ri, 0:L, :].rearrange("p k o -> p (k o)"),
                            start=ri == 0, stop=ri == 1)
            mm.then_inc(k_made, 1)

        def pe_inputs_turned(pe, b):
            pe.wait_ge(k_copied, b + 1)
            for e in range(OG):
                for ri in range(2):
                    mm = nc.tensor.transpose(
                        pair(3)[:, (2 * e + ri) * P:(2 * e + ri) * P + P],
                        bl[:, b % 4, e, ri, :, :].rearrange("p s i -> p (s i)"), ident[:, :])
            mm.then_inc(g_made, 1)

        def pe_tables(pe, half, k):
            if 1 <= k <= 8:
                (pe_lags, pe_inputs_turned)[(k - 1) % 2](pe, 4 * half + (k - 1) // 2)

        def pe_qkv(pe, pr, g, between=None):
            for k in range(12):
                m, quads, kt0, first, last = B_QKV[pr] + k, 3 * g, 4 * (k % 4), k % 4 == 0, k % 4 == 3
                if k == 0:
                    pe.wait_ge(q_copied, START + 3 * pr + g)
                if k == 4:
                    pe.wait_ge(k_act, START + 3 * pr + g)
                if k == 8:
                    pe.wait_ge(v_copied, START + 3 * pr + g)
                if k < 8:
                    piece_f(pe, m, quads, k // 4, a_hi, a_lo, kt0, first, last)
                else:
                    piece_v(pe, m, quads, 2, kt0, first, last)
                if between:
                    between(k)

        def pe_scores(pe, pr, t):
            h, c, n = t // CLS, t % CLS, 8 * pr + t
            if t == 0:
                pe.wait_ge(q_copied, START + 3 * pr + 3)
                pe.wait_ge(k_act, START + 3 * pr + 3)
            if n >= 2:
                pe.wait_ge(biased, n - 1)
            qs = slice(c * P, c * P + P)
            s2 = pair(t % 2)
            nc.tensor.matmul(s2[:, 0:512], q_t[:, 0, h, qs], k_t[:, 0, h, :], start=True, stop=True)
            nc.tensor.matmul(s2[:, 512:640], q_t[:, 1, h, qs], k_t[:, 1, h, qs], start=True, stop=True)
            nc.tensor.matmul(s2[:, 640:768], q_t[:, 2, h, qs], k_t[:, 2, h, qs], start=True,
                             stop=True).then_inc(scores, 1)

        def pe_first_scores(pe, pr, k):
            if k in (9, 10):
                pe_scores(pe, pr, k - 9)

        def pe_attention(pe, pr):
            n0 = 8 * pr
            for t in range(2, 8 + 3):
                if t < 8:
                    pe_scores(pe, pr, t)
                if 2 <= t < 10:
                    n = n0 + t - 2
                    if t == 2:
                        pe.wait_ge(v_copied, START + 3 * pr + 3)
                    pe.wait_ge(normed, n + 1)
                    if n >= 1:
                        pe.wait_ge(probs_copied, n)
                    for k in range(6):
                        mm = nc.tensor.transpose(pair(2)[:, k * P:k * P + P], sc[:, (t - 2) % 3, k * P:k * P + P],
                                                 ident[:, :])
                    mm.then_inc(probs_t, 1)
                if t >= 3:
                    h, c, n = (t - 3) // CLS, (t - 3) % CLS, n0 + t - 3
                    pe.wait_ge(probs_copied, n + 1)
                    if n >= 2:
                        pe.wait_ge(heads_lo, n - 1)
                    es = slice(h * P, h * P + P)
                    for k in range(6):
                        v = v_t[:, 0, k, es] if k < CLS else v_t[:, k - 3, c, es]
                        mm = nc.tensor.matmul(ps[:, 6 + (t - 3) % 2, 0:P], v, p_t[:, (t - 3) % 2, k * P:k * P + P],
                                              start=k == 0, stop=k == 5)
                    mm.then_inc(heads, 1)

        def pe_chunk_inputs(pe, b):
            pe.wait_ge(g_in[b % 2], 16 * (b // 2 + 1))
            if b == 0:
                pe.wait_ge(u_in, 16 * L)
                pe.wait_ge(heads_lo, 8)
            if b >= 2:
                pe.wait_ge(s_copied, b - 1)
            for gh in range(2):
                for e in range(OG):
                    for ri in range(2):
                        col = (2 * e + ri) * NCH
                        mm = nc.tensor.matmul(
                            ps[NST * gh:NST * gh + NST, 6 + b % 2, col:col + NCH],
                            g_r[:, b % 2, e, ri, NST * gh:NST * gh + NST], u_all[:, group(b, gh, e), :],
                            start=True, stop=True)
            mm.then_inc(s_made, 1)

        def pe_outputs(pe, b, gh):
            if not 0 <= b < OCT:
                return
            if gh == 0:
                if b == 0:
                    pe.wait_ge(scan_step, 3 * (NCH - 1))
                    pe.wait_ge(heads_lo, 16)
                pe.wait_ge(h_in[b % 4], 16 * (b // 4 + 1))
                pe.wait_ge(t_in[b // 2], 16 * L)
                if b >= 2:
                    pe.wait_ge(y_copied, b - 1)
            ph = slice(NST * gh, NST * gh + NST)
            for e in range(OG):
                col, bank = e * NCH, 4 + 2 * (b % 2) + gh
                g = group(b, gh, e)
                nc.tensor.matmul(ps[:, bank, col:col + NCH], t_q[b // 2][:, g % 16, :], u_all[:, g, :],
                                 start=True, stop=True)
                for ri in range(2):
                    mm = nc.tensor.matmul(ps[:, bank, col + 1:col + NCH], h_r[b % 4][ph, e, ri, :],
                                          s_t[ph, OG * b + e, ri, 0:NCH - 1], start=False, stop=True,
                                          skip_group_check=True)
            if gh == 1:
                mm.then_inc(y_made, 1)

        @block.tensor
        def _(pe):
            pe.wait_ge(const, 1)
            pe.wait_ge(par_in, 64)
            for ri in range(2):
                nc.tensor.transpose(ps[:, 0, ri * HG:ri * HG + HG], a_raw[:, ri, :], ident[0:HG, 0:HG])
            nc.tensor.matmul(ps[:, 3, 0:P], hot[:, :], hot[:, :], start=True, stop=True).then_inc(par_tr, 1)
            pe.wait_ge(gain_in, 32)
            nc.tensor.transpose(ps[:, 4, 0:2 * KT], gain_rows[:, :], ident[0:2 * KT, 0:2 * KT]).then_inc(par_tr, 1)
            pe.wait_ge(c_in, 32)
            for ri in range(2):
                for k in range(4):
                    mm = nc.tensor.transpose(ps[:, 1 + ri, k * P:k * P + P],
                                             c_raw[:, ri, k, :, :].rearrange("p a b -> p (a b)"), ident[:, :])
            mm.then_inc(par_tr, 1)
            pe.wait_ge(par_banks, 1)
            pe_turn(pe, x_tok, 0)
            with pe.Fori(0, 2) as it:
                for k in range(8):
                    pe_turned(pe, k, 0)
                    if k % 4 == 0:
                        pe.wait_ge(u_copied, START - 1 + 2 * it + k // 4)
                    piece_f(pe, B_U + k, 2 * it, k // 4, a_hi, a_lo, 4 * (k % 4), k % 4 == 0, k % 4 == 3)
            pe.wait_ge(u_copied, START + 4)
            pe_qkv(pe, 0, 0, lambda k: pe_tables(pe, 0, k))
            pe_qkv(pe, 0, 1)
            pe_qkv(pe, 0, 2, lambda k: (pe_tables(pe, 1, k), pe_first_scores(pe, 0, k)))
            pe.wait_ge(k_copied, 8)
            pe.wait_ge(g_copied, 8)
            pe_attention(pe, 0)
            pe_qkv(pe, 1, 0, lambda k: pe_chunk_inputs(pe, k - 2) if 2 <= k < 2 + OCT else None)
            pe_qkv(pe, 1, 1)
            pe_qkv(pe, 1, 2, lambda k: pe_first_scores(pe, 1, k))
            pe.wait_ge(s_copied, OCT)
            pe_attention(pe, 1)
            pe.wait_ge(biased, 16)
            for k in range(8):
                piece_f(pe, B_G0 + k, 0, k // 4, a_hi, a_lo, 4 * (k % 4), k % 4 == 0, k % 4 == 3,
                        lambda: pe_outputs(pe, k - 2, 0))
                pe_outputs(pe, k - 2, 1)
            for k in range(8):
                if k < 2:
                    pe.wait_ge(gated, START + k + 1)
                if k == 2:
                    pe.wait_ge(y_copied, OCT)
                if k >= 4:
                    pe.wait_ge(au_copied, k - 3)
                piece_f(pe, B_AU + k, 0, k % 4, at_hi, at_lo, 0, True, True, lambda: pe_outputs(pe, k + 6, 0))
                pe_outputs(pe, k + 6, 1)
            pe.wait_ge(au_copied, 8)
            pe.wait_ge(gelu_lo, SSM // P)
            for k in range(4):
                piece_f(pe, B_Y0 + k, 0, k // 2 + 2, y_hi, y_lo, 4 * (k % 2), k % 2 == 0, k % 2 == 1)
            with pe.Fori(1, 8) as it:
                for k in range(12):
                    if k < 8:
                        if k % 4 == 0:
                            pe.wait_ge(gated, START - 2 + 3 * it + k // 4)
                        piece_f(pe, B_MRG + k - 12, 3 * it, k // 4, a_hi, a_lo, 4 * (k % 4), k % 4 == 0, k % 4 == 3)
                    else:
                        if k == 8:
                            pe.wait_ge(merge_step, START - 2 + 4 * it)
                        if k == 10:
                            pe.wait_ge(gated, START + 3 * it)
                        piece_f(pe, B_MRG + k - 12, 3 * it, k // 2 - 2, y_hi, y_lo, 4 * (k % 2), k % 2 == 0, k % 2 == 1)
            pe.wait_ge(gated, START + 23)
            with pe.Fori(0, 2) as it:
                for k in range(16):
                    if k in (0, 2, 4, 6, 7):
                        pe.wait_ge(mrg_lo, (k + 1) // 2 + 1)
                    if k == 8:
                        pe.wait_ge(merge_step, START + 32)
                    if k % 8 == 0:
                        pe.wait_ge(o_copied, START - 1 + 2 * it + k // 8)
                    piece_t(pe, B_WO + k, 4 * it, 4 * (k // 8), a_hi, a_lo, 2 * (k % 8), k % 8 == 0, k % 8 == 7)
            pe.wait_ge(o_copied, START + 4)
            pe_turn(pe, o_t, 1)
            with pe.Fori(0, FFG) as g:
                for k in range(24):
                    m = B_FF + k
                    pe_turned(pe, k, 1)
                    if k < 16:
                        if k % 8 == 0:
                            pe.wait_ge(silu, START + 2 * g + k // 8)
                        if k % 8 == 4:
                            pe.wait_ge(f_made, START + 2 * g + k // 8)
                        piece_f(pe, m, 6 * g, k // 4 % 2, a_hi, a_lo, 4 * (k % 4), k % 4 == 0, k % 4 == 3)
                    else:
                        d = (k - 16) // 2
                        if k < 18:
                            pe.wait_ge(f_lo_ready, 2 * g + k - 15)

                        def bank_free(c, d=d, k=k, g=g):
                            if k % 2 == 0:
                                if d == 0:
                                    if c == 0:
                                        pe.wait_ge(down_added, START + 16 * g)
                                else:
                                    pe.wait_ge(down_added, START + 16 * g + 4 * d + c - 3)

                        piece_t(pe, m, 6 * g, 4, f_hi, f_lo, 2 * (k % 2), k % 2 == 0, k % 2 == 1,
                                before=bank_free, done=down if k % 2 else None)

        def act_turn(act, first):
            for kt in range(KT):
                act.wait_ge(turned, KT * first + kt + 1)
                nc.scalar.activation(a_hi[:, kt, :], ps[:, kt % 8, :], ACT.Copy,
                                     scale=gain_t[:, first, kt:kt + 1]).then_inc(turned_hi, 1)

        def act_stats(act, src, scratch, waits, turn, between=None):
            for c in range(CLS):
                waits(c)
                if c:
                    act.wait_ge(sq_done, CLS * turn + c)
                nc.scalar.activation(scratch[:, :], src[:, c, :], ACT.Square,
                                     accum_out=stat[:, 0, c:c + 1]).then_inc(sq_done, 1)
                if between:
                    between(c)
            act_root(act, 2 * turn)

        def act_root(act, n):
            act.wait_ge(rstd_in, n + 1)
            nc.scalar.activation(stat[:, 1, :], stat[:, 1, :], ACT.Sqrt).then_inc(rstd_sqrt, 1)

        def act_tables(act, half, k):
            if k in (3, 5, 7, 9):
                b = 4 * half + (k - 3) // 2
                act.wait_ge(g_made, b + 1)
                if b >= 1:
                    act.wait_ge(g_stored, 16 * b)
                nc.scalar.activation(g_st[:, :, :, :].rearrange("p a b n -> p (a b n)"), pair(3),
                                     ACT.Copy).then_inc(g_copied, 1)
                act.wait_ge(g_copied, b + 1)
                act.dma_start(g_d[b], g_st[:, :, :, :].rearrange("p a b n -> p (a b n)")).then_inc(g_stored, 16)
            if k == 10:
                act.wait_ge(k_copied, 4 * half + 4)
                for e in range(OG):
                    dst = bass.AP(tensor=k_d.tensor, offset=(group(4 * half, 0, e) * CH) * KPAD + (L - 1) * CH,
                                  ap=[[KPAD, CH], [OG * CH * KPAD, 8], [1, P]])
                    act.dma_start(dst, k_st[32 * e:32 * e + CH, :, :, :, :].rearrange("p q a b n -> p (q a b) n")
                                  ).then_inc(k_stored, 16)

        def act_qkv(act, pr, g, after=None):
            for k in range(1, 13):
                split_hi(act, B_QKV[pr] + k, 3 * g)
                if k == 5:
                    nc.scalar.activation(q_t[:, bass.ds(g, 1), :, :].rearrange("p g h n -> p (g h n)"), pair(0),
                                         ACT.Copy).then_inc(q_copied, 1)
                if after:
                    after(k)
            act.wait_ge(piece_done, B_QKV[pr] + 12 + 12 * g)
            nc.scalar.activation(v_t[:, bass.ds(g, 1), :, :].rearrange("p g c n -> p (g c n)"), pair(2),
                                 ACT.Copy).then_inc(v_copied, 1)

        def act_exp(act, pr, t):
            act.wait_ge(negmax, 8 * pr + t + 1)
            nc.scalar.activation(sc[:, t % 3, :], sc[:, t % 3, :], ACT.Exp, bias=smx[:, t % 3, 2:3],
                                 scale=SCALE, accum_out=smx[:, t % 3, 3:4]).then_inc(exped, 1)

        def act_first_exps(act, pr, k):
            if k == 12:
                act_exp(act, pr, 0)
                act_exp(act, pr, 1)

        def act_attention(act, pr):
            n0 = 8 * pr
            for t in range(2, 8 + 4):
                if t < 8:
                    act_exp(act, pr, t)
                if 2 <= t < 10:
                    n = n0 + t - 2
                    act.wait_ge(probs_t, n + 1)
                    if n >= 2:
                        act.wait_ge(heads, n - 1)
                    nc.scalar.activation(p_t[:, t % 2, :], pair(2)[:, 0:768], ACT.Copy).then_inc(probs_copied, 1)
                if t >= 4:
                    h, c, n = (t - 4) // CLS, (t - 4) % CLS, n0 + t - 4
                    act.wait_ge(heads, n + 1)
                    nc.scalar.activation(at_hi[:, 2 * pr + h, c * P:c * P + P], ps[:, 6 + t % 2, 0:P], ACT.Copy
                                         ).then_inc(heads_hi, 1)

        @block.scalar
        def _(act):
            for gh in range(2):
                act.dma_start(a_raw[:, 0, NST * gh:NST * gh + NST],
                              A["ssm_a_re"][0].rearrange("(q a e) p -> a q e p", q=4, a=2)[gh]).then_inc(par_in, 16)
            for gh in range(2):
                act.dma_start(prm[NST * gh:NST * gh + NST, 0, :].rearrange("p (q e) -> p q e", q=4),
                              bass.AP(tensor=A["ssm_log_dt"].tensor, offset=8 * gh, ap=[[0, NST], [16, 4], [1, 8]])
                              ).then_inc(dp_in, 16)
            def between(c):
                if c == 0:
                    act.wait_ge(dp_in, 32)
                    nc.scalar.activation(prm[:, 1, :], prm[:, 0, :], ACT.Exp).then_inc(par_act, 1)
                if c == 1:
                    act.wait_ge(par_dve, 1)
                    nc.scalar.activation(prm[:, 6, :], prm[:, 4, :], ACT.Exp).then_inc(par_act, 1)
                if c == 2:
                    act.wait_ge(par_dve, 2)
                    nc.scalar.activation(prm[:, 9, :], prm[:, 7, :], ACT.Sin).then_inc(par_act, 1)
                    nc.scalar.activation(prm[:, 10, :], prm[:, 8, :], ACT.Sin).then_inc(par_act, 1)

            act_stats(act, x_tok, x_sq, lambda c: act.wait_ge(x_in[c], 16), 0, between)
            act.wait_ge(par_tr, 3)
            nc.scalar.activation(c_t[:, 0, :, :].rearrange("p g c -> p (g c)"), ps[:, 1, :], ACT.Copy)
            nc.scalar.activation(c_t[:, 1, :, :].rearrange("p g c -> p (g c)"), ps[:, 2, :], ACT.Copy, scale=-1.0
                                 ).then_inc(par_banks, 1)
            split_hi(act, 0, 0)
            act_turn(act, 0)

            with act.Fori(0, 2) as it:
                for k in range(1, 9):
                    split_hi(act, B_U + k, 2 * it)
                    if k % 4 == 0:
                        s = k // 4 - 1
                        act.wait_ge(piece_done, k + 8 * it)
                        act.wait_ge(u_stored[s], START + 32 * it)
                        for f in range(2):
                            mm = nc.scalar.activation(
                                u_st[:, s, f, :].rearrange("p (b c n) -> p b c n", b=2, c=CLS),
                                ps[:, 2 * s + f, :].rearrange("p (c n b) -> p b c n", b=2, c=CLS), ACT.Copy)
                        mm.then_inc(u_copied, 1)
                        act.wait_ge(u_copied, START + 2 * it + s + 1)
                        for f in range(2):
                            act.dma_start(u_d[:, bass.ds(512 * it + 256 * s + P * f, P), :].rearrange("s p n -> p s n"),
                                          u_st[:, s, f, :].rearrange("p (s n) -> p s n", s=L)
                                          ).then_inc(u_stored[s], 16)

            def u_is_stored(k):
                if k == 4:
                    act.wait_ge(u_stored[0], START + 64)
                    act.wait_ge(u_stored[1], START + 64)

            act_qkv(act, 0, 0, lambda k: (u_is_stored(k), act_tables(act, 0, k)))
            act_qkv(act, 0, 1)
            act_qkv(act, 0, 2, lambda k: (act_tables(act, 1, k), act_first_exps(act, 0, k)))
            act_attention(act, 0)
            with act.Fori(0, GROUPS - 1) as g:
                act_qkv(act, 1, g)
            act_qkv(act, 1, 2, lambda k: act_first_exps(act, 1, k))
            act_attention(act, 1)
            for k in range(1, 9):
                split_hi(act, B_G0 + k, 0)
                if k % 4 == 0:
                    act.wait_ge(piece_done, B_G0 + k)
                    nc.scalar.activation((sig_a, sig_s)[k // 4 - 1][:, :], pair(k // 4 - 1), ACT.Sigmoid
                                         ).then_inc(gated, 1)

            def act_gelu(t):
                if t == 0:
                    act.wait_ge(y_made, OCT)
                act.wait_ge(y_back[t % 4], 16 * (t // 4 + 1))
                if t >= 2:
                    act.wait_ge(gelu_lo, t - 1)
                nc.scalar.activation(y_act[:, t % 2, :].rearrange("p (c n b) -> p b c n", b=2, c=CLS),
                                     y_in[:, t % 4, :].rearrange("p (b c n) -> p b c n", b=2, c=CLS),
                                     ACT.Gelu_apprx_tanh).then_inc(gelu, 1)
                act.wait_ge(gelu, t + 1)
                nc.scalar.activation(y_hi[:, t, :], y_act[:, t % 2, :], ACT.Copy).then_inc(gelu_hi, 1)

            for k in range(1, 9):
                split_hi(act, B_AU + k, 0)
                act.wait_ge(piece_done, B_AU + k)
                nc.scalar.activation(mrg[:, 2 * k - 2:2 * k, :].rearrange("p a n -> p (a n)"), pair((k - 1) % 4),
                                     ACT.Copy).then_inc(au_copied, 1)
                for t in GELU_AT[k - 1]:
                    act_gelu(t)

            def gate_glu(it, k):
                j = k // 4 - 1
                if j == 0:
                    act.wait_ge(merge_step, START + 4 * it)
                act.wait_ge(piece_done, B_MRG - 12 + k + 12 * it)
                nc.scalar.activation((sig_a, sig_s, sig_g)[j][:, :], pair((0, 1, 3)[j]), ACT.Sigmoid
                                     ).then_inc(gated, 1)

            for k in range(1, 5):
                split_hi(act, B_Y0 + k, 0)
            gate_glu(0, 12)
            def mrg_split_hi(i):
                a, b = MRG_RUNS[i]
                nc.scalar.activation(a_hi[:, a:b, :], mrg[:, a:b, :], ACT.Copy).then_inc(mrg_hi, 1)

            with act.Fori(1, 7) as it:
                for k in range(1, 13):
                    split_hi(act, B_MRG - 12 + k, 3 * it)
                    if k % 4 == 0:
                        gate_glu(it, k)
            for k in range(1, 13):
                split_hi(act, B_MRG - 12 + k, 21)
                if k % 4 == 0:
                    gate_glu(7, k)
                if k == 9:
                    act.wait_ge(merge_step, START + 28)
                if k >= 9:
                    mrg_split_hi(k - 9)
            for k in range(1, 33):
                split_hi(act, B_WO + k, 0)
                if k == 4:
                    act.wait_ge(merge_step, START + 32)
                    mrg_split_hi(4)
                if k in (9, 17, 25, 32):
                    d = (k - 1) // 8 - (k < 32)
                    act.wait_ge(piece_done, B_WO + 8 * d + 8)
                    for c in range(CLS):
                        if d:
                            act.wait_ge(mix_sq, CLS * (d - 1) + c + 1)
                        nc.scalar.activation(sq_t[:, 512 * c:512 * c + 512], ps[:, 4 * (d % 2) + c, :], ACT.Square,
                                             accum_out=sq_part[:, d, c:c + 1]).then_inc(mix_sq, 1)
            act_root(act, 1)
            act_stats(act, x2, sq_t, lambda c: act.wait_ge(x2_ready, c + 1), 1)
            act_turn(act, 1)

            def ffn(g, last, squares=None):
                for k in range(1, 25):
                    if not (last and k == 24):
                        split_hi(act, B_FF + k, 6 * g)
                    if squares and k >= 20 and k % 2 == 0:
                        squares((k - 20) // 2)
                    if k in (4, 12):
                        act.wait_ge(piece_done, B_FF + k + 24 * g)
                        act.wait_ge(f_made, START + 2 * g + k // 8)
                        nc.scalar.activation(f_sg[:, :], pair(0), ACT.Silu).then_inc(silu, 1)
                    if k in (8, 16):
                        a = k // 8 - 1
                        act.wait_ge(f_made, START + 2 * g + a + 1)
                        nc.scalar.activation(f_hi[:, 2 * a:2 * a + 2, :].rearrange("p a n -> p (a n)"), f_t[:, :],
                                             ACT.Copy).then_inc(f_hi_ready, 1)
                if squares:
                    squares(3)

            with act.Fori(0, FFG - 1) as g:
                ffn(g, False)

            def last_squares(d):
                for c in range(CLS):
                    act.wait_ge(down_added, START + 16 * (FFG - 1) + 4 * d + c + 1)
                    if d:
                        act.wait_ge(ffn_sq, CLS * (d - 1) + c + 1)
                    nc.scalar.activation(sq_t[:, 512 * c:512 * c + 512], o_t[:, c, 512 * d:512 * d + 512], ACT.Square,
                                         accum_out=sq_part[:, d, c:c + 1]).then_inc(ffn_sq, 1)

            ffn(FFG - 1, True, last_squares)
            act_root(act, 3)

        chain = [0]

        @block.vector
        def _(dve):
            def link(ins):
                chain[0] += 1
                ins.then_inc(dve_step, 1)
                dve.wait_ge(dve_step, chain[0])

            tt, ts, stt = nc.vector.tensor_tensor, nc.vector.tensor_scalar, nc.vector.scalar_tensor_tensor

            def dve_turn(first):
                for kt in range(KT):
                    dve.wait_ge(turned_hi, KT * first + kt + 1)
                    stt(a_lo[:, kt, :], ps[:, kt % 8, :], gain_t[:, first, kt:kt + 1], a_hi[:, kt, :].bitcast(F32),
                        ALU.mult, ALU.subtract).then_inc(turned_lo, 1)

            def dve_rstd(n, turn=None, between=None):
                if turn is None:
                    link(nc.vector.tensor_reduce(stat[:, 0, :], sq_part[:, :, :].rearrange("p d c -> p c d"), AX,
                                                 ALU.add))
                else:
                    dve.wait_ge(sq_done, CLS * (turn + 1))
                ts(stat[:, 1, :], stat[:, 0, :], 1.0 / D, EPS, ALU.mult, ALU.add).then_inc(rstd_in, 1)
                if between:
                    between()
                dve.wait_ge(rstd_sqrt, n + 1)
                link(nc.vector.reciprocal(stat[:, 2, :], stat[:, 1, :]))

            def dve_tables(half, k):
                if k in (2, 4, 6, 8):
                    b = 4 * half + k // 2 - 1
                    dve.wait_ge(k_made, b + 1)
                    if b == 4:
                        dve.wait_ge(k_stored, 16 * OG)
                    st = k_st[:, b % 4 // 2, :, b % 2, :]
                    link(nc.vector.tensor_copy(st, ps[:, 6:8, 0:P]))
                    i = 4 * (b // 2) + b % 2
                    tt(st[:, :, 0:CH], st[:, :, 0:CH], d_blk[:, i:i + 3:2, :], ALU.add).then_inc(k_copied, 1)

            def dve_qkv(pr, g, between=None):
                for k in range(1, 13):
                    split_lo(dve, B_QKV[pr] + k, 3 * g)
                    if k == 9:
                        nc.vector.tensor_copy(k_t[:, bass.ds(g, 1), :, :].rearrange("p g h n -> p (g h n)"),
                                              pair(1)).then_inc(k_act, 1)
                    if between:
                        between(k)

            def dve_scores(pr, t):
                h, c, n = t // CLS, t % CLS, 8 * pr + t
                s = t % 3
                if n == 0:
                    dve.wait_ge(h_stored, 16 * OCT)
                    dve.wait_ge(g_stored, 16 * OCT)
                dve.wait_ge(scores, n + 1)
                if t % CLS == 0:
                    dve.wait_ge(bias_ready, 2 * pr + h + 1)
                if t >= 3 or pr:
                    dve.wait_ge(probs_t, n - 2 if t >= 3 else 8 * pr)
                link(nc.vector.tensor_tensor_reduce(
                    out=sc[:, s, 0:512], in0=pair(t % 2)[:, 0:512],
                    in1=bias[:, h, 3 - c:7 - c, :].rearrange("p a b -> p (a b)"), scale=1.0, scalar=-3e38,
                    op0=ALU.add, op1=ALU.max, accum_out=smx[:, s, 0:1]))
                nc.vector.tensor_tensor_reduce(
                    out=sc[:, s, 512:768], in0=pair(t % 2)[:, 512:768],
                    in1=bias[:, h, 7:9, :].rearrange("p a b -> p (a b)"), scale=1.0, scalar=smx[:, s, 0:1],
                    op0=ALU.add, op1=ALU.max, accum_out=smx[:, s, 1:2]).then_inc(biased, 1)
                dve.wait_ge(biased, n + 1)
                ts(smx[:, s, 2:3], smx[:, s, 1:2], -SCALE, None, ALU.mult).then_inc(negmax, 1)

            def dve_norm(pr, t):
                s = t % 3
                dve.wait_ge(exped, 8 * pr + t + 1)
                link(nc.vector.reciprocal(smx[:, s, 4:5], smx[:, s, 3:4]))
                ts(sc[:, s, :], sc[:, s, :], smx[:, s, 4:5], None, ALU.mult).then_inc(normed, 1)

            def dve_first_scores(pr, k):
                if k == 11:
                    dve_scores(pr, 0)
                if k == 12:
                    dve_scores(pr, 1)
                    dve_norm(pr, 0)

            def dve_attention(pr):
                n0 = 8 * pr
                for t in range(2, 8 + 4):
                    if t < 8:
                        dve_scores(pr, t)
                    if t < 9:
                        dve_norm(pr, t - 1)
                    if t >= 4:
                        h, c, n = (t - 4) // CLS, (t - 4) % CLS, n0 + t - 4
                        dve.wait_ge(heads_hi, n + 1)
                        qs = slice(c * P, c * P + P)
                        tt(at_lo[:, 2 * pr + h, qs], ps[:, 6 + t % 2, 0:P], at_hi[:, 2 * pr + h, qs].bitcast(F32),
                           ALU.subtract).then_inc(heads_lo, 1)

            def dve_gelu_lo(t):
                dve.wait_ge(gelu_hi, t + 1)
                tt(y_lo[:, t, :], y_act[:, t % 2, :], y_hi[:, t, :].bitcast(F32), ALU.subtract).then_inc(gelu_lo, 1)

            DT, ARE, AIM, RE, TH, ER, ANG, CANG, SIN, COS, T0, T1, T2, T3, QR, QI = (
                1, 2, 3, 4, 5, 6, 7, 8, 9, 10, 11, 12, 13, 14, 15, 16)

            def r(i):
                return prm[:, i, :]

            for free in (u_copied, u_stored[0], u_stored[1], q_copied, k_act, v_copied, gated, merge_step,
                         o_copied, silu, f_made, down_added):
                dve.sem_inc(free, START)
            dve.wait_ge(par_tr, 1)
            dve.wait_ge(par_act, 1)
            nc.vector.tensor_copy(prm[:, ARE:AIM + 1, :], ps[:, 0, 0:2 * HG].rearrange("p (a g) -> p a g", a=2))
            link(ts(pen[:, :], ps[:, 3, 0:P], -BIG, BIG, ALU.mult, ALU.add))
            tt(r(RE), r(ARE), r(DT), ALU.mult).then_inc(par_dve, 1)
            link(tt(r(TH), r(AIM), r(DT), ALU.mult))
            link(ts(r(T0), r(TH), 1.0 / TWO_PI, ROUND, ALU.mult, ALU.add))
            link(ts(r(T1), r(T0), ROUND, None, ALU.subtract))
            link(stt(r(T2), r(T1), -PI_A, r(TH), ALU.mult, ALU.add))
            link(stt(r(T3), r(T1), -PI_B, r(T2), ALU.mult, ALU.add))
            link(stt(r(T2), r(T1), -PI_C, r(T3), ALU.mult, ALU.add))
            link(ts(r(ANG), r(T2), 3.1415925, -3.1415925, ALU.min, ALU.max))
            link(ts(r(T3), r(ANG), -1.0, None, ALU.mult))
            link(tt(r(T3), r(T3), r(ANG), ALU.max))
            ts(r(CANG), r(T3), -1.0, math.pi / 2, ALU.mult, ALU.add).then_inc(par_dve, 1)
            link(tt(r(T0), r(ARE), r(ARE), ALU.mult))
            link(tt(r(T1), r(AIM), r(AIM), ALU.mult))
            link(tt(r(T0), r(T0), r(T1), ALU.add))
            link(nc.vector.reciprocal(r(T1), r(T0)))
            dve.wait_ge(par_act, 4)
            link(nc.vector.memset(lam[:, 0, 0, :], 1.0))
            link(nc.vector.memset(lam[:, 0, 1, :], 0.0))
            link(tt(lam[:, 1, 0, :], r(ER), r(COS), ALU.mult))
            link(tt(lam[:, 1, 1, :], r(ER), r(SIN), ALU.mult))
            link(ts(r(T0), lam[:, 1, 0, :], -1.0, None, ALU.add))
            link(tt(r(T2), r(T0), r(ARE), ALU.mult))
            link(tt(r(T3), lam[:, 1, 1, :], r(AIM), ALU.mult))
            link(tt(r(T2), r(T2), r(T3), ALU.add))
            link(tt(r(QR), r(T2), r(T1), ALU.mult))
            link(tt(r(T2), lam[:, 1, 1, :], r(ARE), ALU.mult))
            link(tt(r(T3), r(T0), r(AIM), ALU.mult))
            link(tt(r(T2), r(T2), r(T3), ALU.subtract))
            tt(r(QI), r(T2), r(T1), ALU.mult).then_inc(par_dve, 1)
            dve.wait_ge(par_tr, 2)
            nc.vector.tensor_copy(gain_t[:, :, :].rearrange("p a k -> p (a k)"), ps[:, 4, 0:2 * KT])
            dve_rstd(0, 0)
            for c in range(CLS):
                ts(x_tok[:, c, :], x_tok[:, c, :], stat[:, 2, c:c + 1], None, ALU.mult).then_inc(scaled, 1)
            split_lo(dve, 0, 0)
            dve_turn(0)
            dve.wait_ge(const, 1)
            dve.wait_ge(skip_in, 16 * OG)
            link(nc.vector.tensor_reduce(e16[:, :], ident[:, :].rearrange("p (j o) -> p o j", j=4)[:, 0:CH, :],
                                         AX, ALU.add))
            tt(d_blk[:, :, :],
               e16[:, :].unsqueeze(1).broadcast_to([P, 2 * OCT, CH]),
               d_pad[:, :].unsqueeze(2).broadcast_to([P, 2 * OCT, CH]), ALU.mult)
            nc.vector.memset(ps[:, 6:8, 0:P], 0.0).then_inc(k_bank, 1)
            with dve.Fori(0, 2) as it:
                for k in range(1, 9):
                    split_lo(dve, B_U + k, 2 * it)
            dve_qkv(0, 0, lambda k: dve_tables(0, k))
            dve_qkv(0, 1)
            dve_qkv(0, 2, lambda k: (dve_tables(1, k), dve_first_scores(0, k)))
            dve_attention(0)

            def dve_chunk_inputs(b):
                dve.wait_ge(s_made, b + 1)
                nc.vector.tensor_copy(s_t[:, OG * b:OG * b + OG, :, :].rearrange("p e r n -> p (e r n)"),
                                      ps[:, 6 + b % 2, :]).then_inc(s_copied, 1)

            dve_qkv(1, 0, lambda k: dve_chunk_inputs(k - 3) if 3 <= k < 3 + OCT else None)
            dve_qkv(1, 1)
            dve_qkv(1, 2, lambda k: dve_first_scores(1, k))
            dve_attention(1)
            def dve_outputs(b):
                dve.wait_ge(y_made, b + 1)
                for gh in range(2):
                    g = group(b, gh, 0)
                    ins = nc.vector.tensor_copy(u_all[:, g:g + OG, :].rearrange("p e n -> p (e n)"),
                                                ps[:, 4 + 2 * (b % 2) + gh, 0:OG * NCH])
                ins.then_inc(y_copied, 1)

            for k in range(1, 9):
                split_lo(dve, B_G0 + k, 0)
                if k >= 3:
                    dve_outputs(k - 3)
            for k in range(1, 9):
                split_lo(dve, B_AU + k, 0)
                if k <= 2:
                    dve_outputs(k + 5)
                for t in GELU_AT[k - 1]:
                    dve_gelu_lo(t)

            def merge(it, step):
                m2 = mrg[:, bass.ds(2 * it, 2), :].rearrange("p a n -> p (a n)")
                if step == 1:
                    dve.wait_ge(gated, START + 3 * it + 3)
                    tt(sig_g[:, :], pair(2), sig_g[:, :], ALU.mult).then_inc(merge_step, 1)
                if step == 2:
                    dve.wait_ge(merge_step, START + 4 * it + 2)
                    tt(sig_g[:, :], sig_g[:, :], sig_s[:, :], ALU.mult).then_inc(merge_step, 1)
                if step == 3:
                    dve.wait_ge(merge_step, START + 4 * it + 3)
                    tt(m2, m2, sig_g[:, :], ALU.add).then_inc(merge_step, 1)

            def merge_attention(it):
                m2 = mrg[:, bass.ds(2 * it, 2), :].rearrange("p a n -> p (a n)")
                dve.wait_ge(gated, START + 3 * it + 2)
                tt(m2, m2, sig_a[:, :], ALU.mult).then_inc(merge_step, 1)

            for k in range(1, 5):
                split_lo(dve, B_Y0 + k, 0)
            dve.wait_ge(au_copied, 1)
            merge_attention(0)
            def out_gain(d):
                dve.wait_ge(mix_sq, CLS * (d + 1))
                if d == 0:
                    dve.wait_ge(gb_in[0], 16)
                cols = slice(512 * d, 512 * d + 512)
                b = 4 * (d % 2)
                tt(o_t[:, :, cols], ps[:, b:b + 4, :], gain_b[:, cols].unsqueeze(1).broadcast_to([P, CLS, 512]),
                   ALU.mult).then_inc(o_copied, 1)

            def mrg_split_lo(i):
                a, b = MRG_RUNS[i]
                dve.wait_ge(mrg_hi, i + 1)
                tt(a_lo[:, a:b, :], mrg[:, a:b, :], a_hi[:, a:b, :].bitcast(F32), ALU.subtract).then_inc(mrg_lo, 1)

            with dve.Fori(1, 7) as it:
                for k in range(1, 13):
                    split_lo(dve, B_MRG - 12 + k, 3 * it)
                    if k <= 3:
                        merge(it - 1, k)
                    if k == 8:
                        merge_attention(it)
            for k in range(1, 13):
                split_lo(dve, B_MRG - 12 + k, 21)
                if k <= 3:
                    merge(6, k)
                if k == 8:
                    merge_attention(7)
                if k >= 9:
                    mrg_split_lo(k - 9)
            for k in range(1, 33):
                split_lo(dve, B_WO + k, 0)
                if k <= 3:
                    merge(7, k)
                if k == 4:
                    mrg_split_lo(4)
                if k in (9, 17, 25):
                    out_gain((k - 9) // 8)
            dve.wait_ge(mix_sq, 4 * CLS)
            dve_rstd(1, between=lambda: out_gain(3))
            dve.wait_ge(o_copied, START + 4)
            dve.wait_ge(x_again, 16)
            for c in range(CLS):
                stt(x2[:, c, :], o_t[:, c, :], stat[:, 2, c:c + 1], x2[:, c, :], ALU.mult, ALU.add
                    ).then_inc(x2_ready, 1)
            dve_rstd(2, 1)
            dve.wait_ge(x2_ready, CLS)
            for c in range(CLS):
                ts(o_t[:, c, :], x2[:, c, :], stat[:, 2, c:c + 1], None, ALU.mult).then_inc(scaled, 1)
            dve_turn(1)

            def ffn(g, last):
                if last:
                    dve.wait_ge(gb_in[1], 16)
                for k in range(1, 25):
                    if not (last and k == 24):
                        split_lo(dve, B_FF + k, 6 * g)
                    if k in (8, 16):
                        a = k // 8 - 1
                        dve.wait_ge(piece_done, B_FF + k + 24 * g)
                        dve.wait_ge(silu, START + 2 * g + a + 1)
                        tt(f_t[:, :], pair(1), f_sg[:, :], ALU.mult).then_inc(f_made, 1)
                        dve.wait_ge(f_hi_ready, 2 * g + a + 1)
                        tt(f_lo[:, 2 * a:2 * a + 2, :].rearrange("p a n -> p (a n)"), f_t[:, :],
                           f_hi[:, 2 * a:2 * a + 2, :].rearrange("p a n -> p (a n)").bitcast(F32), ALU.subtract
                           ).then_inc(f_lo_ready, 1)
                    if k >= 18 and k % 2 == 0:
                        d = (k - 18) // 2
                        if d == 0:
                            dve.wait_ge(acc_zero, 1)
                        for c in range(CLS):
                            if c < CLS - 1:
                                dve.wait_ge(down, 12 * g + 3 * d + c + 1)
                            else:
                                dve.wait_ge(piece_done, B_FF + k + 24 * g)
                            o = o_t[:, c, 512 * d:512 * d + 512]
                            tt(o, o, ps[:, 4 + c, :], ALU.add).then_inc(down_added, 1)
                            if last:
                                dve.wait_ge(down_added, START + 16 * g + 4 * d + c + 1)
                                cols = slice(512 * d, 512 * d + 512)
                                tt(o_gain[:, c, cols], o, gain_b[:, cols], ALU.mult).then_inc(o_gained, 1)

            with dve.Fori(0, FFG - 1) as g:
                ffn(g, False)
            ffn(FFG - 1, True)
            dve.wait_ge(ffn_sq, 4 * CLS)
            dve_rstd(3)
            dve.wait_ge(o_gained, 4 * CLS)
            for c in range(CLS):
                for h in range(2):
                    cols = slice(D // 2 * h, D // 2 * (h + 1))
                    stt(x2[:, c, cols], o_gain[:, c, cols], stat[:, 2, c:c + 1], x2[:, c, cols], ALU.mult, ALU.add
                        ).then_inc(out_ready, 1)

        @block.gpsimd
        def _(pool):
            steps = [0]

            def link(ins):
                steps[0] += 1
                ins.then_inc(pool_step, 1)
                pool.wait_ge(pool_step, steps[0])

            tt, ts = nc.gpsimd.tensor_tensor, nc.gpsimd.tensor_scalar
            nc.gpsimd.memset(zero[:, :], 0.0)
            nc.gpsimd.memset(d_pad[:, :], 0.0)
            nc.gpsimd.memset(hot[:, :], 1.0)
            link(nc.gpsimd.memset(ident[:, :], 0.0))
            nc.gpsimd.affine_select(out=hot[:, :].rearrange("p (a b) -> p a b", b=4),
                                    in_=hot[:, :].rearrange("p (a b) -> p a b", b=4), compare_op=ALU.is_equal,
                                    fill=0.0, base=0, pattern=[[0, P // 4], [1, 4]], channel_multiplier=-1)
            nc.gpsimd.affine_select(out=ident[:, :], in_=ident[:, :], compare_op=ALU.not_equal, fill=1.0, base=0,
                                    pattern=[[-1, P]], channel_multiplier=1).then_inc(const, 1)
            for ri, name in enumerate(("ssm_b_re", "ssm_b_im")):
                for gh in range(2):
                    for q in range(4):
                        pool.dma_start(b_raw[NST * gh:NST * gh + NST, ri, 8 * q:8 * q + 8, :],
                                      A[name][0, 16 * q + 8 * gh:16 * q + 8 * gh + 8].rearrange("g p c -> p g c")
                                      ).then_inc(b_in, 16)
            pool.wait_ge(const, 1)
            d_src = A["ssm_d"][0].rearrange("(m e i) -> e i m", m=2 * OCT, e=OG)
            for e in range(OG):
                pool.dma_start(d_pad[32 * e:32 * e + CH, :], d_src[e],
                              allow_slow_non_contiguous=True).then_inc(skip_in, 16)

            pool.wait_ge(par_dve, 3)
            pool.wait_ge(b_in, 256)
            q16 = [prm[:, i, :].unsqueeze(2).broadcast_to([P, HG, CH]) for i in (15, 16)]
            tmp = [ptmp[:, i, 0:HG * CH].rearrange("p (g c) -> p g c", c=CH) for i in range(2)]
            for ri, (s0, s1, op) in enumerate(((0, 1, ALU.subtract), (1, 0, ALU.add))):
                tt(tmp[0], q16[0], b_raw[:, s0, :, :], ALU.mult)
                link(tt(tmp[1], q16[1], b_raw[:, s1, :, :], ALU.mult))
                link(tt(b_bar[:, ri, :, :], tmp[0], tmp[1], op))

            def power(lo, n, src):
                shape = [P, n, HG]
                ar, ai = (lam[:, lo:lo + 1, j, :].broadcast_to(shape) for j in range(2))
                br, bi = (lam[:, 1:1 + n, j, :] for j in range(2))
                t0, t1 = (ptmp[:, j, 0:n * HG].rearrange("p (n g) -> p n g", g=HG) for j in range(2))
                for ri, (x, y, op) in enumerate(((br, bi, ALU.subtract), (bi, br, ALU.add))):
                    tt(t0, ar, x, ALU.mult)
                    link(tt(t1, ai, y, ALU.mult))
                    link(tt(lam[:, lo + 1:lo + 1 + n, ri, :], t0, t1, op))

            power(1, 1, 1)
            power(2, 2, 1)
            power(4, 4, 1)
            for s in range(L):
                nc.gpsimd.tensor_copy(lam_r[:, s, :, :], lam[:, L - 1 - s, :, :])
            for j in range(2):
                nc.gpsimd.tensor_copy(scan_a[:, 0, :, j], lam[:, L, 0, :])
            ts(scan_a[:, 1, :, 0], lam[:, L, 1, :], -1.0, None, ALU.mult)
            link(nc.gpsimd.tensor_copy(scan_a[:, 1, :, 1], lam[:, L, 1, :]))

            def tables(half):
                for q in range(4):
                    b = 4 * half + q
                    g0 = OG * b
                    if half and q == 0:
                        pool.wait_ge(k_made, 4)
                        pool.wait_ge(g_made, 4)
                        pool.wait_ge(h_stored, 16 * 4)
                    gs = slice(g0, g0 + OG)
                    for dst, pw, src, n, signs in ((bl, lam_r, b_bar, L, (ALU.subtract, ALU.add)),
                                                   (hc, lam, c_t, L + 1, (ALU.add, ALU.subtract))):
                        shape = [P, OG, n, CH]
                        lr, li = (pw[:, 0:n, j, gs].rearrange("p n e -> p e n").unsqueeze(3).broadcast_to(shape)
                                  for j in range(2))
                        xr, xi = (src[:, j, gs, :].unsqueeze(2).broadcast_to(shape) for j in range(2))
                        t0, t1 = (ptmp[:, j, 0:OG * n * CH].rearrange("p (e n c) -> p e n c", e=OG, c=CH)
                                  for j in range(2))
                        for ri, (x, y) in enumerate(((xr, xi), (xi, xr))):
                            tt(t0, lr, x, ALU.mult)
                            link(tt(t1, li, y, ALU.mult))
                            last = tt(dst[:, q, :, ri, :, :], t0, t1, signs[ri])
                            if dst is hc and ri:
                                last.then_inc(tab_ready, 1)
                                pool.wait_ge(tab_ready, b + 1)
                            else:
                                link(last)
                    pool.dma_start(h_d[b], hc[:, q, :, :, :, :].rearrange("p e r k o -> p (e r) (k o)")
                                   ).then_inc(h_stored, 16)
            pool.wait_ge(par_banks, 1)
            tables(0)
            tables(1)
            for h in range(2):
                pool.dma_start(k_d[512 * h:512 * h + 512, 0:(L - 1) * CH].rearrange("(a p) n -> p a n", p=P),
                               zero[:, :].rearrange("p (a n) -> p a n", a=4)).then_inc(zero_stored, 16)

            def biases(pr):
                for h in range(2):
                    if pr:
                        pool.wait_ge(biased, 8)
                    u7, u2 = bias[:, h, 0:7, :], bias[:, h, 7:9, :]
                    nc.gpsimd.iota(u7, pattern=[[-1, 7], [-CLS, P]], base=3, channel_multiplier=CLS,
                                   allow_small_or_imprecise_dtypes=True)
                    link(nc.gpsimd.iota(u2, pattern=[[0, 2], [-CLS, P]], base=0, channel_multiplier=CLS,
                                        allow_small_or_imprecise_dtypes=True))
                    nc.gpsimd.affine_select(out=u2, in_=u2, compare_op=ALU.is_ge, fill=BIG, base=0,
                                            pattern=[[0, 2], [-CLS, P]], channel_multiplier=CLS)
                    link(nc.gpsimd.affine_select(out=u7, in_=u7, compare_op=ALU.is_ge, fill=BIG, base=3,
                                                 pattern=[[-1, 7], [-CLS, P]], channel_multiplier=CLS))
                    link(nc.gpsimd.affine_select(out=u7, in_=u7, compare_op=ALU.is_ge, fill=BIG, base=WINDOW0 - 3,
                                                 pattern=[[1, 7], [CLS, P]], channel_multiplier=-CLS))
                    link(tt(bias[:, h, 8, :], bias[:, h, 8, :], pen[:, :], ALU.add))
                    ts(u7, u7, -slope(2 * pr + h) / SCALE, None, ALU.mult)
                    ts(bias[:, h, 7, :], bias[:, h, 7, :], -slope(HEADS + 2 * pr + h) / SCALE, None, ALU.mult)
                    ts(bias[:, h, 8, :], bias[:, h, 8, :], -slope(2 * HEADS + 2 * pr + h) / SCALE, None, ALU.mult
                       ).then_inc(bias_ready, 1)

            biases(0)
            pool.wait_ge(u_stored[0], START + 64)
            pool.wait_ge(u_stored[1], START + 64)
            pool.wait_ge(g_stored, 16 * OCT)
            pool.wait_ge(k_stored, 16 * 2 * OG)
            pool.wait_ge(zero_stored, 32)
            pool.wait_ge(h_stored, 16 * OCT)
            for s in range(L):
                pool.dma_start(u_all[CH * s:CH * s + CH, :, :], u_d[s].rearrange("(g i) n -> i g n", i=CH)
                               ).then_inc(u_in, 16)
            pool.wait_ge(heads_lo, 8)
            for b in range(OCT):
                s = b % 2
                if b >= 2:
                    pool.wait_ge(s_made, b - 1)
                pool.dma_start(g_r[:, s, :, :, :].rearrange("p e r n -> p (e r n)"), g_d[b]).then_inc(g_in[s], 16)
            biases(1)
            pool.wait_ge(s_copied, OCT)
            with pool.Fori(0, NCH - 1) as n:
                prev = s_t[:, :, :, bass.ds(n, 1)].rearrange("p g r n -> p g (r n)")
                tt(scan_t[:, 0, :, :], prev, scan_a[:, 0, :, :], ALU.mult)
                for r in range(2):
                    other = s_t[:, :, 1 - r, bass.ds(n, 1)].rearrange("p g n -> p (g n)")
                    last = tt(scan_t[:, 1, :, r], other, scan_a[:, 1, :, r], ALU.mult)
                last.then_inc(scan_step, 1)
                pool.wait_ge(scan_step, 3 * n + 1)
                tt(scan_t[:, 0, :, :], scan_t[:, 0, :, :], scan_t[:, 1, :, :], ALU.add).then_inc(scan_step, 1)
                pool.wait_ge(scan_step, 3 * n + 2)
                cur = s_t[:, :, :, bass.ds(n + 1, 1)].rearrange("p g r n -> p g (r n)")
                tt(cur, cur, scan_t[:, 0, :, :], ALU.add).then_inc(scan_step, 1)
                pool.wait_ge(scan_step, 3 * n + 3)

            def lag_tables(q):
                for s in range(L):
                    src = bass.AP(tensor=k_d.tensor, offset=16 * q * CH * KPAD + (L - 1 - s) * CH,
                                  ap=[[KPAD, CH], [CH * KPAD, 16], [1, P]])
                    pool.dma_start(t_q[q][CH * s:CH * s + CH, :, :], src).then_inc(t_in[q], 16)

            def state_tables(b):
                pool.dma_start(h_r[b % 4][:, :, :, :].rearrange("p e r n -> p (e r) n"), h_d[b, :, :, CH:]
                               ).then_inc(h_in[b % 4], 16)

            pool.wait_ge(heads_lo, 16)
            for q in range(4):
                state_tables(q)
                lag_tables(q)
            for b in range(4, OCT):
                pool.wait_ge(y_made, b - 3)
                state_tables(b)
            for h in range(2):
                if h == 0:
                    pool.wait_ge(y_copied, OCT // 2)
                    store_outputs(pool, 0)
                pool.wait_ge(y_stored[h], 16 * L)
                for t in range(4 * h, 4 * h + 4):
                    if h:
                        pool.wait_ge(gelu, t - 3)
                    pool.dma_start(y_in[:, t % 4, :].rearrange("p (s n) -> p s n", s=L),
                                   y_d[:, t * P:t * P + P, :].rearrange("s p n -> p s n")
                                   ).then_inc(y_back[t % 4], 16)
            pool.wait_ge(mrg_lo, 5)
            pool.dma_start(gain_b[:, :], A["norm_mix_post"][0:1, :].partition_broadcast(P)).then_inc(gb_in[0], 16)
            pool.dma_start(x2[:, :, :], A["x"][0].rearrange("(j c) d -> j c d", c=CLS)).then_inc(x_again, 16)
            pool.wait_ge(o_copied, START + 4)
            pool.dma_start(gain_b[:, :], A["norm_ffn_post"][0:1, :].partition_broadcast(P)).then_inc(gb_in[1], 16)
            pool.wait_ge(turned, 2 * KT)
            nc.gpsimd.memset(o_t[:, :, :].rearrange("p c d -> p (c d)"), 0.0).then_inc(acc_zero, 1)


_INS = ["x", "norm_mix_pre", "w_in", "w_attn_up", "ssm_a_re", "ssm_a_im", "ssm_log_dt", "ssm_b_re", "ssm_b_im",
        "ssm_c_re", "ssm_c_im", "ssm_d", "w_glu_v", "w_glu_g", "w_out", "norm_mix_post", "norm_ffn_pre",
        "w_ffn_gate", "w_ffn_up", "w_ffn_down", "norm_ffn_post"]


def kernel(**inputs):
    import numpy as _np
    import concourse.bacc as _bacc
    from concourse import mybir as _mybir
    from concourse.bass_utils import run_bass_kernel_spmd as _run

    nc = _bacc.Bacc("TRN2", target_bir_lowering=False, num_devices=1)
    arrays, aps = {}, {}
    for name in _INS:
        a = _np.ascontiguousarray(inputs[name])
        arrays[f"in_{name}"] = a
        aps[name] = nc.dram_tensor(f"in_{name}", a.shape, _mybir.dt.from_np(a.dtype), kind="ExternalInput").ap()
    out = nc.dram_tensor("out_0", (1, SEQ, D), _mybir.dt.float32, kind="ExternalOutput").ap()
    build(nc, aps, out)
    r = _run(nc, [arrays], core_ids=[0])
    return r.results[0]["out_0"]
```
